# Optimizing a Trainium2 kernel written in Bass

```python
import math
import jax, jax.numpy as jnp
from jax import lax
import numpy as np

D_MODEL = 2048
BATCH = 1
SEQ = 256
DEPTH = 1
DEC_BATCH = 8
DEC_SEQ = 1
PAST_LEN = 1024
PAGE_SIZE = 128

N_ATTN_HEADS = 16
HEAD_DIM = 64
ATTN_WIDTH = N_ATTN_HEADS * HEAD_DIM
MOBA_BLOCK = 256
MOBA_TOPK = 3
Q_SWEEP = 16
D_INNER = D_MODEL
SSM_HEADDIM = 64
N_SSM_HEADS = D_INNER // SSM_HEADDIM
N_SSM_GROUPS = 8
D_STATE = 128
CONV_WIDTH = 4
CONV_DIM = D_INNER + 2 * N_SSM_GROUPS * D_STATE
SSD_CHUNK = 128
D_FF = -(-8 * D_MODEL // (3 * 256)) * 256
EPS = 1e-6
IN_PROJ_DIM = 3 * ATTN_WIDTH + D_INNER + CONV_DIM + N_SSM_HEADS + 2 * D_MODEL

kernel_name = "moba_mamba2_gated_parallel_decoder_step"

def _split_points():
    sizes = [ATTN_WIDTH, ATTN_WIDTH, ATTN_WIDTH, D_INNER, CONV_DIM, N_SSM_HEADS, D_MODEL, D_MODEL]
    return [int(s) for s in np.cumsum(sizes)[:-1]]

def rmsnorm(x, g):
    xf = x.astype(jnp.float32)
    y = xf * lax.rsqrt(jnp.mean(xf * xf, axis=-1, keepdims=True) + EPS)
    return (y * g.astype(jnp.float32)).astype(x.dtype)

def swiglu(h, w_gate, w_up, w_down):
    return (jax.nn.silu(h @ w_gate) * (h @ w_up)) @ w_down

def moba_attention(q, k, v, q_pos0):
    f32 = jnp.float32
    b, Lq, H, d = q.shape
    Lk = k.shape[1]
    nb = -(-Lk // MOBA_BLOCK)
    pad = nb * MOBA_BLOCK - Lk
    kp = jnp.pad(k, ((0, 0), (0, pad), (0, 0), (0, 0)))
    vp = jnp.pad(v, ((0, 0), (0, pad), (0, 0), (0, 0)))
    kb = kp.reshape(b, nb, MOBA_BLOCK, H, d).transpose(0, 3, 1, 2, 4)
    vb = vp.reshape(b, nb, MOBA_BLOCK, H, d).transpose(0, 3, 1, 2, 4)
    q_pos = q_pos0 + jnp.arange(Lq, dtype=jnp.int32)
    q_blk = q_pos // MOBA_BLOCK
    qh = q.transpose(0, 2, 1, 3)
    own = jnp.broadcast_to(q_blk[None, None, :, None], (b, H, Lq, 1))
    n_sel = min(MOBA_TOPK, nb - 1)
    if n_sel > 0:
        kmean = jnp.mean(kb.astype(f32), axis=3)
        gate = jnp.einsum('bhqd,bhnd->bhqn', qh.astype(f32), kmean)
        past = jnp.arange(nb, dtype=jnp.int32)[None, :] < q_blk[:, None]
        gate = jnp.where(past[None, None], gate, -jnp.inf)
        _, sel = lax.top_k(gate, n_sel)
        sel = sel.astype(jnp.int32)
        sel_ok = sel < q_blk[None, None, :, None]
        blk_idx = jnp.concatenate([sel, own], axis=-1)
        blk_ok = jnp.concatenate([sel_ok, jnp.ones_like(own, dtype=bool)], axis=-1)
    else:
        blk_idx = own
        blk_ok = jnp.ones_like(own, dtype=bool)

    qc = Q_SWEEP if Lq % Q_SWEEP == 0 else Lq
    nq = Lq // qc

    def to_chunks(t):
        return jnp.moveaxis(t.reshape(b, H, nq, qc, *t.shape[3:]), 2, 0)

    bi = jnp.arange(b)[:, None, None, None]
    hi = jnp.arange(H)[None, :, None, None]
    key_off = jnp.arange(MOBA_BLOCK, dtype=jnp.int32)
    scale = d ** -0.5

    def attend(args):
        qch, idx, ok, pos = args
        ks = kb[bi, hi, idx]
        vs = vb[bi, hi, idx]
        s = jnp.einsum('bhqd,bhqkjd->bhqkj', qch.astype(f32), ks.astype(f32)) * scale
        kpos = idx[..., None] * MOBA_BLOCK + key_off
        mask = ok[..., None] & (kpos <= pos[None, None, :, None, None])
        s = jnp.where(mask, s, -jnp.inf)
        p = jax.nn.softmax(s.reshape(b, H, qc, -1), axis=-1).reshape(s.shape)
        return jnp.einsum('bhqkj,bhqkjd->bhqd', p, vs.astype(f32))

    out = lax.map(attend, (to_chunks(qh), to_chunks(blk_idx), to_chunks(blk_ok), q_pos.reshape(nq, qc)))
    out = jnp.moveaxis(out, 0, 2).reshape(b, H, Lq, d).transpose(0, 2, 1, 3).reshape(b, Lq, H * d)
    return out.astype(q.dtype)

def causal_dwconv(xbc, prev, w, bias):
    L = xbc.shape[1]
    xp = jnp.concatenate([prev.astype(xbc.dtype), xbc], axis=1)
    y = bias + sum(w[i] * xp[:, i:i + L] for i in range(CONV_WIDTH))
    return y, xp[:, -(CONV_WIDTH - 1):]

def ssd_scan(x, dt, A, Bm, Cm, h0, chunk):
    f32 = jnp.float32
    b, L, H, P = x.shape
    G, N = Bm.shape[2], Bm.shape[3]
    R = H // G
    nc = L // chunk
    xc = x.astype(f32).reshape(b, nc, chunk, G, R, P)
    dtc = dt.astype(f32).reshape(b, nc, chunk, G, R)
    Bc = Bm.astype(f32).reshape(b, nc, chunk, G, N)
    Cc = Cm.astype(f32).reshape(b, nc, chunk, G, N)
    acum = jnp.cumsum(dtc * A.astype(f32).reshape(G, R), axis=2)
    seg = acum[:, :, :, None] - acum[:, :, None, :]
    causal = jnp.tril(jnp.ones((chunk, chunk), dtype=bool))[:, :, None, None]
    decay = jnp.exp(jnp.where(causal, seg, -jnp.inf))
    xdt = xc * dtc[..., None]
    cb = jnp.einsum('bcign,bcjgn->bcijg', Cc, Bc)
    y_diag = jnp.einsum('bcijg,bcijgr,bcjgrp->bcigrp', cb, decay, xdt)
    decay_end = jnp.exp(acum[:, :, -1:] - acum)
    states = jnp.einsum('bcjgn,bcjgr,bcjgrp->bcgrpn', Bc, decay_end, xdt)
    chunk_decay = jnp.exp(acum[:, :, -1])

    def step(h, inp):
        s, dcy = inp
        return dcy[..., None, None] * h + s, h

    h_init = h0.astype(f32).reshape(b, G, R, P, N)
    h_final, h_starts = lax.scan(step, h_init, (jnp.moveaxis(states, 1, 0), jnp.moveaxis(chunk_decay, 1, 0)))
    h_starts = jnp.moveaxis(h_starts, 0, 1)
    y_off = jnp.einsum('bcign,bcgrpn,bcigr->bcigrp', Cc, h_starts, jnp.exp(acum))
    return (y_diag + y_off).reshape(b, L, H, P), h_final.reshape(b, H, P, N)

def mamba2_branch(z, xbc, dt_raw, conv_prev, ssm_prev, conv_w, conv_b, dt_bias, a_log, d_skip, ssm_norm):
    f32 = jnp.float32
    b, L, _ = z.shape
    xbc_c, conv_new = causal_dwconv(xbc, conv_prev, conv_w, conv_b)
    xbc_c = jax.nn.silu(xbc_c)
    xs, Bm, Cm = jnp.split(xbc_c, [D_INNER, D_INNER + N_SSM_GROUPS * D_STATE], axis=-1)
    xs = xs.reshape(b, L, N_SSM_HEADS, SSM_HEADDIM)
    Bm = Bm.reshape(b, L, N_SSM_GROUPS, D_STATE)
    Cm = Cm.reshape(b, L, N_SSM_GROUPS, D_STATE)
    dt = jax.nn.softplus(dt_raw.astype(f32) + dt_bias.astype(f32))
    A = -jnp.exp(a_log.astype(f32))
    chunk = SSD_CHUNK if L % SSD_CHUNK == 0 else L
    y, h_new = ssd_scan(xs, dt, A, Bm, Cm, ssm_prev, chunk)
    y = y + d_skip.astype(f32)[:, None] * xs.astype(f32)
    u = (y.reshape(b, L, D_INNER) * jax.nn.silu(z.astype(f32))).reshape(b, L, N_SSM_GROUPS, D_INNER // N_SSM_GROUPS)
    u = u * lax.rsqrt(jnp.mean(u * u, axis=-1, keepdims=True) + EPS)
    u = u.reshape(b, L, D_INNER) * ssm_norm.astype(f32)
    return u.astype(z.dtype), conv_new, h_new.astype(ssm_prev.dtype)

def _layer(x, k_past, v_past, conv_prev, ssm_prev, q_pos0,
           norm_mix_pre, w_in, conv_w, conv_b, dt_bias, a_log, d_skip, ssm_norm,
           w_attn_out, w_ssm_out, w_out, norm_mix_post,
           norm_ffn_pre, w_gate, w_up, w_down, norm_ffn_post):
    b, L, _ = x.shape
    h = rmsnorm(x, norm_mix_pre)
    proj = h @ w_in
    q, k, v, z, xbc, dt_raw, g_attn, g_ssm = jnp.split(proj, _split_points(), axis=-1)
    q = q.reshape(b, L, N_ATTN_HEADS, HEAD_DIM)
    k = k.reshape(b, L, N_ATTN_HEADS, HEAD_DIM)
    v = v.reshape(b, L, N_ATTN_HEADS, HEAD_DIM)
    if k_past is None:
        k_all, v_all = k, v
    else:
        k_all = jnp.concatenate([k_past.astype(k.dtype), k], axis=1)
        v_all = jnp.concatenate([v_past.astype(v.dtype), v], axis=1)
    attn = moba_attention(q, k_all, v_all, q_pos0)
    ssm, conv_new, ssm_new = mamba2_branch(z, xbc, dt_raw, conv_prev, ssm_prev,
                                           conv_w, conv_b, dt_bias, a_log, d_skip, ssm_norm)
    merged = jax.nn.sigmoid(g_attn) * (attn @ w_attn_out) + jax.nn.sigmoid(g_ssm) * (ssm @ w_ssm_out)
    x = x + rmsnorm(merged @ w_out, norm_mix_post)
    f = swiglu(rmsnorm(x, norm_ffn_pre), w_gate, w_up, w_down)
    x = x + rmsnorm(f, norm_ffn_post)
    return x, k, v, conv_new, ssm_new

def setup_inputs(seed: int = 0) -> dict:
    key = jax.random.key(seed)
    ks = jax.random.split(key, 28)
    f32 = jnp.float32
    n_pages = PAST_LEN // PAGE_SIZE
    n_used = DEC_BATCH * n_pages
    n_phys = n_used + (n_used + 3) // 4

    def nrm(k, shape, scale=1.0):
        return scale * jax.random.normal(k, shape, f32)

    def gain(k, n):
        return 1.0 + 0.05 * jax.random.normal(k, (DEPTH, n), f32)

    page_table = jax.random.permutation(ks[6], n_phys)[:n_used].reshape(DEC_BATCH, n_pages).astype(jnp.int32)
    dt0 = jnp.exp(jax.random.uniform(ks[11], (DEPTH, N_SSM_HEADS), f32, math.log(1e-3), math.log(1e-1)))
    dt_bias = dt0 + jnp.log(-jnp.expm1(-dt0))
    a_log = jnp.log(jax.random.uniform(ks[12], (DEPTH, N_SSM_HEADS), f32, 1.0, 16.0))
    return {
        "x_prompt": nrm(ks[0], (BATCH, SEQ, D_MODEL)),
        "x_sample": nrm(ks[1], (DEC_BATCH, DEC_SEQ, D_MODEL)),
        "cache_k": nrm(ks[2], (DEPTH, n_phys, PAGE_SIZE, N_ATTN_HEADS, HEAD_DIM)),
        "cache_v": nrm(ks[3], (DEPTH, n_phys, PAGE_SIZE, N_ATTN_HEADS, HEAD_DIM)),
        "state_conv": nrm(ks[4], (DEPTH, DEC_BATCH, CONV_WIDTH - 1, CONV_DIM)),
        "state_ssm": nrm(ks[5], (DEPTH, DEC_BATCH, N_SSM_HEADS, SSM_HEADDIM, D_STATE), 0.3),
        "page_table": page_table,
        "norm_mix_pre": gain(ks[7], D_MODEL),
        "w_in": nrm(ks[8], (DEPTH, D_MODEL, IN_PROJ_DIM), D_MODEL ** -0.5),
        "conv_w": nrm(ks[9], (DEPTH, CONV_WIDTH, CONV_DIM), CONV_WIDTH ** -0.5),
        "conv_b": nrm(ks[10], (DEPTH, CONV_DIM), 0.01),
        "dt_bias": dt_bias,
        "a_log": a_log,
        "d_skip": 1.0 + 0.05 * jax.random.normal(ks[13], (DEPTH, N_SSM_HEADS), f32),
        "ssm_norm": gain(ks[14], D_INNER),
        "w_attn_out": nrm(ks[15], (DEPTH, ATTN_WIDTH, D_MODEL), ATTN_WIDTH ** -0.5),
        "w_ssm_out": nrm(ks[16], (DEPTH, D_INNER, D_MODEL), D_INNER ** -0.5),
        "w_out": nrm(ks[17], (DEPTH, D_MODEL, D_MODEL), D_MODEL ** -0.5),
        "norm_mix_post": gain(ks[18], D_MODEL),
        "norm_ffn_pre": gain(ks[19], D_MODEL),
        "w_gate": nrm(ks[20], (DEPTH, D_MODEL, D_FF), D_MODEL ** -0.5),
        "w_up": nrm(ks[21], (DEPTH, D_MODEL, D_FF), D_MODEL ** -0.5),
        "w_down": nrm(ks[22], (DEPTH, D_FF, D_MODEL), D_FF ** -0.5),
        "norm_ffn_post": gain(ks[23], D_MODEL),
    }

def reference(x_prompt, x_sample, cache_k, cache_v, state_conv, state_ssm, page_table,
              norm_mix_pre, w_in, conv_w, conv_b, dt_bias, a_log, d_skip, ssm_norm,
              w_attn_out, w_ssm_out, w_out, norm_mix_post,
              norm_ffn_pre, w_gate, w_up, w_down, norm_ffn_post):
    b_p = x_prompt.shape[0]
    b_s = x_sample.shape[0]
    n_pages = page_table.shape[1]
    past_len = n_pages * PAGE_SIZE
    y_prompt, y_sample = x_prompt, x_sample
    kp_list, vp_list, cp_list, sp_list = [], [], [], []
    ks_list, vs_list, cs_list, ss_list = [], [], [], []
    for l in range(DEPTH):
        lw = (norm_mix_pre[l], w_in[l], conv_w[l], conv_b[l], dt_bias[l], a_log[l], d_skip[l], ssm_norm[l],
              w_attn_out[l], w_ssm_out[l], w_out[l], norm_mix_post[l],
              norm_ffn_pre[l], w_gate[l], w_up[l], w_down[l], norm_ffn_post[l])
        conv0 = jnp.zeros((b_p, CONV_WIDTH - 1, CONV_DIM), x_prompt.dtype)
        ssm0 = jnp.zeros((b_p, N_SSM_HEADS, SSM_HEADDIM, D_STATE), state_ssm.dtype)
        y_prompt, k_p, v_p, c_p, s_p = _layer(y_prompt, None, None, conv0, ssm0, 0, *lw)
        k_past = cache_k[l][page_table].reshape(b_s, past_len, N_ATTN_HEADS, HEAD_DIM)
        v_past = cache_v[l][page_table].reshape(b_s, past_len, N_ATTN_HEADS, HEAD_DIM)
        y_sample, k_s, v_s, c_s, s_s = _layer(y_sample, k_past, v_past, state_conv[l], state_ssm[l], past_len, *lw)
        kp_list.append(k_p); vp_list.append(v_p); cp_list.append(c_p); sp_list.append(s_p)
        ks_list.append(k_s); vs_list.append(v_s); cs_list.append(c_s); ss_list.append(s_s)
    k_prompt = jnp.stack(kp_list)
    v_prompt = jnp.stack(vp_list)
    conv_prompt = jnp.stack(cp_list)
    ssm_prompt = jnp.stack(sp_list)
    k_sample = jnp.stack(ks_list)
    v_sample = jnp.stack(vs_list)
    conv_sample = jnp.stack(cs_list)
    ssm_sample = jnp.stack(ss_list)
    return (y_prompt, y_sample, k_prompt, v_prompt, conv_prompt, ssm_prompt, k_sample, v_sample, conv_sample, ssm_sample)


_drawn_inputs = setup_inputs


def setup_inputs(seed=0):
    import zlib

    import numpy as np

    out = dict(_drawn_inputs(seed))
    spreads = {}
    factors = {'conv_b': 3.569}
    for name, (base, spread) in spreads.items():
        noise = np.random.default_rng([zlib.crc32(name.encode()), seed]).standard_normal(out[name].shape)
        drawn = base * np.exp(spread * noise) if base else spread * noise
        out[name] = __import__('jax').numpy.asarray(drawn.astype(out[name].dtype))
    for name, factor in factors.items():
        out[name] = (out[name] * factor).astype(out[name].dtype)
    return out
```

```python
import concourse.bass as bass
from concourse import mybir
from contextlib import ExitStack

fp32 = mybir.dt.float32
f32r = mybir.dt.float32r
i32 = mybir.dt.int32
ALU = mybir.AluOpType
ACT = mybir.ActivationFunctionType
AX = mybir.AxisListType

P = 128
D = 2048
KT = D // P
TP = 256
NB = 8
T = TP + NB
HEADS = 16
HD = 64
AW = HEADS * HD
AT = AW // P
SH = 32
NG = 8
NST = 128
XT = 16
CT = XT + 2 * NG
FF = 5632
FT = FF // P
PAST = 1024
PG = 128
NPG = PAST // PG
NBLK = 4
EPS = 1e-6
NEG = -1e30
SCALE = HD ** -0.5
CONVC = CT * P
COL_Q, COL_Z, COL_X, COL_DT, COL_GA, COL_GS = 0, 3072, 5120, 9216, 9248, 11296
KG = 8
RING = 4
LAG = 3


def bass_hybrid_decoder_layer(nc, a, o):
    ctx = ExitStack()
    with ctx:
        def sem(name):
            return ctx.enter_context(nc.semaphore(name))

        base = (nc.sbuf_base + 63) // 64 * 64
        room = [base]

        def keep(name, shape, dt=fp32):
            n = 4
            for s in shape[1:]:
                n *= s
            t = nc.alloc_sbuf_tensor_at(name, shape, dt, offset=room[0])
            room[0] += (n + 63) // 64 * 64
            return t

        raw = keep("raw", [P, RING, KG, 256])
        w_hi = keep("w_hi", [P, RING, KG, P], f32r)
        w_lo = keep("w_lo", [P, RING, KG, P], f32r)
        ident = keep("ident", [P, P])
        ones = keep("ones", [P, P])
        upper = keep("upper", [P, P])
        dmask = keep("dmask", [P, NB])
        eps = keep("eps", [P, 1])
        gains = keep("gains", [P, 5, KT])
        conv_k = keep("conv_k", [P, 4, CT])
        conv_bias = keep("conv_bias", [P, CT])
        dskip = keep("dskip", [P, XT])
        heads_c = keep("heads_c", [SH, 4])
        pages = keep("pages", [1, NB * NPG], i32)
        stat = keep("stat", [P, T])
        stat_r = keep("stat_r", [P, T])
        sq = keep("sq", [P, 2, T])
        tmp = keep("tmp", [P, 2, T])
        arena = room[0]
        room_end = nc.sbuf_usable_end - 64

        def at(name, shape, dt, offset):
            n = 4
            for s in shape[1:]:
                n *= s
            assert arena + offset + n <= room_end, (name, arena + offset + n - room_end)
            return nc.alloc_sbuf_tensor_at(name, shape, dt, offset=arena + offset)

        K = 1024
        M0 = (room_end - arena - 16 * K) // 64 * 64
        attn = at("attn", [P, AT, T], fp32, M0)
        tails = at("tails", [P, CT, 3 + NB], fp32, M0 + AT * T * 4)
        state_t = at("state_t", [P, CT, NB, 3], fp32, M0 + 10 * K)
        cmask = at("cmask", [P, 3 * P], fp32, M0 + 13 * K)
        dt_raw = at("dt_raw", [SH, T], fp32, M0 + 14 * K + 512)
        TILE16 = KT * T * 4
        x_hi = at("x_hi", [P, KT, T], f32r, 0)
        x_lo = at("x_lo", [P, KT, T], f32r, TILE16)
        A0 = 2 * TILE16
        xtok = at("xtok", [P, 3, D], fp32, A0)
        xT = at("xT", [P, KT, T], fp32, A0 + 24 * K)
        ctok = at("ctok", [24, CONVC], fp32, A0 + 42 * K)
        xbc = at("xbc", [P, CT, T], fp32, A0)
        A1 = A0 + 2 * TILE16
        qkv = at("qkv", [P, 24, T], fp32, A1)
        A2 = A1 + 24 * T * 4
        vtok = at("vtok", [P, 2, AW], fp32, A2)
        att_s = at("att_s", [P, 2, 3 * P], fp32, A2 + 8 * K)
        att_pt = at("att_pt", [P, 2, 3 * P], fp32, A2 + 11 * K)
        att_st = at("att_st", [P, 2, 8], fp32, A2 + 14 * K)
        qk_head = at("qk_head", [P, 2, TP], fp32, A2 + 14 * K + 64)
        v_head = at("v_head", [P, 2, P], fp32, A2 + 16 * K + 64)
        conv_in = at("conv_in", [P, 2, 3 + TP + 4 * NB], fp32, A2 + 17 * K + 64)
        conv_out = at("conv_out", [P, 2, TP + 4 * NB], fp32, A2 + 19 * K + 512)
        conv_th = at("conv_th", [P, 2, TP + 4 * NB], fp32, A2 + 22 * K)
        ktok = at("ktok", [P, 2, AW], fp32, A0 + 12 * T * 4)
        stok = at("stok", [NB, 3 * AW], fp32, A0 + 12 * T * 4 + 8 * K)
        assert 12 * T * 4 + 20 * K <= 2 * TILE16
        dt_w = at("dt_w", [SH, 6, T], fp32, A1)
        S0 = A1 - K
        bcrow = at("bcrow", [NB, 2 * NG * P], fp32, S0 + 40 * K)
        xdt = at("xdt", [P, 2, D], fp32, S0 + 8 * K)
        btok = at("btok", [P, 2, NG * P], fp32, S0 + 24 * K)
        xw = at("xw", [P, 256], fp32, S0 + 32 * K)
        xw1 = at("xw1", [P, 2, 256], fp32, S0 + 33 * K)
        hT0 = at("hT0", [P, 256], fp32, S0 + 35 * K)
        seg = at("seg", [P, 2, 4 * P], fp32, S0 + 36 * K)
        dec = at("dec", [P, 2, 4 * P], fp32, S0 + 40 * K)
        cexp = at("cexp", [P, 4 * P], fp32, S0 + 44 * K)
        cbm = at("cbm", [P, 2, P], fp32, S0 + 46 * K)
        dtok = at("dtok", [P, 2, 2, SH], fp32, S0 + 47 * K)
        acum = at("acum", [P, 2, SH], fp32, S0 + 47 * K + 512)
        dend = at("dend", [P, 2, SH], fp32, S0 + 47 * K + 768)
        cdec = at("cdec", [P, SH], fp32, S0 + 48 * K)
        hfin = at("hfin", [P, 2, P], fp32, S0 + 48 * K + 128)
        expand = at("expand", [SH, D], fp32, A1 + 7 * K)
        crow = at("crow", [3 + NB, CONVC], fp32, A1)
        scal = at("scal", [P, XT, 2 * NB], fp32, A1 + 16 * K)
        xdts = at("xdts", [P, XT, NB], fp32, A1 + 17 * K)
        st = at("st", [P, 3, 4, P], fp32, A1 + 18 * K)
        bc = at("bc", [P, 3, 2, 256], fp32, A1 + 24 * K)
        stx = at("stx", [P, 4, P], fp32, A1 + 30 * K)
        sty = at("sty", [P, 4, P], fp32, A1 + 32 * K)
        ysam = at("ysam", [P, XT, NB], fp32, A1 + 34 * K)
        gate_s = at("gate_s", [P, KT, T], fp32, A0 + TILE16)
        gate_a = at("gate_a", [P, KT, T], fp32, A1)
        F0 = A1 + TILE16
        kv = at("kv", [P, 4, AW], fp32, F0)
        qb = at("qb", [P, 2, AW], fp32, F0 + 16 * K)
        sc = at("sc", [P, NPG + 1, NB, HEADS], fp32, F0 + 24 * K)
        m_w = at("m_w", [P, 10, P], fp32, F0 + 29 * K)
        un = at("un", [P, 2, 4, T], fp32, F0)
        own_v = at("own_v", [NB, AW], fp32, M0 + 10 * K)
        own_qk = at("own_qk", [NB, 2, AW], fp32, F0 + 8 * K)
        a_hi = at("a_hi", [P, AT, T], f32r, F0)
        a_lo = at("a_lo", [P, AT, T], f32r, F0 + AT * T * 4)
        mo = at("mo", [P, KT, T], fp32, A0)
        x1 = at("x1", [P, KT, T], fp32, A0 + TILE16)
        xtok2 = at("xtok2", [P, 3, D], fp32, A0 + 2 * TILE16)
        g_hi = at("g_hi", [P, FT, T], f32r, A0)
        g_lo = at("g_lo", [P, FT, T], f32r, A0 + FT * T * 4)
        glu = at("glu", [P, 3, 2, T], fp32, A0 + 2 * FT * T * 4)
        fo = at("fo", [P, KT, T], fp32, 0)
        x2 = at("x2", [P, KT, T], fp32, TILE16)
        ytok = at("ytok", [P, 3, D], fp32, A0)

        gemm_ps = [ctx.enter_context(nc.psum_tensor(f"gemm{n}", [P, 512], fp32)) for n in range(4)]
        side = [ctx.enter_context(nc.psum_tensor(f"side{n}", [P, 512], fp32)) for n in range(4)]

        q_row = nc.dram_tensor("q_row", [NB, AW], fp32, kind="Internal").ap()
        bc_row = nc.dram_tensor("bc_row", [NB, 2, NG * P], fp32, kind="Internal").ap()
        x1_spill = nc.dram_tensor("x1_spill", [P, KT * T], fp32, kind="Internal").ap()

        w_in, w_ao, w_so, w_o = a["w_in"][0], a["w_attn_out"][0], a["w_ssm_out"][0], a["w_out"][0]
        w_g, w_u, w_d = a["w_gate"][0], a["w_up"][0], a["w_down"][0]

        class Phase:
            made = []

            def __init__(self, ws, col, kt, pairs, hi, lo, per=2):
                self.ws, self.col, self.kt, self.pairs, self.per = ws, col, kt, pairs, per
                self.hi, self.lo = hi, lo
                self.loads = -(-kt // KG)
                self.lag = min(LAG, 2 * self.loads - 1)
                before = Phase.made[-1] if Phase.made else None
                self.load0 = before.load0 + before.pairs * before.loads if before else 0
                self.pair0 = before.pair0 + before.pairs if before else 0
                self.iters = pairs // per
                assert pairs % per == 0 and (self.load0 % 2 == 0) and self.pair0 % 2 in (0, 1)
                assert self.iters == 1 or (per * self.loads % RING == 0 and per % 2 == 0)
                Phase.made.append(self)

        ph_qkv = Phase([w_in], COL_Q, KT, 12, x_hi, x_lo)
        ph_dt = Phase([w_in], COL_DT, KT, 1, x_hi, x_lo, per=1)
        ph_xbc = Phase([w_in], COL_X, KT, 16, x_hi, x_lo)
        ph_z = Phase([w_in], COL_Z, KT, 8, x_hi, x_lo)
        ph_gs = Phase([w_in], COL_GS, KT, 8, x_hi, x_lo)
        ph_ga = Phase([w_in], COL_GA, KT, 8, x_hi, x_lo)
        ph_so = Phase([w_so], 0, KT, 8, x_hi, x_lo)
        ph_ao = Phase([w_ao], 0, AT, 8, a_hi, a_lo, per=4)
        ph_o = Phase([w_o], 0, KT, 8, x_hi, x_lo)
        ph_ff = Phase([w_g, w_u], 0, KT, 44, x_hi, x_lo)
        ph_dn = Phase([w_d], 0, FT, 8, g_hi, g_lo)

        loaded = [sem(f"loaded{s}") for s in range(RING)]
        free_out = [sem("free_out0"), sem("free_out1")]
        (hi_done, lo_done, mm_done, consts_in, pages_in, state_in, consts_made, x_in, x_tr, x_cp, nrm_sq, nrm_mm,
         nrm_sd, nrm_rs, h_mul, h_hi, h_lo, tok_tr, tok_out, cst_tr, cst_cp, qk_staged, v_staged, s_mm, s_masked,
         s_max, s_nmax, s_exp, s_rcp, s_norm, pt_mm, pt_cp, pv_mm, attn_cp, conv_st, conv_step, conv_tanh,
         xbc_done, tail_cp, dt_act, dt_dve, dt_tr, dt_tok, dt_sum, dt_ac, dt_de, xb_tr, r_mm, cb_mm, seg_done,
         cbm_done, dec_done, m_done, cx_exp, cx_done, xw_done, xwf_done, ht_mm, ht_cp, y_mm, y_done, fin_mm,
         fin_cp, fin_out, ct_tr, ct_cp, ct_out, bc_tr, bc_cp, bc_out, ex_made, ex_mm, ex_cp, sx_mul, stx_done,
         st_new, st_prod, st_sum, ysam_done, z_tanh, u_done, un_sq, un_mm, un_sd, un_rs, un_mul, own_in, own_mul,
         own_sum, own_put, k_mul, k_red, sel_mm, sel_dve, max_tr, max_dve, max_mm, p_sub, p_exp, p_sum, p_mm,
         p_rcp, p_done, v_mm, v_cp, u_hi, u_lo, a_hi_done, a_lo_done, ao_sum, ao_hi, ao_lo, x1_done, x1_out,
         x1_in, ff_tanh, ff_hi, ff_lo, y2_done, y_tr, y_cp, y_out, cs_out, y_cp2, o_scaled, f_scaled) = [sem(n) for n in (
            "hi_done lo_done mm_done consts_in pages_in state_in consts_made x_in x_tr x_cp nrm_sq nrm_mm "
            "nrm_sd nrm_rs h_mul h_hi h_lo tok_tr tok_out cst_tr cst_cp qk_staged v_staged s_mm s_masked "
            "s_max s_nmax s_exp s_rcp s_norm pt_mm pt_cp pv_mm attn_cp conv_st conv_step conv_tanh xbc_done "
            "tail_cp dt_act dt_dve dt_tr dt_tok dt_sum dt_ac dt_de xb_tr r_mm cb_mm seg_done cbm_done "
            "dec_done m_done cx_exp cx_done xw_done xwf_done ht_mm ht_cp y_mm y_done fin_mm fin_cp fin_out "
            "ct_tr ct_cp ct_out bc_tr bc_cp bc_out ex_made ex_mm ex_cp sx_mul stx_done st_new st_prod st_sum "
            "ysam_done z_tanh u_done un_sq un_mm un_sd un_rs un_mul own_in own_mul own_sum own_put k_mul "
            "k_red sel_mm sel_dve max_tr max_dve max_mm p_sub p_exp p_sum p_mm p_rcp p_done v_mm v_cp u_hi "
            "u_lo a_hi_done a_lo_done ao_sum ao_hi ao_lo x1_done x1_out x1_in ff_tanh ff_hi ff_lo y2_done "
            "y_tr y_cp y_out cs_out y_cp2 o_scaled f_scaled ").split()]
        tok_cp = [sem("tok_cp0"), sem("tok_cp1")]
        xb_cp = [sem("xb_cp0"), sem("xb_cp1")]
        kv_in = [sem(f"kv_in{s}") for s in range(4)]
        qb_in = [sem("qb_in0"), sem("qb_in1")]
        st_in = [sem(f"st_in{s}") for s in range(3)]
        st_out = [sem(f"st_out{s}") for s in range(3)]
        CONSTS = 13

        def wait(eng, s, v):
            if not isinstance(v, int) or v > 0:
                eng.wait_ge(s, v)

        def then(eng, ins, s, v):
            ins.then_inc(s, 1)
            eng.wait_ge(s, v)

        def block_no(ph, i, qq):
            return 2 * (ph.load0 + ph.per * ph.loads * i) + qq

        def k_tiles(ph, q):
            return min(KG, ph.kt - KG * (q // 2))

        def last_block(ph, pr, n):
            return 2 * (ph.load0 + ph.loads * pr) + 2 * ph.loads - 1 + n

        def blocks(eng, ph, step, evac=None, before=None, side_work=None):
            n = 2 * ph.loads

            def previous(i, j):
                par = (ph.pair0 + j - 1) % 2
                evac(ph.per * i + j - 1, par, (ph.pair0 + j - 1 - par) // 2 + ph.per // 2 * i)

            def body(i, first):
                for j in range(ph.per):
                    for q in range(n):
                        step(i, j, q, j * n + q)
                        if q == ph.lag - 1 and j == 0:
                            first()
                        elif q == ph.lag - 1 and evac:
                            previous(i, j)
                        if side_work:
                            side_work(i, j * n + q)

            body(0, before or (lambda: None))
            if ph.iters > 1:
                with eng.Fori(1, ph.iters) as i:
                    body(i, (lambda: previous(i, 0)) if evac else (lambda: None))
            end = ph.pairs - 1
            par = (ph.pair0 + end) % 2
            return (lambda: evac(end, par, (ph.pair0 + end - par) // 2)) if evac else None

        def none_free(ph):
            total = ph.pair0 + ph.pairs
            return [2 * ((total + 1) // 2), 2 * (total // 2)]

        CW = TP + 4 * NB

        def news(t, n):
            return t[:, n, TP + 3:TP + 3 + 4 * NB].rearrange("p (b w) -> p b w", w=4)

        def one(t, k):
            return t[:, bass.ds(k, 1)].rearrange("p o t -> p (o t)")

        def tok_dst(n):
            if n < 8:
                dst = (ktok, vtok)[n // 4][:, (n // 2) % 2, (n % 2) * 512:(n % 2) * 512 + 512]
                return dst, side[n % 4][:, :]
            return stok[:, (n - 8) * 512:(n - 7) * 512], side[n % 4][0:NB, :]

        def state_at(n):
            return n // 4, n % 4, n % 3

        def y_dst(n):
            m, c = n // 3, n % 3
            rows = P if c < 2 else NB
            return ytok[0:rows, c, m * 512:(m + 1) * 512], side[n % 4][0:rows, :]

        block = ctx.enter_context(nc.Block())

        @block.sync
        def _(sp):
            def vec(ap):
                return ap.rearrange("(k p) -> p k", p=P)

            for c in range(2):
                sp.dma_start(xtok[:, c, :], a["x_prompt"][0, c * P:(c + 1) * P, :]).then_inc(x_in, 16)
            sp.dma_start(xtok[0:NB, 2, :], a["x_sample"][:, 0, :]).then_inc(x_in, 16)

            def load(ph, i, l):
                j, kg = l // ph.loads, l % ph.loads
                kts = min(KG, ph.kt - KG * kg)
                s = (ph.load0 + l) % RING
                w = ph.ws[j % len(ph.ws)]
                pair = (ph.per * i + j) if len(ph.ws) == 1 else i
                src = w[kg * KG * P:(kg * KG + kts) * P, bass.ds(ph.col + 256 * pair, 256)]
                wait(sp, lo_done, 2 * (ph.load0 + ph.per * ph.loads * i + l - RING) + 2)
                sp.dma_start(raw[:, s, 0:kts, :], src.rearrange("(k p) n -> p k n", p=P)).then_inc(loaded[s], 16)

            def weights(ph):
                for l in range(ph.per * ph.loads):
                    load(ph, 0, l)
                if ph.iters > 1:
                    with sp.Fori(1, ph.iters) as i:
                        for l in range(ph.per * ph.loads):
                            load(ph, i, l)

            with nc.allow_non_contiguous_dma(reason="per-channel vectors"):
                for n, g in enumerate(("norm_mix_pre", "norm_mix_post", "norm_ffn_pre", "norm_ffn_post", "ssm_norm")):
                    sp.dma_start(gains[:, n, :], vec(a[g][0])).then_inc(consts_in, 16)
                for n in range(4):
                    sp.dma_start(conv_k[:, n, :], vec(a["conv_w"][0, n])).then_inc(consts_in, 16)
                sp.dma_start(conv_bias[:, :], vec(a["conv_b"][0])).then_inc(consts_in, 16)
                for n, g in enumerate(("dt_bias", "a_log")):
                    sp.dma_start(heads_c[:, n:n + 1], a[g][0].rearrange("(h o) -> h o", o=1)).then_inc(consts_in, 16)
                for h in range(2):
                    d = a["d_skip"][0].rearrange("(t h) -> h t", h=2)[h]
                    sp.dma_start(dskip[h * HD:(h + 1) * HD, :], d.partition_broadcast(HD)).then_inc(consts_in, 16)
            sp.dma_start(pages[0:1, :], a["page_table"].rearrange("b g -> (b g)").rearrange("(o n) -> o n", o=1))\
                .then_inc(pages_in, 16)
            sp.dma_start(ctok[:, :], a["state_conv"][0].rearrange("b w c -> (b w) c")).then_inc(state_in, 16)
            sp.dma_start(o["conv_sample"][0, :, 0:2, :], a["state_conv"][0, :, 1:3, :]).then_inc(cs_out, 16)
            weights(ph_qkv)
            weights(ph_dt)
            for s in tok_cp:
                sp.wait_ge(s, 7)
            for c in range(2):
                rows = slice(c * P, (c + 1) * P)
                for name, t in (("k_prompt", ktok), ("v_prompt", vtok)):
                    sp.dma_start(o[name][0, 0, rows].rearrange("s h d -> s (h d)"), t[:, c, :]).then_inc(tok_out, 16)
            sp.dma_start(q_row, stok[:, 0:AW]).then_inc(tok_out, 16)
            for n, name in enumerate(("k_sample", "v_sample")):
                sp.dma_start(o[name][0, :, 0].rearrange("b h d -> b (h d)"), stok[:, (n + 1) * AW:(n + 2) * AW])\
                    .then_inc(tok_out, 16)
            weights(ph_xbc)
            for g in range(NG):
                sp.wait_ge(fin_cp, g + 1)
                dst = o["ssm_prompt"][0, 0].rearrange("h p n -> (h p) n")[g * 256:(g + 1) * 256]
                sp.dma_start(dst.rearrange("(t p) n -> p t n", p=P), hfin[:, :, :]).then_inc(fin_out, 16)
            sp.wait_ge(bc_cp, 4)
            sp.dma_start(bc_row.rearrange("b w n -> b (w n)"), bcrow[:, :]).then_inc(bc_out, 16)
            sp.wait_ge(bc_out, 16)
            hs = a["state_ssm"][0].rearrange("b h p n -> b (h p) n")
            ho = o["ssm_sample"][0].rearrange("b h p n -> b (h p) n")

            def state_rows(x, b, r):
                return x[b, r * 512:(r + 1) * 512, :].rearrange("(t p) n -> p t n", p=P)

            sp.wait_ge(y_done, 2 * NG)
            sp.wait_ge(fin_out, 16 * NG)
            for n in range(4 * NB + 2):
                if n < 4 * NB:
                    b, r, s = state_at(n)
                    if n >= 3:
                        sp.wait_ge(st_out[s], 16 * (n // 3))
                    sp.dma_start(st[:, s], state_rows(hs, b, r)).then_inc(st_in[s], 16)
                    sp.dma_start(bc[:, s], bc_row[b, :, r * 256:(r + 1) * 256].partition_broadcast(P))\
                        .then_inc(st_in[s], 16)
                if n >= 2:
                    b, r, s = state_at(n - 2)
                    sp.wait_ge(st_sum, n - 1)
                    sp.dma_start(state_rows(ho, b, r), st[:, s]).then_inc(st_out[s], 16)
            sp.wait_ge(ct_cp, 8)
            sp.dma_start(o["conv_prompt"][0, 0], crow[0:3, :]).then_inc(ct_out, 16)
            sp.dma_start(o["conv_sample"][0, :, 2, :], crow[3:3 + NB, :]).then_inc(ct_out, 16)
            weights(ph_z)
            weights(ph_gs)
            weights(ph_ga)
            for par in range(2):
                sp.wait_ge(free_out[par], none_free(ph_ga)[par])
            sp.wait_ge(tok_out, 16 * 7)
            for s in range(3):
                sp.wait_ge(st_out[s], 16 * ((4 * NB - 1 - s) // 3 + 1))
            sp.wait_ge(ct_out, 32)
            sp.dma_start(own_qk[:, 0, :], q_row).then_inc(own_in, 16)
            sp.dma_start(own_qk[:, 1, :], o["k_sample"][0, :, 0].rearrange("b h d -> b (h d)")).then_inc(own_in, 16)
            sp.dma_start(own_v[:, :], o["v_sample"][0, :, 0].rearrange("b h d -> b (h d)")).then_inc(own_in, 16)
            kc = a["cache_k"][0].rearrange("g s h d -> g s (h d)")
            vc = a["cache_v"][0].rearrange("g s h d -> g s (h d)")

            def page_in(cache, n, freed):
                pg = sp.value_load(pages[0:1, n:n + 1], min_val=0, max_val=a["cache_k"].shape[1] - 1)
                src = cache[bass.ds(pg, 1)].rearrange("g p n -> p g n")
                wait(sp, *freed)
                sp.dma_start(kv[:, n % 4:n % 4 + 1, :], src).then_inc(kv_in[n % 4], 16)

            sp.wait_ge(pages_in, 16)
            sp.wait_ge(own_put, 1)
            for n in range(NB * NPG):
                if n % NPG == 0:
                    b = n // NPG
                    wait(sp, k_mul, NPG * (b - 1))
                    sp.dma_start(qb[:, b % 2, :], q_row[b, :].partition_broadcast(P)).then_inc(qb_in[b % 2], 16)
                page_in(kc, n, (k_red, n - 3))
            for n in range(NB * NPG):
                page_in(vc, n, (k_red, NB * NPG - 3 + n) if n < 4 else (v_mm, n - 3))
            weights(ph_so)
            weights(ph_ao)
            weights(ph_o)
            sp.wait_ge(ao_lo, KT)
            for c in range(2):
                sp.dma_start(xtok2[:, c, :], a["x_prompt"][0, c * P:(c + 1) * P, :]).then_inc(x_in, 16)
            sp.dma_start(xtok2[0:NB, 2, :], a["x_sample"][:, 0, :]).then_inc(x_in, 16)
            sp.wait_ge(x1_done, KT)
            sp.dma_start(x1_spill, x1[:, :, :].rearrange("p k t -> p (k t)")).then_inc(x1_out, 16)
            weights(ph_ff)
            weights(ph_dn)
            sp.wait_ge(x1_out, 16)
            sp.wait_ge(mm_done, block_no(ph_dn, 0, 0))
            sp.dma_start(x2[:, :, :].rearrange("p k t -> p (k t)"), x1_spill).then_inc(x1_in, 16)
            sp.wait_ge(y_cp, 6)
            sp.wait_ge(y_cp2, 6)
            for c in range(2):
                sp.dma_start(o["y_prompt"][0, c * P:(c + 1) * P, :], ytok[:, c, :]).then_inc(y_out, 16)
            sp.dma_start(o["y_sample"][:, 0, :], ytok[0:NB, 2, :]).then_inc(y_out, 16)
            sp.wait_ge(y_out, 16 * 3)
            sp.wait_ge(cs_out, 16)

        @block.gpsimd
        def _(gp):
            made = [0]

            def made_one(ins):
                made[0] += 1
                then(gp, ins, consts_made, made[0])

            made_one(gp.memset(ident[:, :], 0.0))
            made_one(gp.affine_select(out=ident[:, :], in_=ident[:, :], compare_op=ALU.not_equal, fill=1.0, base=0,
                                      pattern=[[-1, P]], channel_multiplier=1))
            made_one(gp.memset(ones[:, :], 1.0))
            made_one(gp.memset(eps[:, :], EPS))
            made_one(gp.affine_select(out=upper[:, :], in_=ones[:, :], compare_op=ALU.is_ge, fill=0.0, base=0,
                                      pattern=[[1, P]], channel_multiplier=-1))
            made_one(gp.memset(cmask[:, :], 0.0))
            for c in (0, 2):
                made_one(gp.affine_select(out=cmask[:, c * P:(c + 1) * P], in_=cmask[:, c * P:(c + 1) * P],
                                          compare_op=ALU.is_ge, fill=NEG, base=0, pattern=[[-1, P]],
                                          channel_multiplier=1))
            made_one(gp.memset(dmask[:, :], 0.0))
            made_one(gp.affine_select(out=dmask[:, :], in_=dmask[:, :], compare_op=ALU.is_equal, fill=NEG, base=0,
                                      pattern=[[-1, NB]], channel_multiplier=1))
            made_one(gp.memset(conv_in[:, :, 0:3], 0.0))
            gp.wait_ge(consts_in, 16 * 14)
            made_one(gp.tensor_scalar(out=conv_k[:, :, :], in0=conv_k[:, :, :], scalar1=0.5, scalar2=None,
                                      op0=ALU.mult))
            made_one(gp.tensor_scalar(out=conv_bias[:, :], in0=conv_bias[:, :], scalar1=0.5, scalar2=None,
                                      op0=ALU.mult))
            assert made[0] == CONSTS

            for par in range(2):
                gp.wait_ge(free_out[par], none_free(ph_qkv)[par])
            gp.wait_ge(cst_cp, 8)

            def stage_qk(i):
                for w in range(2):
                    ins = gp.tensor_copy(qk_head[:, w:w + 1, :],
                                         qkv[:, bass.ds(i + AT * w, 1), 0:TP])
                ins.then_inc(qk_staged, 1)

            def stage_v(i):
                wait(gp, pv_mm, 2 * i)
                gp.tensor_copy(v_head[:, :, :], vtok[:, :, bass.ds(P * i, P)]).then_inc(v_staged, 1)

            def conv_pair(i, j):
                base = (ph_xbc.pair0 + j) // 2 * 2 + 2 * i
                for n in range(2):
                    t = 4 * i + 2 * j + n
                    wait(gp, conv_step, 4 * t - 4)
                    gp.tensor_copy(news(conv_in, n)[:, :, 0:3],
                                   state_t[:, bass.ds(t, 1)].rearrange("p o b w -> p (o b) w")).then_inc(conv_st, 1)
                for n in range(2):
                    t = 4 * i + 2 * j + n
                    gp.wait_ge(free_out[(ph_xbc.pair0 + j) % 2], base + n + 1)
                    gp.tensor_copy(tails[:, bass.ds(t, 1), 0:3], conv_in[:, n:n + 1, TP:TP + 3])
                    gp.tensor_copy(tails[:, bass.ds(t, 1), 3:3 + NB],
                                   news(conv_in, n)[:, :, 3:4].rearrange("p b o -> p o b")).then_inc(tail_cp, 1)

            stage_qk(0)
            for s in tok_cp:
                gp.wait_ge(s, 7)

            def xbc_iter(i, more):
                stage_v(i)
                conv_pair(i, 0)
                if more:
                    gp.wait_ge(s_mm, 2 * i + 2)
                    stage_qk(i + 1)
                conv_pair(i, 1)

            xbc_iter(0, True)
            with gp.Fori(1, ph_xbc.iters - 1) as i:
                xbc_iter(i, True)
            xbc_iter(ph_xbc.iters - 1, False)
            gp.wait_ge(dt_de, 2)
            gp.wait_ge(xb_cp[0], 8)
            gp.wait_ge(xb_cp[1], 4)

            def by_head(x):
                return x.rearrange("p (h d) -> p h d", d=HD)

            for g in range(NG):
                for c in range(2):
                    wait(gp, fin_mm, g)
                    w = dend[:, c, 4 * g:4 * g + 4].unsqueeze(2).to_broadcast([P, 4, HD])
                    then(gp, gp.tensor_tensor(out=by_head(xw1[:, c]), in0=by_head(xdt[:, c, g * 256:(g + 1) * 256]),
                                              in1=w, op=ALU.mult), xw_done, 2 * g + c + 1)
                w = cdec[:, 4 * g:4 * g + 4].unsqueeze(2).to_broadcast([P, 4, HD])
                gp.tensor_tensor(out=by_head(xw[:, :]), in0=by_head(xw1[:, 0]), in1=w, op=ALU.mult).then_inc(xwf_done, 1)
            gp.wait_ge(y_done, 2 * NG)
            gp.wait_ge(fin_mm, NG)
            gp.wait_ge(fin_out, 16 * NG)
            then(gp, gp.memset(expand[:, :], 1.0), ex_made, 1)
            then(gp, gp.affine_select(out=expand[:, :], in_=expand[:, :], compare_op=ALU.is_ge, fill=0.0, base=0,
                                      pattern=[[1, D]], channel_multiplier=-HD), ex_made, 2)
            then(gp, gp.affine_select(out=expand[:, :], in_=expand[:, :], compare_op=ALU.is_ge, fill=0.0,
                                      base=HD - 1, pattern=[[-1, D]], channel_multiplier=HD), ex_made, 3)
            for n in range(NB * NPG):
                b = n // NPG
                if n % NPG == 0:
                    gp.wait_ge(qb_in[b % 2], 16 * (b // 2 + 1))
                gp.wait_ge(kv_in[n % 4], 16 * (n // 4 + 1))
                gp.tensor_tensor(out=kv[:, n % 4], in0=kv[:, n % 4], in1=qb[:, b % 2], op=ALU.mult).then_inc(k_mul, 1)

        @block.scalar
        def _(act):
            def func(out, in_, f=ACT.Copy, **kw):
                return nc.scalar.activation(out, in_, f, **kw)

            def hi_of(ph):
                def step(i, j, q, qq):
                    s, n, kts = (ph.load0 + qq // 2) % RING, qq % 2, k_tiles(ph, q)
                    if n == 0:
                        act.wait_ge(loaded[s], 16 * ((ph.load0 + qq // 2) // RING + 1 + ph.per * ph.loads // RING * i))
                    wait(act, mm_done, block_no(ph, i, qq) - RING + 1)
                    func(w_hi[:, (2 * ph.load0 + qq) % RING, 0:kts], raw[:, s, 0:kts, n * P:(n + 1) * P])\
                        .then_inc(hi_done, 1)
                return step

            def x_copies(dst, n0):
                for k in range(KT):
                    act.wait_ge(x_tr, n0 + k + 1)
                    func(dst[:, k, :], side[k % 4][:, 0:T]).then_inc(x_cp, 1)

            def root(n):
                act.wait_ge(nrm_mm, KT * (n + 1))
                wait(act, nrm_rs, n)
                func(stat[:, :], side[3][:, 0:T], ACT.Sqrt, bias=eps[:, 0:1], scale=1.0 / D).then_inc(nrm_sd, 1)

            def x_hi_from(src, n):
                for k in range(KT):
                    act.wait_ge(h_mul, KT * n + k + 1)
                    func(x_hi[:, k, :], src[:, k, :]).then_inc(h_hi, 1)

            act.wait_ge(consts_made, CONSTS)
            x_copies(xT, 0)
            root(0)
            x_hi_from(xT, 0)
            for n in range(8):
                act.wait_ge(cst_tr, n + 1)
                src = side[n % 4][:, 0:4 * 3 * NB].rearrange("p (t b w) -> p t b w", t=4, w=3)
                func(state_t[:, 4 * n:4 * n + 4], src).then_inc(cst_cp, 1)

            def qkv_evac(pr, par, gen):
                for n in range(2):
                    act.wait_ge(mm_done, last_block(ph_qkv, pr, n))
                    func(one(qkv, 2 * pr + n), gemm_ps[2 * par + n][:, 0:T]).then_inc(free_out[par], 1)

            def dt_evac(pr, par, gen):
                act.wait_ge(mm_done, last_block(ph_dt, pr, 1))
                func(dt_raw[:, :], gemm_ps[2 * par][0:SH, 0:T]).then_inc(free_out[par], 2)

            last = blocks(act, ph_qkv, hi_of(ph_qkv), qkv_evac)
            last = blocks(act, ph_dt, hi_of(ph_dt), dt_evac, last)
            last()
            for n in range(0, 14, 2):
                act.wait_ge(tok_tr, n + 1)
                func(*tok_dst(n)).then_inc(tok_cp[0], 1)

            def conv_evac(pr, par, gen):
                for n in range(2):
                    t = 2 * pr + n
                    act.wait_ge(mm_done, last_block(ph_xbc, pr, n))
                    act.wait_ge(conv_st, t + 1)
                    wait(act, tail_cp, t - 1)
                    ps = gemm_ps[2 * par + n]
                    func(conv_in[:, n, 3:3 + TP], ps[:, 0:TP])
                    func(news(conv_in, n)[:, :, 3], ps[:, TP:T]).then_inc(free_out[par], 1)
                for n in range(2):
                    t = 2 * pr + n
                    act.wait_ge(conv_step, 4 * t + 4)
                    wait(act, xbc_done, t - 1)
                    func(conv_th[:, n, :], conv_out[:, n, :], ACT.Tanh).then_inc(conv_tanh, 1)

            def attn_out(i):
                act.wait_ge(pv_mm, 2 * i + 2)
                func(attn[:, bass.ds(i, 1), 0:TP].rearrange("p o t -> p (o t)"), side[3][:, 0:TP]).then_inc(attn_cp, 1)

            def attn_act(i, qq):
                if qq == 1 and not (isinstance(i, int) and i == 0):
                    attn_out(i - 1)
                if qq in (4, 5):
                    x = qq - 4
                    act.wait_ge(s_nmax, 2 * i + x + 1)
                    wait(act, s_norm, 2 * i - 1 + x)
                    for m, cols in enumerate((slice(0, P), slice(P, 3 * P))):
                        ins = func(att_s[:, x, cols], att_s[:, x, cols], ACT.Exp, scale=SCALE,
                                   bias=att_st[:, x, 2 + m:3 + m], accum_out=att_st[:, x, 4 + m:5 + m])
                    ins.then_inc(s_exp, 1)
                if qq == 7:
                    for x in range(2):
                        act.wait_ge(pt_mm, 2 * i + x + 1)
                        wait(act, pv_mm, 2 * i - 1 + x)
                        func(att_pt[:, x, :], side[2][:, 0:3 * P]).then_inc(pt_cp, 1)

            last = blocks(act, ph_xbc, hi_of(ph_xbc), conv_evac, None, attn_act)
            last()
            attn_out(AT - 1)

            act.wait_ge(free_out[ph_dt.pair0 % 2], none_free(ph_dt)[ph_dt.pair0 % 2])
            then(act, func(dt_w[:, 0, :], dt_raw[:, :], ACT.Abs, bias=heads_c[:, 0:1]), dt_act, 1)
            then(act, func(dt_w[:, 1, :], dt_w[:, 0, :], ACT.Exp, scale=-1.0), dt_act, 2)
            then(act, func(dt_w[:, 2, :], dt_w[:, 1, :], ACT.Ln, bias=1.0), dt_act, 3)
            then(act, func(heads_c[:, 2:3], heads_c[:, 1:2], ACT.Exp), dt_act, 4)
            act.wait_ge(dt_dve, 3)
            func(dt_w[:, 3, 0:NB], dt_w[:, 4, TP:T]).then_inc(dt_act, 1)
            func(dt_w[:, 3, NB:2 * NB], dt_w[:, 5, TP:T], ACT.Exp).then_inc(dt_act, 1)
            act.wait_ge(dt_ac, 2)
            func(dend[:, :, :], dend[:, :, :], ACT.Exp).then_inc(dt_de, 1)
            func(cdec[:, :], side[1][:, 3 * SH:4 * SH], ACT.Exp).then_inc(dt_de, 1)
            for n in range(12):
                c, m = n // 6, n % 6
                if m >= 4:
                    act.wait_ge(xb_tr, n + 1)
                    func(btok[:, c, (m - 4) * 512:(m - 3) * 512], side[n % 4][:, :]).then_inc(xb_cp[1], 1)

            def fin_copy(g):
                act.wait_ge(fin_mm, g + 1)
                wait(act, fin_out, 16 * g)
                func(hfin[:, :, :], gemm_ps[3][:, 0:256].rearrange("p (t n) -> p t n", t=2)).then_inc(fin_cp, 1)

            for s in range(2 * NG):
                g, c = s // 2, s % 2
                act.wait_ge(seg_done, s + 1)
                wait(act, m_done, s - 1)
                func(dec[:, c, :], seg[:, c, :], ACT.Exp).then_inc(dec_done, 1)
                if c == 1:
                    wait(act, y_mm, s - 1)
                    func(cexp[:, :], side[1][:, :], ACT.Exp).then_inc(cx_exp, 1)
                else:
                    if g:
                        fin_copy(g - 1)
                    act.wait_ge(ht_mm, g + 1)
                    wait(act, y_mm, 2 * g)
                    func(hT0[:, :], gemm_ps[2][:, 0:256]).then_inc(ht_cp, 1)
            fin_copy(NG - 1)
            act.wait_ge(y_mm, 2 * NG)
            act.wait_ge(m_done, 2 * NG)
            act.wait_ge(xw_done, 2 * NG)
            for n in range(4):
                act.wait_ge(bc_tr, n + 1)
                func(bcrow[:, n * 512:(n + 1) * 512], side[n % 4][0:NB, :]).then_inc(bc_cp, 1)
            act.wait_ge(ex_mm, 1)
            func(scal[:, :, :], side[0][:, 0:XT * 2 * NB].rearrange("p (t n) -> p t n", n=2 * NB)).then_inc(ex_cp, 1)
            act.wait_ge(ct_tr, 1)
            for n in range(8):
                act.wait_ge(ct_tr, n + 1)
                func(crow[:, n * 512:(n + 1) * 512], side[n % 4][0:3 + NB, :]).then_inc(ct_cp, 1)
            act.wait_ge(sx_mul, 1)
            for n in range(4 * NB):
                b, r, s = state_at(n)
                act.wait_ge(st_in[s], 32 * (n // 3 + 1))
                wait(act, st_new, n)
                for t in range(4):
                    ins = func(stx[:, t, :], bc[:, s, 0, (t // 2) * P:(t // 2 + 1) * P],
                               scale=xdts[:, 4 * r + t, b:b + 1])
                ins.then_inc(stx_done, 1)

            def z_evac(pr, par, gen):
                for n in range(2):
                    t = 2 * pr + n
                    act.wait_ge(mm_done, last_block(ph_z, pr, n))
                    wait(act, u_done, t - 1)
                    func(sq[:, n, :], gemm_ps[2 * par + n][:, 0:T], ACT.Tanh, scale=0.5).then_inc(z_tanh, 1)

            act.wait_ge(ysam_done, 2)
            blocks(act, ph_z, hi_of(ph_z), z_evac)()
            for s in range(3):
                act.wait_ge(st_out[s], 16 * ((4 * NB - 1 - s) // 3 + 1))
            for g in range(NG):
                act.wait_ge(un_mm, 2 * g + 2)
                wait(act, un_rs, g - 3)
                func(un[:, 0, g % 4, :], side[g % 4][:, 0:T], ACT.Sqrt, bias=eps[:, 0:1], scale=1.0 / 256)\
                    .then_inc(un_sd, 1)

            def gate_evac(ph, gate):
                def evac(pr, par, gen):
                    for n in range(2):
                        act.wait_ge(mm_done, last_block(ph, pr, n))
                        func(one(gate, 2 * pr + n), gemm_ps[2 * par + n][:, 0:T], ACT.Tanh, scale=0.5)\
                            .then_inc(free_out[par], 1)
                return evac

            act.wait_ge(ct_out, 32)
            last = blocks(act, ph_gs, hi_of(ph_gs), gate_evac(ph_gs, gate_s))
            last = blocks(act, ph_ga, hi_of(ph_ga), gate_evac(ph_ga, gate_a), last)
            last()
            act.wait_ge(mm_done, block_no(ph_so, 0, 0))
            act.wait_ge(un_mul, KT)
            for k in range(KT):
                func(x_hi[:, k, :], xbc[:, k, :]).then_inc(u_hi, 1)
            act.wait_ge(p_sub, 1)
            func(sc[:, :, :, :], sc[:, :, :, :], ACT.Exp, scale=SCALE).then_inc(p_exp, 1)
            act.wait_ge(v_cp, 2)
            act.wait_ge(attn_cp, AT)
            for k in range(AT):
                func(a_hi[:, k, :], attn[:, k, :]).then_inc(a_hi_done, 1)

            def ao_evac(pr, par, gen):
                for n in range(2):
                    t = 2 * pr + n
                    act.wait_ge(ao_sum, t + 1)
                    func(one(x_hi, t), one(gate_a, t), scale=0.5).then_inc(ao_hi, 1)

            def copy_evac(ph, dst):
                def evac(pr, par, gen):
                    for n in range(2):
                        act.wait_ge(mm_done, last_block(ph, pr, n))
                        func(one(dst, 2 * pr + n), gemm_ps[2 * par + n][:, 0:T]).then_inc(free_out[par], 1)
                return evac

            blocks(act, ph_so, hi_of(ph_so))
            blocks(act, ph_ao, hi_of(ph_ao), ao_evac)()
            blocks(act, ph_o, hi_of(ph_o), copy_evac(ph_o, mo))()
            x_copies(x1, KT)
            root(1)
            root(2)
            act.wait_ge(mm_done, block_no(ph_ff, 0, 0))
            x_hi_from(mo, 1)

            def ff_evac(pr, par, gen):
                if par == ph_ff.pair0 % 2:
                    for n in range(2):
                        act.wait_ge(mm_done, last_block(ph_ff, pr, n))
                        func(glu[:, 0, n, :], gemm_ps[2 * par + n][:, 0:T], ACT.Tanh, scale=0.5).then_inc(ff_tanh, 1)
                else:
                    for n in range(2):
                        act.wait_ge(free_out[par], 2 * gen + n + 1)
                        func(one(g_hi, pr - 1 + n), glu[:, 2, n, :]).then_inc(ff_hi, 1)

            blocks(act, ph_ff, hi_of(ph_ff), ff_evac)()
            blocks(act, ph_dn, hi_of(ph_dn), copy_evac(ph_dn, fo))()
            root(3)
            for n in range(0, 12, 2):
                act.wait_ge(y_tr, n + 1)
                func(*y_dst(n)).then_inc(y_cp, 1)

        @block.vector
        def _(dve):
            v = nc.vector

            def mul(out, x, y):
                return v.tensor_tensor(out, x, y, ALU.mult)

            def stt(out, x, scalar, y, op0, op1):
                return v.scalar_tensor_tensor(out=out, in0=x, scalar=scalar, in1=y, op0=op0, op1=op1)

            def lo_of(ph):
                def step(i, j, q, qq):
                    s, n, kts = (ph.load0 + qq // 2) % RING, qq % 2, k_tiles(ph, q)
                    w = (2 * ph.load0 + qq) % RING
                    dve.wait_ge(hi_done, block_no(ph, i, qq) + 1)
                    v.tensor_tensor(w_lo[:, w, 0:kts], raw[:, s, 0:kts, n * P:(n + 1) * P],
                                    w_hi[:, w, 0:kts].bitcast(fp32), ALU.subtract).then_inc(lo_done, 1)
                return step

            def squares(src, n, ready=None):
                for k in range(KT):
                    if ready:
                        dve.wait_ge(ready[0], ready[1] + k + 1)
                    wait(dve, nrm_mm, KT * n + k - 1)
                    mul(sq[:, k % 2, :], src[:, k, :], src[:, k, :]).then_inc(nrm_sq, 1)

            def scale_by_norm(dst, src, n, gain, done):
                dve.wait_ge(nrm_sd, n + 1)
                then(dve, v.reciprocal(stat_r[:, :], stat[:, :]), nrm_rs, n + 1)
                for k in range(KT):
                    ins = stt(dst[:, k, :], src[:, k, :], gains[:, gain, k:k + 1], stat_r[:, :], ALU.mult, ALU.mult)
                    ins.then_inc(*done)

            def x_lo_from(src, hi, lo, done, n, count):
                for k in range(count):
                    dve.wait_ge(done[0], n + k + 1)
                    v.tensor_tensor(lo[:, k, :], src[:, k, :], hi[:, k, :].bitcast(fp32), ALU.subtract)\
                        .then_inc(done[1], 1)

            dve.wait_ge(consts_made, CONSTS)
            squares(xT, 0, (x_cp, 0))
            scale_by_norm(xT, xT, 0, 0, (h_mul, 1))
            x_lo_from(xT, x_hi, x_lo, (h_hi, h_lo), 0, KT)
            blocks(dve, ph_qkv, lo_of(ph_qkv))
            blocks(dve, ph_dt, lo_of(ph_dt))
            for n in range(1, 14, 2):
                dve.wait_ge(tok_tr, n + 1)
                v.tensor_copy(*tok_dst(n)).then_inc(tok_cp[1], 1)

            def conv_evac(pr, par, gen):
                for n in range(2):
                    t = 2 * pr + n
                    k = [conv_k[:, w, bass.ds(t, 1)] for w in range(4)]
                    dve.wait_ge(free_out[par], 2 * gen + n + 1)
                    then(dve, v.tensor_scalar(conv_out[:, n, :], conv_in[:, n, 0:CW], k[0], conv_bias[:, bass.ds(t, 1)],
                                              ALU.mult, ALU.add), conv_step, 4 * t + 1)
                    for w in range(1, 4):
                        then(dve, stt(conv_out[:, n, 0:CW], conv_in[:, n, w:w + CW], k[w],
                                      conv_out[:, n, 0:CW], ALU.mult, ALU.add), conv_step, 4 * t + 1 + w)
                for n in range(2):
                    t = 2 * pr + n
                    dve.wait_ge(conv_tanh, t + 1)
                    x = one(xbc, t)
                    stt(x[:, 0:TP], conv_th[:, n, 0:TP], 1.0, conv_out[:, n, 0:TP], ALU.add, ALU.mult)
                    new = [z[:, n, TP + 3:TP + 3 + 4 * NB - 3:4] for z in (conv_th, conv_out)]
                    stt(x[:, TP:T], new[0], 1.0, new[1], ALU.add, ALU.mult).then_inc(xbc_done, 1)

            def attn_dve(i, qq):
                if qq in (3, 4):
                    x = qq - 3
                    dve.wait_ge(s_mm, 2 * i + x + 1)
                    wait(dve, pt_mm, 2 * i - 1 + x)
                    then(dve, v.tensor_tensor(att_s[:, x, :], side[x][:, 0:3 * P], cmask[:, :], ALU.add),
                         s_masked, 2 * i + x + 1)
                    for m, cols in enumerate((slice(0, P), slice(P, 3 * P))):
                        ins = v.tensor_reduce(out=att_st[:, x, m:m + 1], in_=att_s[:, x, cols], axis=AX.X, op=ALU.max)
                    then(dve, ins, s_max, 2 * i + x + 1)
                    v.tensor_scalar(att_st[:, x, 2:4], att_st[:, x, 0:2], -SCALE, None, ALU.mult).then_inc(s_nmax, 1)
                if qq in (5, 6):
                    x = qq - 5
                    dve.wait_ge(s_exp, 2 * i + x + 1)
                    then(dve, v.reciprocal(att_st[:, x, 6:8], att_st[:, x, 4:6]), s_rcp, 2 * i + x + 1)
                    for m, cols in enumerate((slice(0, P), slice(P, 3 * P))):
                        ins = v.tensor_scalar(att_s[:, x, cols], att_s[:, x, cols], att_st[:, x, 6 + m:7 + m], None,
                                              ALU.mult)
                    ins.then_inc(s_norm, 1)

            blocks(dve, ph_xbc, lo_of(ph_xbc), conv_evac, None, attn_dve)()

            dve.wait_ge(tail_cp, CT)
            dve.wait_ge(dt_act, 4)
            then(dve, v.tensor_scalar(dt_w[:, 3, :], dt_raw[:, :], heads_c[:, 0:1], 0.0, ALU.add, ALU.max), dt_dve, 1)
            then(dve, v.tensor_tensor(dt_w[:, 4, :], dt_w[:, 3, :], dt_w[:, 2, :], ALU.add), dt_dve, 2)
            then(dve, v.tensor_scalar(dt_w[:, 5, :], dt_w[:, 4, :], heads_c[:, 2:3], -1.0, ALU.mult, ALU.mult),
                 dt_dve, 3)
            dve.wait_ge(dt_tr, 1)
            then(dve, v.tensor_copy(dtok[:, :, :, :].rearrange("p k c h -> p (k c h)"), side[0][:, 0:P]), dt_tok, 1)
            dve.wait_ge(dt_sum, 1)
            then(dve, v.tensor_copy(acum[:, :, :].rearrange("p c h -> p (c h)"), side[1][:, 0:2 * SH]), dt_ac, 1)
            v.tensor_tensor(dend[:, :, :].rearrange("p c h -> p (c h)"), side[1][:, 2 * SH:4 * SH],
                            acum[:, :, :].rearrange("p c h -> p (c h)"), ALU.subtract).then_inc(dt_ac, 1)
            for n in range(12):
                c, m = n // 6, n % 6
                if m < 4:
                    dve.wait_ge(xb_tr, n + 1)
                    w = dtok[:, 0, c, 8 * m:8 * m + 8].unsqueeze(2).to_broadcast([P, 8, HD])
                    v.tensor_tensor(xdt[:, c, m * 512:(m + 1) * 512].rearrange("p (h d) -> p h d", d=HD),
                                    side[n % 4][:, :].rearrange("p (h d) -> p h d", d=HD), w, ALU.mult)\
                        .then_inc(xb_cp[0], 1)

            def ssd_seg(s):
                g, c = s // 2, s % 2
                dve.wait_ge(r_mm, s + 1)
                wait(dve, y_mm, s - 1)
                for h in range(4):
                    ins = v.tensor_scalar(seg[:, c, h * P:(h + 1) * P], side[c][:, h * P:(h + 1) * P],
                                          acum[:, c, 4 * g + h:4 * g + h + 1], 0.0, ALU.subtract, ALU.min)
                ins.then_inc(seg_done, 1)
                dve.wait_ge(cb_mm, s + 1)
                mul(cbm[:, c, :], side[2 + c][:, 0:P], upper[:, :]).then_inc(cbm_done, 1)

            def ssd_y(s):
                g, c = s // 2, s % 2
                dve.wait_ge(y_mm, s + 1)
                for t in range(2):
                    x = xbc[:, 2 * g + t, c * P:(c + 1) * P]
                    ins = stt(x, x, dskip[:, 2 * g + t:2 * g + t + 1], gemm_ps[c][:, t * P:(t + 1) * P],
                              ALU.mult, ALU.add)
                ins.then_inc(y_done, 1)

            ssd_seg(0)
            for s in range(2 * NG):
                g, c = s // 2, s % 2
                if s + 1 < 2 * NG:
                    ssd_seg(s + 1)
                dve.wait_ge(dec_done, s + 1)
                dve.wait_ge(cbm_done, s + 1)
                mul(seg[:, c, :].rearrange("p (h i) -> p h i", h=4), dec[:, c, :].rearrange("p (h i) -> p h i", h=4),
                    cbm[:, c, :].unsqueeze(1).to_broadcast([P, 4, P])).then_inc(m_done, 1)
                if c == 1:
                    dve.wait_ge(cx_exp, g + 1)
                    cx = cexp[:, :].rearrange("p (h i) -> p h i", h=4)
                    mul(cx, cx, xbc[:, XT + NG + g, P:2 * P].unsqueeze(1).to_broadcast([P, 4, P])).then_inc(cx_done, 1)
                if s:
                    ssd_y(s - 1)
            ssd_y(2 * NG - 1)
            dve.wait_ge(ex_cp, 1)
            mul(xdts[:, :, :], xbc[:, 0:XT, TP:T], scal[:, :, 0:NB]).then_inc(sx_mul, 1)
            for n in range(4 * NB):
                b, r, s = state_at(n)
                dve.wait_ge(stx_done, n + 1)
                for t in range(4):
                    ins = stt(st[:, s, t, :], st[:, s, t, :], scal[:, 4 * r + t, NB + b:NB + b + 1], stx[:, t, :],
                              ALU.mult, ALU.add)
                then(dve, ins, st_new, n + 1)
                cb = bc[:, s, 1, :].rearrange("p (g n) -> p g n", g=2).unsqueeze(2).to_broadcast([P, 2, 2, P])
                then(dve, mul(sty[:, :, :].rearrange("p (g t) n -> p g t n", g=2),
                              st[:, s].rearrange("p (g t) n -> p g t n", g=2), cb), st_prod, n + 1)
                v.tensor_reduce(out=ysam[:, 4 * r:4 * r + 4, b], in_=sty[:, :, :], axis=AX.X, op=ALU.add)\
                    .then_inc(st_sum, 1)
            dve.wait_ge(st_sum, 4 * NB)
            xn = xbc[:, 0:XT, TP:T]
            then(dve, mul(xn, xn, dskip[:, :].unsqueeze(2).to_broadcast([P, XT, NB])), ysam_done, 1)
            v.tensor_tensor(xn, xn, ysam[:, :, :], ALU.add).then_inc(ysam_done, 1)

            def z_evac(pr, par, gen):
                for n in range(2):
                    t = 2 * pr + n
                    dve.wait_ge(z_tanh, t + 1)
                    then(dve, stt(tmp[:, n, :], sq[:, n, :], 1.0, gemm_ps[2 * par + n][:, 0:T], ALU.add, ALU.mult),
                         free_out[par], 2 * gen + n + 1)
                    stt(one(xbc, t), tmp[:, n, :], 0.5, one(xbc, t), ALU.mult, ALU.mult).then_inc(u_done, 1)

            dve.wait_ge(ysam_done, 2)
            blocks(dve, ph_z, lo_of(ph_z), z_evac)()
            dve.wait_ge(u_done, KT)
            for k in range(KT):
                wait(dve, un_mm, k - 1)
                mul(sq[:, k % 2, :], xbc[:, k, :], xbc[:, k, :]).then_inc(un_sq, 1)
            for g in range(NG):
                dve.wait_ge(un_sd, g + 1)
                then(dve, v.reciprocal(un[:, 1, g % 4, :], un[:, 0, g % 4, :]), un_rs, g + 1)
                for k in (2 * g, 2 * g + 1):
                    stt(xbc[:, k, :], xbc[:, k, :], gains[:, 4, k:k + 1], un[:, 1, g % 4, :], ALU.mult, ALU.mult)\
                        .then_inc(un_mul, 1)
            blocks(dve, ph_gs, lo_of(ph_gs))
            blocks(dve, ph_ga, lo_of(ph_ga))
            x_lo_from(xbc, x_hi, x_lo, (u_hi, u_lo), 0, KT)

            dve.wait_ge(own_in, 48)
            qk = own_qk[:, 0, :]
            then(dve, mul(qk, qk, own_qk[:, 1, :]), own_mul, 1)
            then(dve, v.tensor_reduce(out=m_w[0:NB, 0, 0:HEADS], in_=qk.rearrange("p (h d) -> p h d", d=HD), axis=AX.X,
                                      op=ALU.add), own_sum, 1)
            then(dve, v.tensor_copy(sc[:, NPG], dmask[:, :].unsqueeze(2).to_broadcast([P, NB, HEADS])), own_sum, 2)
            v.tensor_tensor(sc[0:NB, NPG], sc[0:NB, NPG],
                            m_w[0:NB, 0, 0:HEADS].unsqueeze(1).to_broadcast([NB, NB, HEADS]), ALU.add)\
                .then_inc(own_put, 1)
            for n in range(NB * NPG):
                dve.wait_ge(k_mul, n + 1)
                v.tensor_reduce(out=sc[:, n % NPG, n // NPG, :], in_=kv[:, n % 4].rearrange("p (h d) -> p h d", d=HD),
                                axis=AX.X, op=ALU.add).then_inc(k_red, 1)
            dve.wait_ge(sel_mm, 1)
            step = [0]

            def sel(ins):
                step[0] += 1
                then(dve, ins, sel_dve, step[0])

            scp = sc[:, :, :, :].rearrange("p g b h -> p g (b h)")
            dve.wait_ge(own_put, 1)
            for n in range(2):
                sel(v.tensor_reduce(out=m_w[:, 2 * n:2 * n + 2, :],
                                    in_=side[n][:, :].rearrange("p (k u x) -> p k x u", u=2, x=P), axis=AX.X,
                                    op=ALU.add))
            low, eq, rest = m_w[:, 4, :], m_w[:, 5, :], m_w[:, 6, :]
            sel(v.tensor_tensor(low, m_w[:, 0, :], m_w[:, 1, :], ALU.min))
            sel(v.tensor_tensor(eq, m_w[:, 2, :], m_w[:, 3, :], ALU.min))
            sel(v.tensor_tensor(low, low, eq, ALU.min))
            sel(v.tensor_tensor(m_w[:, 3, :], m_w[:, 3, :], low, ALU.is_equal))
            sel(v.tensor_scalar(rest, m_w[:, 3, :], -1.0, 1.0, ALU.mult, ALU.add))
            for n in (2, 1):
                sel(v.tensor_tensor(eq, m_w[:, n, :], low, ALU.is_equal))
                sel(mul(m_w[:, n, :], eq, rest))
                sel(v.tensor_tensor(rest, rest, m_w[:, n, :], ALU.subtract))
            for n in range(NBLK):
                drop = (rest if n == 0 else m_w[:, n, :]).unsqueeze(1).to_broadcast([P, 2, P])
                sel(stt(scp[:, 2 * n:2 * n + 2], drop, NEG, scp[:, 2 * n:2 * n + 2], ALU.mult, ALU.add))
            v.tensor_reduce(out=m_w[:, 5, :], in_=scp.rearrange("p g x -> p x g"), axis=AX.X, op=ALU.max)\
                .then_inc(max_dve, 1)
            dve.wait_ge(max_tr, 1)
            then(dve, v.tensor_reduce(out=m_w[:, 6, 0:1], in_=side[2][:, 0:P], axis=AX.X, op=ALU.max), max_dve, 2)
            v.tensor_scalar(m_w[:, 7, :], ident[:, :], m_w[:, 6, 0:1], None, ALU.mult).then_inc(max_dve, 1)
            dve.wait_ge(max_mm, 1)
            every = [P, NPG + 1, P]
            v.tensor_tensor(scp, scp, side[3][:, 0:P].unsqueeze(1).to_broadcast(every), ALU.subtract).then_inc(p_sub, 1)
            dve.wait_ge(p_exp, 1)
            v.tensor_reduce(out=m_w[:, 8, :], in_=scp.rearrange("p g x -> p x g"), axis=AX.X, op=ALU.add)\
                .then_inc(p_sum, 1)
            dve.wait_ge(p_mm, 1)
            then(dve, v.reciprocal(m_w[:, 9, :], side[0][:, 0:P]), p_rcp, 1)
            mul(scp, scp, m_w[:, 9, :].unsqueeze(1).to_broadcast(every)).then_inc(p_done, 1)
            dve.wait_ge(v_mm, NB * NPG + 1)
            acc = side[1][:, 0:P].rearrange("p (b k e) -> p k b e", b=NB, e=2)
            for e in range(2):
                rows = slice(e * HD, (e + 1) * HD)
                v.tensor_copy(attn[rows, :, TP:T], acc[rows, :, :, e]).then_inc(v_cp, 1)
            x_lo_from(attn, a_hi, a_lo, (a_hi_done, a_lo_done), 0, AT)

            def so_evac(pr, par, gen):
                for n in range(2):
                    t = one(gate_s, 2 * pr + n)
                    dve.wait_ge(mm_done, last_block(ph_so, pr, n))
                    stt(t, t, 1.0, gemm_ps[2 * par + n][:, 0:T], ALU.add, ALU.mult).then_inc(free_out[par], 1)

            def ao_evac(pr, par, gen):
                for n in range(2):
                    t = 2 * pr + n
                    ga, gs = one(gate_a, t), one(gate_s, t)
                    dve.wait_ge(mm_done, last_block(ph_ao, pr, n))
                    then(dve, stt(ga, ga, 1.0, gemm_ps[2 * par + n][:, 0:T], ALU.add, ALU.mult),
                         free_out[par], 2 * gen + n + 1)
                    v.tensor_tensor(ga, ga, gs, ALU.add).then_inc(ao_sum, 1)
                for n in range(2):
                    t = 2 * pr + n
                    dve.wait_ge(ao_hi, t + 1)
                    stt(one(x_lo, t), one(gate_a, t), 0.5, one(x_hi, t).bitcast(fp32), ALU.mult, ALU.subtract)\
                        .then_inc(ao_lo, 1)

            last = blocks(dve, ph_so, lo_of(ph_so), so_evac)
            blocks(dve, ph_ao, lo_of(ph_ao), ao_evac, last)()
            blocks(dve, ph_o, lo_of(ph_o))
            for par in range(2):
                dve.wait_ge(free_out[par], none_free(ph_o)[par])
            squares(mo, 1)
            scale_by_norm(mo, mo, 1, 1, (o_scaled, 1))
            for k in range(KT):
                dve.wait_ge(x_cp, KT + k + 1)
                dve.wait_ge(o_scaled, k + 1)
                v.tensor_tensor(x1[:, k, :], x1[:, k, :], mo[:, k, :], ALU.add).then_inc(x1_done, 1)
            squares(x1, 2, (x1_done, 0))
            scale_by_norm(mo, x1, 2, 2, (h_mul, 1))
            x_lo_from(mo, x_hi, x_lo, (h_hi, h_lo), KT, KT)

            def ff_evac(pr, par, gen):
                other = 1 - par
                if par == ph_ff.pair0 % 2:
                    for n in range(2):
                        dve.wait_ge(ff_tanh, pr + n + 1)
                        stt(glu[:, 1, n, :], glu[:, 0, n, :], 1.0, gemm_ps[2 * par + n][:, 0:T], ALU.add, ALU.mult)\
                            .then_inc(free_out[par], 1)
                else:
                    for n in range(2):
                        dve.wait_ge(mm_done, last_block(ph_ff, pr, n))
                        dve.wait_ge(free_out[other], 2 * (gen - ph_ff.pair0 % 2) + n + 1)
                        stt(glu[:, 2, n, :], glu[:, 1, n, :], 0.5, gemm_ps[2 * par + n][:, 0:T], ALU.mult, ALU.mult)\
                            .then_inc(free_out[par], 1)
                    for n in range(2):
                        t = pr - 1 + n
                        dve.wait_ge(ff_hi, t + 1)
                        v.tensor_tensor(one(g_lo, t), glu[:, 2, n, :], one(g_hi, t).bitcast(fp32), ALU.subtract)\
                            .then_inc(ff_lo, 1)

            dve.wait_ge(x1_out, 16)
            blocks(dve, ph_ff, lo_of(ph_ff), ff_evac)()
            blocks(dve, ph_dn, lo_of(ph_dn))
            for par in range(2):
                dve.wait_ge(free_out[par], none_free(ph_dn)[par])
            squares(fo, 3)
            scale_by_norm(fo, fo, 3, 3, (f_scaled, 1))
            dve.wait_ge(x1_in, 16)
            for k in range(KT):
                dve.wait_ge(f_scaled, k + 1)
                v.tensor_tensor(x2[:, k, :], x2[:, k, :], fo[:, k, :], ALU.add).then_inc(y2_done, 1)
            for n in range(1, 12, 2):
                dve.wait_ge(y_tr, n + 1)
                v.tensor_copy(*y_dst(n)).then_inc(y_cp2, 1)

        @block.tensor
        def _(pe):
            mm = nc.tensor.matmul

            def turn(out, in_):
                k = in_.shape[0]
                return mm(out, in_, ident[0:k, 0:k], start=True, stop=True)

            def mm_of(ph):
                def step(i, j, q, qq):
                    n, kg, kts = q % 2, q // 2, k_tiles(ph, q)
                    par = (ph.pair0 + j) % 2
                    if q == 0:
                        wait(pe, free_out[par], 2 * ((ph.pair0 + j) // 2 + ph.per // 2 * i))
                    pe.wait_ge(lo_done, block_no(ph, i, qq) + 1)
                    w = (2 * ph.load0 + qq) % RING
                    out = gemm_ps[2 * par + n][:, 0:T]
                    for k in range(kts):
                        x = kg * KG + k
                        mm(out, w_hi[:, w, k], ph.hi[:, x], start=(x == 0), stop=False)
                        mm(out, w_hi[:, w, k], ph.lo[:, x], start=False, stop=False)
                        ins = mm(out, w_lo[:, w, k], ph.hi[:, x], start=False, stop=(x == ph.kt - 1))
                    ins.then_inc(mm_done, 1)
                return step

            def x_turns(src, n0):
                for k in range(KT):
                    if n0:
                        wait(pe, x_cp, n0 + k - 3)
                    else:
                        wait(pe, x_cp, k - 3)
                    cols = slice(k * P, (k + 1) * P)
                    for c in range(2):
                        turn(side[k % 4][:, c * P:(c + 1) * P], src[:, c, cols])
                    turn(side[k % 4][:, TP:T], src[0:NB, 2, cols]).then_inc(x_tr, 1)

            def norm_sums(n, out):
                for k in range(KT):
                    pe.wait_ge(nrm_sq, KT * n + k + 1)
                    mm(out[:, 0:T], ones[:, :], sq[:, k % 2, :], start=(k == 0), stop=(k == KT - 1)).then_inc(nrm_mm, 1)

            pe.wait_ge(consts_made, 3)
            pe.wait_ge(x_in, 48)
            x_turns(xtok, 0)
            pe.wait_ge(x_cp, KT)
            norm_sums(0, side[3])
            pe.wait_ge(state_in, 16)
            pe.wait_ge(nrm_sd, 1)
            for n in range(8):
                wait(pe, cst_cp, n - 3)
                for u in range(4):
                    t = 4 * n + u
                    ins = turn(side[n % 4][:, u * 24:(u + 1) * 24], ctok[:, t * P:(t + 1) * P])
                ins.then_inc(cst_tr, 1)
            pe.wait_ge(h_lo, KT)
            blocks(pe, ph_qkv, mm_of(ph_qkv))
            blocks(pe, ph_dt, mm_of(ph_dt))
            pe.wait_ge(cst_cp, 8)
            for par in range(2):
                pe.wait_ge(free_out[par], none_free(ph_dt)[par])
            for n in range(14):
                wait(pe, tok_cp[n % 2], (n - 4) // 2 + 1)
                if n < 8:
                    for u in range(4):
                        src = qkv[:, AT * (1 + n // 4) + 4 * (n % 2) + u, (n // 2) % 2 * P:((n // 2) % 2 + 1) * P]
                        ins = turn(side[n % 4][:, u * P:(u + 1) * P], src)
                else:
                    for u in range(4):
                        ins = turn(side[n % 4][0:NB, u * P:(u + 1) * P], qkv[:, 4 * (n - 8) + u, TP:T])
                ins.then_inc(tok_tr, 1)
            for s in tok_cp:
                pe.wait_ge(s, 7)

            def attn_pe(i, qq):
                if qq in (0, 1):
                    x = qq
                    if x == 0:
                        pe.wait_ge(qk_staged, i + 1)
                    wait(pe, s_masked, 2 * i - 1 + x)
                    q, k = (qk_head[x * HD:(x + 1) * HD, w, :] for w in range(2))
                    mm(side[x][:, 0:P], q[:, 0:P], k[:, 0:P], start=True, stop=True)
                    mm(side[x][:, P:3 * P], q[:, P:TP], k[:, 0:TP], start=True, stop=True).then_inc(s_mm, 1)
                if qq in (4, 5):
                    x = qq - 4
                    pe.wait_ge(s_norm, 2 * i + x + 1)
                    wait(pe, pt_cp, 2 * i + x)
                    for m in range(3):
                        ins = turn(side[2][:, m * P:(m + 1) * P], att_s[:, x, m * P:(m + 1) * P])
                    ins.then_inc(pt_mm, 1)
                if qq == 7:
                    pe.wait_ge(v_staged, i + 1)
                    wait(pe, attn_cp, i)
                    for x in range(2):
                        pe.wait_ge(pt_cp, 2 * i + x + 1)
                        rows = slice(x * HD, (x + 1) * HD)
                        mm(side[3][rows, 0:TP], v_head[:, 0, rows], att_pt[:, x, 0:TP], start=True, stop=False)
                        mm(side[3][rows, P:TP], v_head[:, 1, rows], att_pt[:, x, TP:3 * P], start=False, stop=True)\
                            .then_inc(pv_mm, 1)

            def xbc_step(ph):
                step = mm_of(ph)

                def both(i, j, q, qq):
                    attn_pe(i, qq) if qq < 7 else None
                    step(i, j, q, qq)
                    attn_pe(i, qq) if qq == 7 else None
                return both

            blocks(pe, ph_xbc, xbc_step(ph_xbc))

            pe.wait_ge(dt_dve, 3)
            pe.wait_ge(attn_cp, AT)
            for par in range(2):
                pe.wait_ge(free_out[par], none_free(ph_xbc)[par])
            for w in range(2):
                for c in range(2):
                    ins = turn(side[0][:, (2 * w + c) * SH:(2 * w + c + 1) * SH], dt_w[:, 4 + w, c * P:(c + 1) * P])
            ins.then_inc(dt_tr, 1)
            pe.wait_ge(dt_tok, 1)
            for w, m in enumerate((upper, ones)):
                for c in range(2):
                    ins = mm(side[1][:, (2 * w + c) * SH:(2 * w + c + 1) * SH], m[:, :], dtok[:, 1, c, :],
                             start=True, stop=True)
            ins.then_inc(dt_sum, 1)
            pe.wait_ge(dt_de, 2)
            pe.wait_ge(xbc_done, CT)

            def copied(n):
                if n >= 0:
                    c, m = n // 6, n % 6
                    pe.wait_ge(xb_cp[m // 4], 4 * c + m + 1 if m < 4 else 2 * c + m - 3)

            for n in range(12):
                c, m = n // 6, n % 6
                copied(n - 4)
                for u in range(4):
                    ins = turn(side[n % 4][:, u * P:(u + 1) * P], xbc[:, 4 * m + u, c * P:(c + 1) * P])
                ins.then_inc(xb_tr, 1)
            for n in range(8, 12):
                copied(n)

            def ssd_rc(s):
                g, c = s // 2, s % 2
                wait(pe, seg_done, s - 1)
                if c:
                    wait(pe, cx_exp, g)
                for h in range(4):
                    ins = mm(side[c][:, h * P:(h + 1) * P], dtok[:, 1, c, 4 * g + h:4 * g + h + 1].to_broadcast([P, P]),
                             upper[:, :], start=True, stop=True)
                ins.then_inc(r_mm, 1)
                wait(pe, cbm_done, s - 1)
                mm(side[2 + c][:, 0:P], xbc[:, XT + g, c * P:(c + 1) * P], xbc[:, XT + NG + g, c * P:(c + 1) * P],
                   start=True, stop=True).then_inc(cb_mm, 1)

            ssd_rc(0)
            for s in range(2 * NG):
                g, c = s // 2, s % 2
                if s + 1 < 2 * NG:
                    ssd_rc(s + 1)
                if c == 0:
                    pe.wait_ge(xw_done, 2 * g + 1)
                    wait(pe, ht_cp, g)
                    mm(gemm_ps[2][:, 0:256], btok[:, 0, g * P:(g + 1) * P], xw1[:, 0, :], start=True, stop=True)\
                        .then_inc(ht_mm, 1)
                pe.wait_ge(m_done, s + 1)
                if c:
                    pe.wait_ge(cx_done, g + 1)
                    pe.wait_ge(ht_cp, g + 1)
                wait(pe, y_done, s - 1)
                for h in range(4):
                    out = gemm_ps[c][(h % 2) * HD:(h % 2 + 1) * HD, (h // 2) * P:(h // 2 + 1) * P]
                    ins = mm(out, xdt[:, c, (4 * g + h) * HD:(4 * g + h + 1) * HD], seg[:, c, h * P:(h + 1) * P],
                             start=True, stop=(c == 0))
                    if c:
                        ins = mm(out, hT0[:, h * HD:(h + 1) * HD], cexp[:, h * P:(h + 1) * P], start=False, stop=True)
                ins.then_inc(y_mm, 1)
                if c:
                    pe.wait_ge(xwf_done, g + 1)
                    pe.wait_ge(xw_done, 2 * g + 2)
                    wait(pe, fin_cp, g)
                    for t in range(2):
                        out, cols = gemm_ps[3][:, t * P:(t + 1) * P], slice(t * P, (t + 1) * P)
                        mm(out, xw[:, cols], btok[:, 0, g * P:(g + 1) * P], start=True, stop=False)
                        ins = mm(out, xw1[:, 1, cols], btok[:, 1, g * P:(g + 1) * P], start=False, stop=True)
                    ins.then_inc(fin_mm, 1)
            pe.wait_ge(seg_done, 2 * NG)
            pe.wait_ge(cx_exp, NG)
            pe.wait_ge(cbm_done, 2 * NG)
            for n in range(4):
                for u in range(4):
                    ins = turn(side[n][0:NB, u * P:(u + 1) * P], xbc[:, XT + 4 * n + u, TP:T])
                ins.then_inc(bc_tr, 1)
            pe.wait_ge(bc_cp, 4)
            pe.wait_ge(ex_made, 3)
            pe.wait_ge(dt_act, 6)
            for t in range(XT):
                ins = mm(side[0][:, t * 2 * NB:(t + 1) * 2 * NB], expand[:, t * P:(t + 1) * P], dt_w[:, 3, 0:2 * NB],
                         start=True, stop=True)
            ins.then_inc(ex_mm, 1)
            pe.wait_ge(ex_cp, 1)
            pe.wait_ge(tail_cp, CT)
            for n in range(8):
                wait(pe, ct_cp, n - 3)
                for u in range(4):
                    ins = turn(side[n % 4][0:3 + NB, u * P:(u + 1) * P], tails[:, 4 * n + u, :])
                ins.then_inc(ct_tr, 1)
            pe.wait_ge(y_done, 2 * NG)
            pe.wait_ge(fin_cp, NG)
            blocks(pe, ph_z, mm_of(ph_z))
            pe.wait_ge(ct_cp, 8)
            for k in range(KT):
                g = k // 2
                pe.wait_ge(un_sq, k + 1)
                wait(pe, un_sd, g - 3)
                mm(side[g % 4][:, 0:T], ones[:, :], sq[:, k % 2, :], start=(k % 2 == 0), stop=(k % 2 == 1))\
                    .then_inc(un_mm, 1)
            blocks(pe, ph_gs, mm_of(ph_gs))
            blocks(pe, ph_ga, mm_of(ph_ga))
            pe.wait_ge(un_sd, NG)
            pe.wait_ge(k_red, NB * NPG)
            for n in range(2):
                ins = mm(side[n][:, :], ones[:, :], sc[:, 4 * n:4 * n + 4].rearrange("p g b h -> p (g b h)"),
                         start=True, stop=True)
            ins.then_inc(sel_mm, 1)
            pe.wait_ge(max_dve, 1)
            turn(side[2][:, 0:P], m_w[:, 5, :]).then_inc(max_tr, 1)
            pe.wait_ge(max_dve, 3)
            mm(side[3][:, 0:P], ones[:, :], m_w[:, 7, :], start=True, stop=True).then_inc(max_mm, 1)
            pe.wait_ge(p_sum, 1)
            mm(side[0][:, 0:P], ones[:, :], m_w[:, 8, :], start=True, stop=True).then_inc(p_mm, 1)
            pe.wait_ge(p_done, 1)
            for n in range(NB * NPG):
                b, g = n // NPG, n % NPG
                pe.wait_ge(kv_in[n % 4], 16 * (NB * NPG // 4 + n // 4 + 1))
                for k in range(AT):
                    c = 16 * b + 2 * k
                    ins = mm(side[1][:, c:c + 2], kv[:, n % 4, k * P:(k + 1) * P], sc[:, g, b, 2 * k:2 * k + 2],
                             start=(n == 0 and k == 0), stop=False, skip_group_check=True)
                ins.then_inc(v_mm, 1)
            pe.wait_ge(own_in, 48)
            for b in range(NB):
                for k in range(AT):
                    c = 16 * b + 2 * k
                    ins = mm(side[1][:, c:c + 2], own_v[:, k * P:(k + 1) * P], sc[0:NB, NPG, b, 2 * k:2 * k + 2],
                             start=False, stop=(b == NB - 1 and k == AT - 1), skip_group_check=True)
            ins.then_inc(v_mm, 1)
            pe.wait_ge(u_lo, KT)
            blocks(pe, ph_so, mm_of(ph_so))
            pe.wait_ge(a_lo_done, AT)
            blocks(pe, ph_ao, mm_of(ph_ao))
            pe.wait_ge(ao_lo, KT)
            blocks(pe, ph_o, mm_of(ph_o))
            pe.wait_ge(x_in, 96)
            pe.wait_ge(v_cp, 2)
            x_turns(xtok2, KT)
            pe.wait_ge(x_cp, 2 * KT)
            norm_sums(1, side[3])
            pe.wait_ge(nrm_sd, 2)
            norm_sums(2, side[3])
            pe.wait_ge(h_lo, 2 * KT)
            blocks(pe, ph_ff, mm_of(ph_ff))
            pe.wait_ge(ff_lo, FT)
            blocks(pe, ph_dn, mm_of(ph_dn))
            pe.wait_ge(nrm_sd, 3)
            norm_sums(3, side[3])
            pe.wait_ge(y2_done, KT)
            pe.wait_ge(nrm_sd, 4)
            for n in range(12):
                m = n // 3
                wait(pe, (y_cp, y_cp2)[n % 2], (n - 4) // 2 + 1)
                c = n % 3
                for u in range(4):
                    out = side[n % 4][0:(P if c < 2 else NB), u * P:(u + 1) * P]
                    ins = turn(out, x2[:, 4 * m + u, c * P:(c + 1) * P if c < 2 else T])
                ins.then_inc(y_tr, 1)


_INS = ["x_prompt", "x_sample", "cache_k", "cache_v", "state_conv", "state_ssm", "page_table",
        "norm_mix_pre", "w_in", "conv_w", "conv_b", "dt_bias", "a_log", "d_skip", "ssm_norm",
        "w_attn_out", "w_ssm_out", "w_out", "norm_mix_post",
        "norm_ffn_pre", "w_gate", "w_up", "w_down", "norm_ffn_post"]
_OUTS = [("y_prompt", (1, TP, D)), ("y_sample", (NB, 1, D)),
         ("k_prompt", (1, 1, TP, HEADS, HD)), ("v_prompt", (1, 1, TP, HEADS, HD)),
         ("conv_prompt", (1, 1, 3, CONVC)), ("ssm_prompt", (1, 1, SH, HD, NST)),
         ("k_sample", (1, NB, 1, HEADS, HD)), ("v_sample", (1, NB, 1, HEADS, HD)),
         ("conv_sample", (1, NB, 3, CONVC)), ("ssm_sample", (1, NB, SH, HD, NST))]


def kernel(**inputs):
    import numpy as np
    import concourse.bacc as bacc
    from concourse.bass_utils import run_bass_kernel_spmd

    nc = bacc.Bacc("TRN2", target_bir_lowering=False, num_devices=1)
    arrays, a, o = {}, {}, {}
    for name in _INS:
        x = np.ascontiguousarray(inputs[name])
        arrays[f"in_{name}"] = x
        a[name] = nc.dram_tensor(f"in_{name}", x.shape, mybir.dt.from_np(x.dtype), kind="ExternalInput").ap()
    for name, shape in _OUTS:
        o[name] = nc.dram_tensor(f"out_{name}", shape, fp32, kind="ExternalOutput").ap()
    bass_hybrid_decoder_layer(nc, a, o)
    r = run_bass_kernel_spmd(nc, [arrays], core_ids=[0])
    return tuple(r.results[0][f"out_{name}"] for name, _ in _OUTS)
```

```python
import concourse.bass as bass
from concourse import mybir
from contextlib import ExitStack

fp32 = mybir.dt.float32
f32r = mybir.dt.float32r
i32 = mybir.dt.int32
ALU = mybir.AluOpType
ACT = mybir.ActivationFunctionType
AX = mybir.AxisListType

P = 128
D = 2048
KT = D // P
TP = 256
NB = 8
T = TP + NB
HEADS = 16
HD = 64
AW = HEADS * HD
AT = AW // P
SH = 32
NG = 8
NST = 128
XT = 16
CT = XT + 2 * NG
FF = 5632
FT = FF // P
PAST = 1024
PG = 128
NPG = PAST // PG
NBLK = 4
EPS = 1e-6
NEG = -1e30
SCALE = HD ** -0.5
CONVC = CT * P
COL_Q, COL_Z, COL_X, COL_DT, COL_GA, COL_GS = 0, 3072, 5120, 9216, 9248, 11296
KG = 8
RING = 4
LAG = 3


def bass_hybrid_decoder_layer(nc, a, o):
    ctx = ExitStack()
    with ctx:
        def sem(name):
            return ctx.enter_context(nc.semaphore(name))

        base = (nc.sbuf_base + 63) // 64 * 64
        room = [base]

        def keep(name, shape, dt=fp32):
            n = 4
            for s in shape[1:]:
                n *= s
            t = nc.alloc_sbuf_tensor_at(name, shape, dt, offset=room[0])
            room[0] += (n + 63) // 64 * 64
            return t

        raw = keep("raw", [P, RING, KG, 256])
        w_hi = keep("w_hi", [P, RING, KG, P], f32r)
        w_lo = keep("w_lo", [P, RING, KG, P], f32r)
        ident = keep("ident", [P, P])
        ones = keep("ones", [P, P])
        upper = keep("upper", [P, P])
        dmask = keep("dmask", [P, NB])
        hmask = keep("hmask", [P, HEADS])
        bsel = keep("bsel", [P, NB])
        eps = keep("eps", [P, 1])
        zero = keep("zero", [P, 1])
        gains = keep("gains", [P, 5, KT])
        conv_k = keep("conv_k", [P, 4, CT])
        conv_bias = keep("conv_bias", [P, CT])
        dskip = keep("dskip", [P, XT])
        heads_c = keep("heads_c", [SH, 4])
        pages = keep("pages", [1, NB * NPG], i32)
        stat = keep("stat", [P, T])
        stat_r = keep("stat_r", [P, T])
        sq = keep("sq", [P, 2, T])
        tmp = keep("tmp", [P, 2, T])
        arena = room[0]
        room_end = nc.sbuf_usable_end - 64

        def at(name, shape, dt, offset):
            n = 4
            for s in shape[1:]:
                n *= s
            assert arena + offset + n <= room_end, (name, arena + offset + n - room_end)
            return nc.alloc_sbuf_tensor_at(name, shape, dt, offset=arena + offset)

        K = 1024
        M0 = (room_end - arena - 16 * K) // 64 * 64
        attn = at("attn", [P, AT, T], fp32, M0)
        tails = at("tails", [P, CT, 3 + NB], fp32, M0 + AT * T * 4)
        state_t = at("state_t", [P, CT, NB, 3], fp32, M0 + 10 * K)
        cmask = at("cmask", [P, 3 * P], fp32, M0 + 13 * K)
        dt_raw = at("dt_raw", [SH, T], fp32, M0 + 14 * K + 512)
        TILE16 = KT * T * 4
        x_hi = at("x_hi", [P, KT, T], f32r, 0)
        x_lo = at("x_lo", [P, KT, T], f32r, TILE16)
        A0 = 2 * TILE16
        xtok = at("xtok", [P, 3, D], fp32, A0)
        xT = at("xT", [P, KT, T], fp32, A0 + 24 * K)
        ctok = at("ctok", [24, CONVC], fp32, A0 + 42 * K)
        xbc = at("xbc", [P, CT, T], fp32, A0)
        A1 = A0 + 2 * TILE16
        qkv = at("qkv", [P, 24, T], fp32, A1)
        A2 = A1 + 24 * T * 4
        vtok = at("vtok", [P, 2, AW], fp32, A2)
        att_s = at("att_s", [P, 2, 3 * P], fp32, A2 + 8 * K)
        att_pt = at("att_pt", [P, 2, 3 * P], fp32, A2 + 11 * K)
        att_st = at("att_st", [P, 2, 8], fp32, A2 + 14 * K)
        qk_head = at("qk_head", [P, 2, TP], fp32, A2 + 14 * K + 64)
        v_head = at("v_head", [P, 2, P], fp32, A2 + 16 * K + 64)
        conv_in = at("conv_in", [P, 2, 3 + TP + 4 * NB], fp32, A2 + 17 * K + 64)
        conv_out = at("conv_out", [P, 2, TP + 4 * NB], fp32, A2 + 19 * K + 512)
        conv_th = at("conv_th", [P, 2, TP + 4 * NB], fp32, A2 + 22 * K)
        ktok = at("ktok", [P, 2, AW], fp32, A0 + 12 * T * 4)
        stok = at("stok", [NB, 3 * AW], fp32, A0 + 12 * T * 4 + 8 * K)
        assert 12 * T * 4 + 20 * K <= 2 * TILE16
        dt_w = at("dt_w", [SH, 6, T], fp32, A1)
        S0 = A1 - K
        bcrow = at("bcrow", [NB, 2 * NG * P], fp32, S0 + 40 * K)
        xdt = at("xdt", [P, 2, D], fp32, S0 + 8 * K)
        btok = at("btok", [P, 2, NG * P], fp32, S0 + 24 * K)
        xw = at("xw", [P, 256], fp32, S0 + 32 * K)
        xw1 = at("xw1", [P, 2, 256], fp32, S0 + 33 * K)
        hT0 = at("hT0", [P, 256], fp32, S0 + 35 * K)
        seg = at("seg", [P, 2, 4 * P], fp32, S0 + 36 * K)
        dec = at("dec", [P, 2, 4 * P], fp32, S0 + 40 * K)
        cexp = at("cexp", [P, 4 * P], fp32, S0 + 44 * K)
        cbm = at("cbm", [P, 2, P], fp32, S0 + 46 * K)
        dtok = at("dtok", [P, 2, 2, SH], fp32, S0 + 47 * K)
        acum = at("acum", [P, 2, SH], fp32, S0 + 47 * K + 512)
        dend = at("dend", [P, 2, SH], fp32, S0 + 47 * K + 768)
        cdec = at("cdec", [P, SH], fp32, S0 + 48 * K)
        hfin = at("hfin", [P, 2, P], fp32, S0 + 48 * K + 128)
        expand = at("expand", [SH, D], fp32, A1 + 7 * K)
        crow = at("crow", [3 + NB, CONVC], fp32, A1)
        scal = at("scal", [P, XT, 2 * NB], fp32, M0 + 14 * K)
        xdts = at("xdts", [P, XT, NB], fp32, M0 + 15 * K)
        ysam = at("ysam", [P, XT, NB], fp32, M0 + 15 * K + 512)
        zs = at("zs", [P, XT, NB], fp32, M0 + AT * T * 4)
        gate_s = at("gate_s", [P, KT, T], fp32, A0 + TILE16)
        gate_a = at("gate_a", [P, KT, T], fp32, A1)
        F0 = A1 + TILE16
        kv = at("kv", [P, 4, AW], fp32, F0)
        vm = at("vm", [P, AW], fp32, F0)
        qb = at("qb", [P, 2, AW], fp32, F0 + 16 * K)
        pz = at("pz", [P, NPG, P], fp32, F0 + 16 * K)
        bc = at("bc", [P, 2, 2, 256], fp32, F0 + 20 * K)
        sc = at("sc", [P, NPG + 1, NB, HEADS], fp32, F0 + 24 * K)
        un = at("un", [P, 2, T], fp32, F0 + 24 * K)
        W0 = F0 + 24 * K + (NPG + 1) * P * 4
        m_w = at("m_w", [P, 10, P], fp32, W0)
        st = at("st", [P, 2, 4, P], fp32, W0)
        stx = at("stx", [P, 4, P], fp32, W0 + 4 * K)
        assert W0 + 6 * K <= M0
        own_v = at("own_v", [NB, AW], fp32, M0 + 10 * K)
        own_qk = at("own_qk", [NB, 2, AW], fp32, F0 + 8 * K)
        a_hi = at("a_hi", [P, AT, T], f32r, F0)
        a_lo = at("a_lo", [P, AT, T], f32r, F0 + AT * T * 4)
        m_hi = at("m_hi", [P, KT, T], f32r, A0)
        m_lo = at("m_lo", [P, KT, T], f32r, F0)
        mo = at("mo", [P, KT, T], fp32, A1)
        x1 = at("x1", [P, KT, T], fp32, A0 + TILE16)
        xtok2 = at("xtok2", [P, 3, D], fp32, F0 + TILE16)
        g_hi = at("g_hi", [P, FT, T], f32r, A0)
        g_lo = at("g_lo", [P, FT, T], f32r, A0 + FT * T * 4)
        glu = at("glu", [P, 3, 2, T], fp32, A0 + 2 * FT * T * 4)
        fo = at("fo", [P, KT, T], fp32, 0)
        x2 = at("x2", [P, KT, T], fp32, TILE16)
        ytok = at("ytok", [P, 3, D], fp32, A0)

        gemm_ps = [ctx.enter_context(nc.psum_tensor(f"gemm{n}", [P, 512], fp32)) for n in range(4)]
        side = [ctx.enter_context(nc.psum_tensor(f"side{n}", [P, 512], fp32)) for n in range(4)]

        q_row = nc.dram_tensor("q_row", [NB, AW], fp32, kind="Internal").ap()
        bc_row = nc.dram_tensor("bc_row", [NB, 2, NG * P], fp32, kind="Internal").ap()
        x1_spill = nc.dram_tensor("x1_spill", [P, KT * T], fp32, kind="Internal").ap()

        w_in, w_ao, w_so, w_o = a["w_in"][0], a["w_attn_out"][0], a["w_ssm_out"][0], a["w_out"][0]
        w_g, w_u, w_d = a["w_gate"][0], a["w_up"][0], a["w_down"][0]

        class Phase:
            made = []

            def __init__(self, ws, col, kt, pairs, hi, lo, per=2):
                self.ws, self.col, self.kt, self.pairs, self.per = ws, col, kt, pairs, per
                self.hi, self.lo = hi, lo
                self.loads = -(-kt // KG)
                self.lag = min(LAG, 2 * self.loads - 1)
                before = Phase.made[-1] if Phase.made else None
                self.load0 = before.load0 + before.pairs * before.loads if before else 0
                self.pair0 = before.pair0 + before.pairs if before else 0
                self.iters = pairs // per
                assert pairs % per == 0 and (self.load0 % 2 == 0) and self.pair0 % 2 in (0, 1)
                assert self.iters == 1 or (per * self.loads % RING == 0 and per % 2 == 0)
                Phase.made.append(self)

        ph_qkv = Phase([w_in], COL_Q, KT, 12, x_hi, x_lo)
        ph_dt = Phase([w_in], COL_DT, KT, 1, x_hi, x_lo, per=1)
        ph_xbc = Phase([w_in], COL_X, KT, 16, x_hi, x_lo)
        ph_gs = Phase([w_in], COL_GS, KT, 8, x_hi, x_lo)
        ph_ga = Phase([w_in], COL_GA, KT, 8, x_hi, x_lo)
        ph_z = Phase([w_in], COL_Z, KT, 8, x_hi, x_lo)
        ph_ao = Phase([w_ao], 0, AT, 8, a_hi, a_lo, per=4)
        ph_so = Phase([w_so], 0, KT, 8, x_hi, x_lo)
        ph_o = Phase([w_o], 0, KT, 8, m_hi, m_lo)
        ph_ff = Phase([w_g, w_u], 0, KT, 44, x_hi, x_lo)
        ph_dn = Phase([w_d], 0, FT, 8, g_hi, g_lo)

        loaded = [sem(f"loaded{s}") for s in range(RING)]
        free_out = [sem("free_out0"), sem("free_out1")]
        (hi_done, lo_done, mm_done, consts_in, pages_in, state_in, consts_made, x_in, x_tr, x_cp, nrm_sq, nrm_mm,
         nrm_sd, nrm_rs, h_mul, h_hi, h_lo, tok_tr, tok_out, cst_tr, cst_cp, qk_staged, v_staged, s_mm, s_masked,
         s_max, s_nmax, s_exp, s_rcp, s_norm, pt_mm, pt_cp, pv_mm, attn_cp, conv_st, conv_step, conv_tanh,
         xbc_done, tail_cp, dt_act, dt_dve, dt_tr, dt_tok, dt_sum, dt_ac, dt_de, xb_tr, r_mm, cb_mm, seg_done,
         cbm_done, dec_done, m_done, cx_exp, cx_done, xw_done, xwf_done, ht_mm, ht_cp, y_mm, y_done, fin_mm,
         fin_cp, fin_out, ct_tr, ct_cp, ct_out, bc_tr, bc_cp, bc_out, ex_made, ex_mm, ex_cp, sx_mul, stx_done,
         st_new, st_prod, st_sum, ysam_done, z_tanh, u_done, un_sq, un_mm, un_sd, un_rs, un_mul, own_in, own_mul,
         own_sum, own_put, k_mul, k_red, sel_mm, sel_dve, max_tr, max_dve, max_mm, p_sub, p_exp, p_sum, p_mm,
         p_rcp, p_done, v_mm, v_cp, u_hi, u_lo, a_hi_done, a_lo_done, ao_sum, ao_hi, ao_lo, x1_done, x1_out,
         x1_in, ff_tanh, ff_hi, ff_lo, y2_done, y_tr, y_cp, y_out, cs_out, y_cp2, o_scaled, f_scaled, qb_in, pz_done, vm_done) = [sem(n) for n in (
            "hi_done lo_done mm_done consts_in pages_in state_in consts_made x_in x_tr x_cp nrm_sq nrm_mm "
            "nrm_sd nrm_rs h_mul h_hi h_lo tok_tr tok_out cst_tr cst_cp qk_staged v_staged s_mm s_masked "
            "s_max s_nmax s_exp s_rcp s_norm pt_mm pt_cp pv_mm attn_cp conv_st conv_step conv_tanh xbc_done "
            "tail_cp dt_act dt_dve dt_tr dt_tok dt_sum dt_ac dt_de xb_tr r_mm cb_mm seg_done cbm_done "
            "dec_done m_done cx_exp cx_done xw_done xwf_done ht_mm ht_cp y_mm y_done fin_mm fin_cp fin_out "
            "ct_tr ct_cp ct_out bc_tr bc_cp bc_out ex_made ex_mm ex_cp sx_mul stx_done st_new st_prod st_sum "
            "ysam_done z_tanh u_done un_sq un_mm un_sd un_rs un_mul own_in own_mul own_sum own_put k_mul "
            "k_red sel_mm sel_dve max_tr max_dve max_mm p_sub p_exp p_sum p_mm p_rcp p_done v_mm v_cp u_hi "
            "u_lo a_hi_done a_lo_done ao_sum ao_hi ao_lo x1_done x1_out x1_in ff_tanh ff_hi ff_lo y2_done "
            "y_tr y_cp y_out cs_out y_cp2 o_scaled f_scaled qb_in pz_done vm_done").split()]
        tok_cp = [sem("tok_cp0"), sem("tok_cp1")]
        xb_cp = [sem("xb_cp0"), sem("xb_cp1")]
        kv_in = [sem(f"kv_in{s}") for s in range(4)]
        st_in = [sem(f"st_in{s}") for s in range(2)]
        st_out = [sem(f"st_out{s}") for s in range(2)]
        CONSTS = 13 + 5 + NB

        def wait(eng, s, v):
            if not isinstance(v, int) or v > 0:
                eng.wait_ge(s, v)

        def then(eng, ins, s, v):
            ins.then_inc(s, 1)
            eng.wait_ge(s, v)

        def block_no(ph, i, qq):
            return 2 * (ph.load0 + ph.per * ph.loads * i) + qq

        def k_tiles(ph, q):
            return min(KG, ph.kt - KG * (q // 2))

        def last_block(ph, pr, n):
            return 2 * (ph.load0 + ph.loads * pr) + 2 * ph.loads - 1 + n

        def blocks(eng, ph, step, evac=None, before=None, side_work=None):
            n = 2 * ph.loads

            def previous(i, j):
                par = (ph.pair0 + j - 1) % 2
                evac(ph.per * i + j - 1, par, (ph.pair0 + j - 1 - par) // 2 + ph.per // 2 * i)

            def body(i, first):
                for j in range(ph.per):
                    for q in range(n):
                        step(i, j, q, j * n + q)
                        if q == ph.lag - 1 and j == 0:
                            first()
                        elif q == ph.lag - 1 and evac:
                            previous(i, j)
                        if side_work:
                            side_work(i, j * n + q)

            body(0, before or (lambda: None))
            if ph.iters > 1:
                with eng.Fori(1, ph.iters) as i:
                    body(i, (lambda: previous(i, 0)) if evac else (lambda: None))
            end = ph.pairs - 1
            par = (ph.pair0 + end) % 2
            return (lambda: evac(end, par, (ph.pair0 + end - par) // 2)) if evac else None

        def none_free(ph):
            total = ph.pair0 + ph.pairs
            return [2 * ((total + 1) // 2), 2 * (total // 2)]

        CW = TP + 4 * NB

        def news(t, n):
            return t[:, n, TP + 3:TP + 3 + 4 * NB].rearrange("p (b w) -> p b w", w=4)

        def one(t, k):
            return t[:, bass.ds(k, 1)].rearrange("p o t -> p (o t)")

        def tok_dst(n):
            if n < 8:
                dst = (ktok, vtok)[n // 4][:, (n // 2) % 2, (n % 2) * 512:(n % 2) * 512 + 512]
                return dst, side[n % 4][:, :]
            return stok[:, (n - 8) * 512:(n - 7) * 512], side[n % 4][0:NB, :]

        def earlier(i, m, lag, per):
            i, m = (i - 1, m - lag + per) if m < lag else (i, m - lag)
            return None if isinstance(i, int) and i < 0 else (i, m)

        SP_LAG = 4

        def kpage(ph, i, m):
            return (0 if ph is ph_gs else NB // 2) + i, m

        def y_dst(n):
            m, c = n // 3, n % 3
            rows = P if c < 2 else NB
            return ytok[0:rows, c, m * 512:(m + 1) * 512], side[n % 4][0:rows, :]

        block = ctx.enter_context(nc.Block())

        @block.sync
        def _(sp):
            def vec(ap):
                return ap.rearrange("(k p) -> p k", p=P)

            for c in range(2):
                sp.dma_start(xtok[:, c, :], a["x_prompt"][0, c * P:(c + 1) * P, :]).then_inc(x_in, 16)
            sp.dma_start(xtok[0:NB, 2, :], a["x_sample"][:, 0, :]).then_inc(x_in, 16)

            def load(ph, i, l):
                j, kg = l // ph.loads, l % ph.loads
                kts = min(KG, ph.kt - KG * kg)
                s = (ph.load0 + l) % RING
                w = ph.ws[j % len(ph.ws)]
                pair = (ph.per * i + j) if len(ph.ws) == 1 else i
                src = w[kg * KG * P:(kg * KG + kts) * P, bass.ds(ph.col + 256 * pair, 256)]
                wait(sp, lo_done, 2 * (ph.load0 + ph.per * ph.loads * i + l - RING) + 2)
                sp.dma_start(raw[:, s, 0:kts, :], src.rearrange("(k p) n -> p k n", p=P)).then_inc(loaded[s], 16)

            def weights(ph, side_work=None):
                def body(i):
                    for l in range(ph.per * ph.loads):
                        load(ph, i, l)
                        if side_work:
                            side_work(i, l)

                body(0)
                if ph.iters > 1:
                    with sp.Fori(1, ph.iters) as i:
                        body(i)

            with nc.allow_non_contiguous_dma(reason="per-channel vectors"):
                for n, g in enumerate(("norm_mix_pre", "norm_mix_post", "norm_ffn_pre", "norm_ffn_post", "ssm_norm")):
                    sp.dma_start(gains[:, n, :], vec(a[g][0])).then_inc(consts_in, 16)
                for n in range(4):
                    sp.dma_start(conv_k[:, n, :], vec(a["conv_w"][0, n])).then_inc(consts_in, 16)
                sp.dma_start(conv_bias[:, :], vec(a["conv_b"][0])).then_inc(consts_in, 16)
                for n, g in enumerate(("dt_bias", "a_log")):
                    sp.dma_start(heads_c[:, n:n + 1], a[g][0].rearrange("(h o) -> h o", o=1)).then_inc(consts_in, 16)
                for h in range(2):
                    d = a["d_skip"][0].rearrange("(t h) -> h t", h=2)[h]
                    sp.dma_start(dskip[h * HD:(h + 1) * HD, :], d.partition_broadcast(HD)).then_inc(consts_in, 16)
            sp.dma_start(pages[0:1, :], a["page_table"].rearrange("b g -> (b g)").rearrange("(o n) -> o n", o=1))\
                .then_inc(pages_in, 16)
            sp.dma_start(ctok[:, :], a["state_conv"][0].rearrange("b w c -> (b w) c")).then_inc(state_in, 16)
            sp.dma_start(o["conv_sample"][0, :, 0:2, :], a["state_conv"][0, :, 1:3, :]).then_inc(cs_out, 16)
            weights(ph_qkv)
            weights(ph_dt)
            for s in tok_cp:
                sp.wait_ge(s, 7)
            for c in range(2):
                rows = slice(c * P, (c + 1) * P)
                for name, t in (("k_prompt", ktok), ("v_prompt", vtok)):
                    sp.dma_start(o[name][0, 0, rows].rearrange("s h d -> s (h d)"), t[:, c, :]).then_inc(tok_out, 16)
            sp.dma_start(q_row, stok[:, 0:AW]).then_inc(tok_out, 16)
            for n, name in enumerate(("k_sample", "v_sample")):
                sp.dma_start(o[name][0, :, 0].rearrange("b h d -> b (h d)"), stok[:, (n + 1) * AW:(n + 2) * AW])\
                    .then_inc(tok_out, 16)
            weights(ph_xbc)
            for g in range(NG):
                sp.wait_ge(fin_cp, g + 1)
                dst = o["ssm_prompt"][0, 0].rearrange("h p n -> (h p) n")[g * 256:(g + 1) * 256]
                sp.dma_start(dst.rearrange("(t p) n -> p t n", p=P), hfin[:, :, :]).then_inc(fin_out, 16)
            sp.wait_ge(bc_cp, 4)
            sp.dma_start(bc_row.rearrange("b w n -> b (w n)"), bcrow[:, :]).then_inc(bc_out, 16)
            sp.wait_ge(bc_out, 16)
            sp.wait_ge(ct_cp, 8)
            sp.dma_start(o["conv_prompt"][0, 0], crow[0:3, :]).then_inc(ct_out, 16)
            sp.dma_start(o["conv_sample"][0, :, 2, :], crow[3:3 + NB, :]).then_inc(ct_out, 16)
            sp.wait_ge(y_done, 2 * NG)
            sp.wait_ge(fin_out, 16 * NG)
            sp.wait_ge(ex_cp, 1)
            sp.wait_ge(tok_out, 16 * 7)
            sp.dma_start(own_qk[:, 0, :], q_row).then_inc(own_in, 16)
            sp.dma_start(own_qk[:, 1, :], o["k_sample"][0, :, 0].rearrange("b h d -> b (h d)")).then_inc(own_in, 16)
            sp.dma_start(own_v[:, :], o["v_sample"][0, :, 0].rearrange("b h d -> b (h d)")).then_inc(own_in, 16)
            kc = a["cache_k"][0].rearrange("g s h d -> g s (h d)")
            vc = a["cache_v"][0].rearrange("g s h d -> g s (h d)")

            def page_in(cache, b, g, freed, v):
                pg = sp.value_load(pages[0:1, bass.ds(NPG * b + g, 1)], min_val=0, max_val=a["cache_k"].shape[1] - 1)
                src = cache[bass.ds(pg, 1)].rearrange("g p n -> p g n")
                wait(sp, freed, v)
                sp.dma_start(kv[:, g % 4:g % 4 + 1, :], src).then_inc(kv_in[g % 4], 16)

            def k_in(b, g):
                if g == 0:
                    src = q_row[bass.ds(b, 1), :].rearrange("o n -> (o n)").partition_broadcast(P)
                    dst = qb[:, bass.ds(b % 2, 1), :].rearrange("p o n -> p (o n)")
                    if not (isinstance(b, int) and b == 0):
                        wait(sp, k_mul, NPG * b - NPG + 1)
                    sp.dma_start(dst, src).then_inc(qb_in, 16)
                page_in(kc, b, g, k_red, NPG * b + g - 3)

            def k_side(ph):
                def side_work(i, l):
                    for m in (2 * l, 2 * l + 1):
                        at_ = earlier(i, m, SP_LAG, 8)
                        if at_:
                            k_in(*kpage(ph, *at_))
                        elif ph is ph_ga:
                            k_in(NB // 2 - 1, m + 8 - SP_LAG)
                return side_work

            sp.wait_ge(pages_in, 16)
            sp.wait_ge(own_put, 1)
            weights(ph_gs, k_side(ph_gs))
            weights(ph_ga, k_side(ph_ga))
            for m in range(8 - SP_LAG, 8):
                k_in(NB - 1, m)

            hs = a["state_ssm"][0].rearrange("b h p n -> b (h p) n")
            ho = o["ssm_sample"][0].rearrange("b h p n -> b (h p) n")

            def state_rows(x, b, r):
                return x[bass.ds(b, 1), r * 512:(r + 1) * 512, :].rearrange("o (t p) n -> p (o t) n", p=P)

            def state_store(i, m):
                dst = state_rows(ho, 2 * i + m // 4, m % 4)
                sp.wait_ge(st_sum, 8 * i + m + 1)
                sp.dma_start(dst, st[:, m % 2]).then_inc(st_out[m % 2], 16)

            def state_load(i, m):
                b, r = 2 * i + m // 4, m % 4
                src = state_rows(hs, b, r)
                rows = bc_row[bass.ds(b, 1), :, r * 256:(r + 1) * 256].rearrange("o w n -> (o w) n")
                wait(sp, st_out[m % 2], 16 * (4 * i + m // 2))
                sp.dma_start(st[:, m % 2], src).then_inc(st_in[m % 2], 16)
                sp.dma_start(bc[:, m % 2], rows.partition_broadcast(P)).then_inc(st_in[m % 2], 16)

            def v_in(i, m):
                page_in(vc, 2 * i + m // NPG, m % NPG, v_mm, 16 * i + m - 3)

            def z_items(i, l, lag):
                for m in (2 * l, 2 * l + 1):
                    before = earlier(i, m, lag + 2, 8)
                    if before:
                        state_store(*before)
                    at_ = earlier(i, m, lag, 8)
                    if at_:
                        for u in range(2):
                            v_in(at_[0], 2 * at_[1] + u)
                        state_load(*at_)

            sp.wait_ge(k_red, NB * NPG)
            sp.wait_ge(k_mul, NB * NPG)
            sp.wait_ge(p_done, 1)
            weights(ph_z, lambda i, l: z_items(i, l, SP_LAG))
            for l in range(2):
                z_items(ph_z.iters, l, SP_LAG)
            for m in (6, 7):
                state_store(ph_z.iters - 1, m)
            weights(ph_ao)
            weights(ph_so)
            weights(ph_o)
            for s in range(2):
                sp.wait_ge(st_out[s], 16 * 2 * NB)
            sp.wait_ge(ct_out, 32)
            sp.wait_ge(ao_lo, KT)
            for c in range(2):
                sp.dma_start(xtok2[:, c, :], a["x_prompt"][0, c * P:(c + 1) * P, :]).then_inc(x_in, 16)
            sp.dma_start(xtok2[0:NB, 2, :], a["x_sample"][:, 0, :]).then_inc(x_in, 16)
            sp.wait_ge(x1_done, KT)
            sp.dma_start(x1_spill, x1[:, :, :].rearrange("p k t -> p (k t)")).then_inc(x1_out, 16)
            weights(ph_ff)
            weights(ph_dn)
            sp.wait_ge(x1_out, 16)
            sp.wait_ge(mm_done, block_no(ph_dn, 0, 0))
            sp.dma_start(x2[:, :, :].rearrange("p k t -> p (k t)"), x1_spill).then_inc(x1_in, 16)
            sp.wait_ge(y_cp, 6)
            sp.wait_ge(y_cp2, 6)
            for c in range(2):
                sp.dma_start(o["y_prompt"][0, c * P:(c + 1) * P, :], ytok[:, c, :]).then_inc(y_out, 16)
            sp.dma_start(o["y_sample"][:, 0, :], ytok[0:NB, 2, :]).then_inc(y_out, 16)
            sp.wait_ge(y_out, 16 * 3)
            sp.wait_ge(cs_out, 16)

        @block.gpsimd
        def _(gp):
            made = [0]

            def made_one(ins):
                made[0] += 1
                then(gp, ins, consts_made, made[0])

            made_one(gp.memset(ident[:, :], 0.0))
            made_one(gp.affine_select(out=ident[:, :], in_=ident[:, :], compare_op=ALU.not_equal, fill=1.0, base=0,
                                      pattern=[[-1, P]], channel_multiplier=1))
            made_one(gp.memset(ones[:, :], 1.0))
            made_one(gp.memset(eps[:, :], EPS))
            made_one(gp.affine_select(out=upper[:, :], in_=ones[:, :], compare_op=ALU.is_ge, fill=0.0, base=0,
                                      pattern=[[1, P]], channel_multiplier=-1))
            made_one(gp.memset(cmask[:, :], 0.0))
            for c in (0, 2):
                made_one(gp.affine_select(out=cmask[:, c * P:(c + 1) * P], in_=cmask[:, c * P:(c + 1) * P],
                                          compare_op=ALU.is_ge, fill=NEG, base=0, pattern=[[-1, P]],
                                          channel_multiplier=1))
            made_one(gp.memset(dmask[:, :], 0.0))
            made_one(gp.affine_select(out=dmask[:, :], in_=dmask[:, :], compare_op=ALU.is_equal, fill=NEG, base=0,
                                      pattern=[[-1, NB]], channel_multiplier=1))
            made_one(gp.memset(conv_in[:, :, 0:3], 0.0))
            gp.wait_ge(consts_in, 16 * 14)
            made_one(gp.tensor_scalar(out=conv_k[:, :, :], in0=conv_k[:, :, :], scalar1=0.5, scalar2=None,
                                      op0=ALU.mult))
            made_one(gp.tensor_scalar(out=conv_bias[:, :], in0=conv_bias[:, :], scalar1=0.5, scalar2=None,
                                      op0=ALU.mult))
            made_one(gp.memset(bsel[:, :], 1.0))
            for sign, off in ((1, 0), (-1, HEADS - 1)):
                made_one(gp.affine_select(out=bsel[:, :], in_=bsel[:, :], compare_op=ALU.is_ge, fill=0.0, base=off,
                                          pattern=[[-sign * HEADS, NB]], channel_multiplier=sign))
            made_one(gp.memset(hmask[:, :], 0.0))
            made_one(gp.memset(zero[:, :], 0.0))
            for b in range(NB):
                ins = gp.affine_select(out=hmask[:, :], in_=hmask[:, :], compare_op=ALU.not_equal, fill=1.0,
                                       base=-HEADS * b, pattern=[[-1, HEADS]], channel_multiplier=1)
                made_one(ins)
            assert made[0] == CONSTS

            for par in range(2):
                gp.wait_ge(free_out[par], none_free(ph_qkv)[par])
            gp.wait_ge(cst_cp, 8)

            def stage_qk(i):
                for w in range(2):
                    ins = gp.tensor_copy(qk_head[:, w:w + 1, :],
                                         qkv[:, bass.ds(i + AT * w, 1), 0:TP])
                ins.then_inc(qk_staged, 1)

            def stage_v(i):
                wait(gp, pv_mm, 2 * i)
                gp.tensor_copy(v_head[:, :, :], vtok[:, :, bass.ds(P * i, P)]).then_inc(v_staged, 1)

            def conv_pair(i, j):
                base = (ph_xbc.pair0 + j) // 2 * 2 + 2 * i
                for n in range(2):
                    t = 4 * i + 2 * j + n
                    wait(gp, conv_step, 4 * t - 4)
                    gp.tensor_copy(news(conv_in, n)[:, :, 0:3],
                                   state_t[:, bass.ds(t, 1)].rearrange("p o b w -> p (o b) w")).then_inc(conv_st, 1)
                for n in range(2):
                    t = 4 * i + 2 * j + n
                    gp.wait_ge(free_out[(ph_xbc.pair0 + j) % 2], base + n + 1)
                    gp.tensor_copy(tails[:, bass.ds(t, 1), 0:3], conv_in[:, n:n + 1, TP:TP + 3])
                    gp.tensor_copy(tails[:, bass.ds(t, 1), 3:3 + NB],
                                   news(conv_in, n)[:, :, 3:4].rearrange("p b o -> p o b")).then_inc(tail_cp, 1)

            stage_qk(0)
            for s in tok_cp:
                gp.wait_ge(s, 7)

            def xbc_iter(i, more):
                stage_v(i)
                conv_pair(i, 0)
                if more:
                    gp.wait_ge(s_mm, 2 * i + 2)
                    stage_qk(i + 1)
                conv_pair(i, 1)

            xbc_iter(0, True)
            with gp.Fori(1, ph_xbc.iters - 1) as i:
                xbc_iter(i, True)
            xbc_iter(ph_xbc.iters - 1, False)
            gp.wait_ge(dt_de, 2)
            gp.wait_ge(xb_cp[0], 8)
            gp.wait_ge(xb_cp[1], 4)

            def by_head(x):
                return x.rearrange("p (h d) -> p h d", d=HD)

            for g in range(NG):
                for c in range(2):
                    wait(gp, fin_mm, g)
                    w = dend[:, c, 4 * g:4 * g + 4].unsqueeze(2).to_broadcast([P, 4, HD])
                    then(gp, gp.tensor_tensor(out=by_head(xw1[:, c]), in0=by_head(xdt[:, c, g * 256:(g + 1) * 256]),
                                              in1=w, op=ALU.mult), xw_done, 2 * g + c + 1)
                w = cdec[:, 4 * g:4 * g + 4].unsqueeze(2).to_broadcast([P, 4, HD])
                gp.tensor_tensor(out=by_head(xw[:, :]), in0=by_head(xw1[:, 0]), in1=w, op=ALU.mult).then_inc(xwf_done, 1)
            gp.wait_ge(y_done, 2 * NG)
            gp.wait_ge(fin_mm, NG)
            gp.wait_ge(fin_out, 16 * NG)
            then(gp, gp.memset(expand[:, :], 1.0), ex_made, 1)
            then(gp, gp.affine_select(out=expand[:, :], in_=expand[:, :], compare_op=ALU.is_ge, fill=0.0, base=0,
                                      pattern=[[1, D]], channel_multiplier=-HD), ex_made, 2)
            then(gp, gp.affine_select(out=expand[:, :], in_=expand[:, :], compare_op=ALU.is_ge, fill=0.0,
                                      base=HD - 1, pattern=[[-1, D]], channel_multiplier=HD), ex_made, 3)
            def k_times_q(i):
                for n in range(2):
                    b = 2 * i + n
                    gp.wait_ge(qb_in, 16 * b + 16)
                    for g in range(NPG):
                        s = g % 4
                        gp.wait_ge(kv_in[s], 16 * (2 * b + g // 4 + 1))
                        gp.tensor_tensor(out=kv[:, s], in0=kv[:, s], in1=qb[:, n], op=ALU.mult).then_inc(k_mul, 1)

            k_times_q(0)
            with gp.Fori(1, NB // 2) as i:
                k_times_q(i)
            gp.wait_ge(p_done, 1)

            def place_p(b):
                cols = sc[:, 0:NPG, bass.ds(b, 1), :].rearrange("p g b h -> p g (b h)")
                if not isinstance(b, int):
                    gp.wait_ge(v_mm, NPG * b)
                    then(gp, gp.tensor_copy(pz[:, :, bass.ds(HEADS * b - HEADS, HEADS)],
                                            zero[:, :].unsqueeze(2).to_broadcast([P, NPG, HEADS])), pz_done, 2 * b + 1)
                gp.tensor_copy(pz[:, :, bass.ds(HEADS * b, HEADS)], cols).then_inc(pz_done, 1)

            then(gp, gp.memset(pz[:, :, :], 0.0), pz_done, 1)
            place_p(0)
            with gp.Fori(1, NB) as b:
                place_p(b)

        @block.scalar
        def _(act):
            def func(out, in_, f=ACT.Copy, **kw):
                return nc.scalar.activation(out, in_, f, **kw)

            def hi_of(ph):
                def step(i, j, q, qq):
                    s, n, kts = (ph.load0 + qq // 2) % RING, qq % 2, k_tiles(ph, q)
                    if n == 0:
                        act.wait_ge(loaded[s], 16 * ((ph.load0 + qq // 2) // RING + 1 + ph.per * ph.loads // RING * i))
                    wait(act, mm_done, block_no(ph, i, qq) - RING + 1)
                    func(w_hi[:, (2 * ph.load0 + qq) % RING, 0:kts], raw[:, s, 0:kts, n * P:(n + 1) * P])\
                        .then_inc(hi_done, 1)
                return step

            def x_copies(dst, n0):
                for k in range(KT):
                    act.wait_ge(x_tr, n0 + k + 1)
                    func(dst[:, k, :], side[k % 4][:, 0:T]).then_inc(x_cp, 1)

            def root(n):
                act.wait_ge(nrm_mm, KT * (n + 1))
                wait(act, nrm_rs, n)
                func(stat[:, :], side[3][:, 0:T], ACT.Sqrt, bias=eps[:, 0:1], scale=1.0 / D).then_inc(nrm_sd, 1)

            def x_hi_from(src, n):
                for k in range(KT):
                    act.wait_ge(h_mul, KT * n + k + 1)
                    func(x_hi[:, k, :], src[:, k, :]).then_inc(h_hi, 1)

            act.wait_ge(consts_made, CONSTS)
            x_copies(xT, 0)
            root(0)
            x_hi_from(xT, 0)
            for n in range(8):
                act.wait_ge(cst_tr, n + 1)
                src = side[n % 4][:, 0:4 * 3 * NB].rearrange("p (t b w) -> p t b w", t=4, w=3)
                func(state_t[:, 4 * n:4 * n + 4], src).then_inc(cst_cp, 1)

            def qkv_evac(pr, par, gen):
                for n in range(2):
                    act.wait_ge(mm_done, last_block(ph_qkv, pr, n))
                    func(one(qkv, 2 * pr + n), gemm_ps[2 * par + n][:, 0:T]).then_inc(free_out[par], 1)

            def dt_evac(pr, par, gen):
                act.wait_ge(mm_done, last_block(ph_dt, pr, 1))
                func(dt_raw[:, :], gemm_ps[2 * par][0:SH, 0:T]).then_inc(free_out[par], 2)

            last = blocks(act, ph_qkv, hi_of(ph_qkv), qkv_evac)
            last = blocks(act, ph_dt, hi_of(ph_dt), dt_evac, last)
            last()
            for n in range(0, 14, 2):
                act.wait_ge(tok_tr, n + 1)
                func(*tok_dst(n)).then_inc(tok_cp[0], 1)

            def conv_evac(pr, par, gen):
                for n in range(2):
                    t = 2 * pr + n
                    act.wait_ge(mm_done, last_block(ph_xbc, pr, n))
                    act.wait_ge(conv_st, t + 1)
                    wait(act, tail_cp, t - 1)
                    ps = gemm_ps[2 * par + n]
                    func(conv_in[:, n, 3:3 + TP], ps[:, 0:TP])
                    func(news(conv_in, n)[:, :, 3], ps[:, TP:T]).then_inc(free_out[par], 1)
                for n in range(2):
                    t = 2 * pr + n
                    act.wait_ge(conv_step, 4 * t + 4)
                    wait(act, xbc_done, t - 1)
                    func(conv_th[:, n, :], conv_out[:, n, :], ACT.Tanh).then_inc(conv_tanh, 1)

            def attn_out(i):
                act.wait_ge(pv_mm, 2 * i + 2)
                func(attn[:, bass.ds(i, 1), 0:TP].rearrange("p o t -> p (o t)"), side[3][:, 0:TP]).then_inc(attn_cp, 1)

            def attn_act(i, qq):
                if qq == 1 and not (isinstance(i, int) and i == 0):
                    attn_out(i - 1)
                if qq in (4, 5):
                    x = qq - 4
                    act.wait_ge(s_nmax, 2 * i + x + 1)
                    wait(act, s_norm, 2 * i - 1 + x)
                    for m, cols in enumerate((slice(0, P), slice(P, 3 * P))):
                        ins = func(att_s[:, x, cols], att_s[:, x, cols], ACT.Exp, scale=SCALE,
                                   bias=att_st[:, x, 2 + m:3 + m], accum_out=att_st[:, x, 4 + m:5 + m])
                    ins.then_inc(s_exp, 1)
                if qq == 7:
                    for x in range(2):
                        act.wait_ge(pt_mm, 2 * i + x + 1)
                        wait(act, pv_mm, 2 * i - 1 + x)
                        func(att_pt[:, x, :], side[2][:, 0:3 * P]).then_inc(pt_cp, 1)

            last = blocks(act, ph_xbc, hi_of(ph_xbc), conv_evac, None, attn_act)
            last()
            attn_out(AT - 1)

            act.wait_ge(free_out[ph_dt.pair0 % 2], none_free(ph_dt)[ph_dt.pair0 % 2])
            then(act, func(dt_w[:, 0, :], dt_raw[:, :], ACT.Abs, bias=heads_c[:, 0:1]), dt_act, 1)
            then(act, func(dt_w[:, 1, :], dt_w[:, 0, :], ACT.Exp, scale=-1.0), dt_act, 2)
            then(act, func(dt_w[:, 2, :], dt_w[:, 1, :], ACT.Ln, bias=1.0), dt_act, 3)
            then(act, func(heads_c[:, 2:3], heads_c[:, 1:2], ACT.Exp), dt_act, 4)
            act.wait_ge(dt_dve, 3)
            func(dt_w[:, 3, 0:NB], dt_w[:, 4, TP:T]).then_inc(dt_act, 1)
            func(dt_w[:, 3, NB:2 * NB], dt_w[:, 5, TP:T], ACT.Exp).then_inc(dt_act, 1)
            act.wait_ge(dt_ac, 2)
            func(dend[:, :, :], dend[:, :, :], ACT.Exp).then_inc(dt_de, 1)
            func(cdec[:, :], side[1][:, 3 * SH:4 * SH], ACT.Exp).then_inc(dt_de, 1)
            for n in range(12):
                c, m = n // 6, n % 6
                if m >= 4:
                    act.wait_ge(xb_tr, n + 1)
                    func(btok[:, c, (m - 4) * 512:(m - 3) * 512], side[n % 4][:, :]).then_inc(xb_cp[1], 1)

            def fin_copy(g):
                act.wait_ge(fin_mm, g + 1)
                wait(act, fin_out, 16 * g)
                func(hfin[:, :, :], gemm_ps[3][:, 0:256].rearrange("p (t n) -> p t n", t=2)).then_inc(fin_cp, 1)

            for s in range(2 * NG):
                g, c = s // 2, s % 2
                act.wait_ge(seg_done, s + 1)
                wait(act, m_done, s - 1)
                func(dec[:, c, :], seg[:, c, :], ACT.Exp).then_inc(dec_done, 1)
                if c == 1:
                    wait(act, y_mm, s - 1)
                    func(cexp[:, :], side[1][:, :], ACT.Exp).then_inc(cx_exp, 1)
                else:
                    if g:
                        fin_copy(g - 1)
                    act.wait_ge(ht_mm, g + 1)
                    wait(act, y_mm, 2 * g)
                    func(hT0[:, :], gemm_ps[2][:, 0:256]).then_inc(ht_cp, 1)
            fin_copy(NG - 1)
            act.wait_ge(y_mm, 2 * NG)
            act.wait_ge(m_done, 2 * NG)
            act.wait_ge(xw_done, 2 * NG)
            for n in range(4):
                act.wait_ge(bc_tr, n + 1)
                func(bcrow[:, n * 512:(n + 1) * 512], side[n % 4][0:NB, :]).then_inc(bc_cp, 1)
            act.wait_ge(ex_mm, 1)
            func(scal[:, :, :], side[0][:, 0:XT * 2 * NB].rearrange("p (t n) -> p t n", n=2 * NB)).then_inc(ex_cp, 1)
            act.wait_ge(ct_tr, 1)
            for n in range(8):
                act.wait_ge(ct_tr, n + 1)
                func(crow[:, n * 512:(n + 1) * 512], side[n % 4][0:3 + NB, :]).then_inc(ct_cp, 1)
            def gate_evac(ph, gate):
                def evac(pr, par, gen):
                    for n in range(2):
                        act.wait_ge(mm_done, last_block(ph, pr, n))
                        func(one(gate, 2 * pr + n), gemm_ps[2 * par + n][:, 0:T], ACT.Tanh, scale=0.5)\
                            .then_inc(free_out[par], 1)
                return evac

            act.wait_ge(ct_out, 32)
            last = blocks(act, ph_gs, hi_of(ph_gs), gate_evac(ph_gs, gate_s))
            last = blocks(act, ph_ga, hi_of(ph_ga), gate_evac(ph_ga, gate_a), last)
            last()
            act.wait_ge(p_sub, 1)
            func(sc[:, :, :, :], sc[:, :, :, :], ACT.Exp, scale=SCALE).then_inc(p_exp, 1)

            def z_evac(pr, par, gen):
                for n in range(2):
                    t = 2 * pr + n
                    act.wait_ge(mm_done, last_block(ph_z, pr, n))
                    wait(act, u_done, t - 1)
                    func(sq[:, n, :], gemm_ps[2 * par + n][:, 0:T], ACT.Tanh, scale=0.5).then_inc(z_tanh, 1)

            def state_act(i, m):
                b, r, s = 2 * i + m // 4, m % 4, m % 2
                act.wait_ge(st_in[s], 32 * (4 * i + m // 2 + 1))
                wait(act, st_sum, 8 * i + m)
                for t in range(4):
                    ins = func(stx[:, t, :], bc[:, s, 0, (t // 2) * P:(t // 2 + 1) * P],
                               scale=xdts[:, 4 * r + t, bass.ds(b, 1)])
                ins.then_inc(stx_done, 1)

            act.wait_ge(sx_mul, 1)
            blocks(act, ph_z, hi_of(ph_z), z_evac, None, state_act)()
            act.wait_ge(v_cp, 1)
            act.wait_ge(attn_cp, AT)
            for k in range(AT):
                func(a_hi[:, k, :], attn[:, k, :]).then_inc(a_hi_done, 1)

            act.wait_ge(mm_done, block_no(ph_ao, 0, 0))

            def u_hi_of(g):
                for n in range(2):
                    act.wait_ge(un_mul, 2 * g + n + 1)
                    func(one(x_hi, 2 * g + n), one(xbc, 2 * g + n)).then_inc(u_hi, 1)

            def norm_act(i, qq):
                if qq % 2:
                    g = 4 * i + qq // 2
                    if not (isinstance(i, int) and g == 0):
                        u_hi_of(g - 1)
                    act.wait_ge(un_mm, 2 * g + 2)
                    wait(act, un_rs, g)
                    func(un[:, 0, :], side[3][:, 0:T], ACT.Sqrt, bias=eps[:, 0:1], scale=1.0 / 256).then_inc(un_sd, 1)

            def so_evac(pr, par, gen):
                for n in range(2):
                    t = 2 * pr + n
                    act.wait_ge(ao_sum, t + 1)
                    func(one(m_hi, t), one(gate_s, t), scale=0.5).then_inc(ao_hi, 1)

            def copy_evac(ph, dst):
                def evac(pr, par, gen):
                    for n in range(2):
                        act.wait_ge(mm_done, last_block(ph, pr, n))
                        func(one(dst, 2 * pr + n), gemm_ps[2 * par + n][:, 0:T]).then_inc(free_out[par], 1)
                return evac

            blocks(act, ph_ao, hi_of(ph_ao), None, None, norm_act)
            u_hi_of(NG - 1)
            blocks(act, ph_so, hi_of(ph_so), so_evac)()
            blocks(act, ph_o, hi_of(ph_o), copy_evac(ph_o, mo))()
            x_copies(x1, KT)
            root(1)
            root(2)
            act.wait_ge(mm_done, block_no(ph_ff, 0, 0))
            x_hi_from(mo, 1)

            def ff_evac(pr, par, gen):
                if par == ph_ff.pair0 % 2:
                    for n in range(2):
                        act.wait_ge(mm_done, last_block(ph_ff, pr, n))
                        func(glu[:, 0, n, :], gemm_ps[2 * par + n][:, 0:T], ACT.Tanh, scale=0.5).then_inc(ff_tanh, 1)
                else:
                    for n in range(2):
                        act.wait_ge(free_out[par], 2 * gen + n + 1)
                        func(one(g_hi, pr - 1 + n), glu[:, 2, n, :]).then_inc(ff_hi, 1)

            blocks(act, ph_ff, hi_of(ph_ff), ff_evac)()
            blocks(act, ph_dn, hi_of(ph_dn), copy_evac(ph_dn, fo))()
            root(3)
            for n in range(0, 12, 2):
                act.wait_ge(y_tr, n + 1)
                func(*y_dst(n)).then_inc(y_cp, 1)

        @block.vector
        def _(dve):
            v = nc.vector

            def mul(out, x, y):
                return v.tensor_tensor(out, x, y, ALU.mult)

            def stt(out, x, scalar, y, op0, op1):
                return v.scalar_tensor_tensor(out=out, in0=x, scalar=scalar, in1=y, op0=op0, op1=op1)

            def lo_of(ph):
                def step(i, j, q, qq):
                    s, n, kts = (ph.load0 + qq // 2) % RING, qq % 2, k_tiles(ph, q)
                    w = (2 * ph.load0 + qq) % RING
                    dve.wait_ge(hi_done, block_no(ph, i, qq) + 1)
                    v.tensor_tensor(w_lo[:, w, 0:kts], raw[:, s, 0:kts, n * P:(n + 1) * P],
                                    w_hi[:, w, 0:kts].bitcast(fp32), ALU.subtract).then_inc(lo_done, 1)
                return step

            def squares(src, n, ready=None):
                for k in range(KT):
                    if ready:
                        dve.wait_ge(ready[0], ready[1] + k + 1)
                    wait(dve, nrm_mm, KT * n + k - 1)
                    mul(sq[:, k % 2, :], src[:, k, :], src[:, k, :]).then_inc(nrm_sq, 1)

            def scale_by_norm(dst, src, n, gain, done):
                dve.wait_ge(nrm_sd, n + 1)
                then(dve, v.reciprocal(stat_r[:, :], stat[:, :]), nrm_rs, n + 1)
                for k in range(KT):
                    ins = stt(dst[:, k, :], src[:, k, :], gains[:, gain, k:k + 1], stat_r[:, :], ALU.mult, ALU.mult)
                    ins.then_inc(*done)

            def x_lo_from(src, hi, lo, done, n, count):
                for k in range(count):
                    dve.wait_ge(done[0], n + k + 1)
                    v.tensor_tensor(lo[:, k, :], src[:, k, :], hi[:, k, :].bitcast(fp32), ALU.subtract)\
                        .then_inc(done[1], 1)

            dve.wait_ge(consts_made, CONSTS)
            squares(xT, 0, (x_cp, 0))
            scale_by_norm(xT, xT, 0, 0, (h_mul, 1))
            x_lo_from(xT, x_hi, x_lo, (h_hi, h_lo), 0, KT)
            blocks(dve, ph_qkv, lo_of(ph_qkv))
            blocks(dve, ph_dt, lo_of(ph_dt))
            for n in range(1, 14, 2):
                dve.wait_ge(tok_tr, n + 1)
                v.tensor_copy(*tok_dst(n)).then_inc(tok_cp[1], 1)

            def conv_evac(pr, par, gen):
                for n in range(2):
                    t = 2 * pr + n
                    k = [conv_k[:, w, bass.ds(t, 1)] for w in range(4)]
                    dve.wait_ge(free_out[par], 2 * gen + n + 1)
                    then(dve, v.tensor_scalar(conv_out[:, n, :], conv_in[:, n, 0:CW], k[0], conv_bias[:, bass.ds(t, 1)],
                                              ALU.mult, ALU.add), conv_step, 4 * t + 1)
                    for w in range(1, 4):
                        then(dve, stt(conv_out[:, n, 0:CW], conv_in[:, n, w:w + CW], k[w],
                                      conv_out[:, n, 0:CW], ALU.mult, ALU.add), conv_step, 4 * t + 1 + w)
                for n in range(2):
                    t = 2 * pr + n
                    dve.wait_ge(conv_tanh, t + 1)
                    x = one(xbc, t)
                    stt(x[:, 0:TP], conv_th[:, n, 0:TP], 1.0, conv_out[:, n, 0:TP], ALU.add, ALU.mult)
                    new = [z[:, n, TP + 3:TP + 3 + 4 * NB - 3:4] for z in (conv_th, conv_out)]
                    stt(x[:, TP:T], new[0], 1.0, new[1], ALU.add, ALU.mult).then_inc(xbc_done, 1)

            def attn_dve(i, qq):
                if qq in (3, 4):
                    x = qq - 3
                    dve.wait_ge(s_mm, 2 * i + x + 1)
                    wait(dve, pt_mm, 2 * i - 1 + x)
                    then(dve, v.tensor_tensor(att_s[:, x, :], side[x][:, 0:3 * P], cmask[:, :], ALU.add),
                         s_masked, 2 * i + x + 1)
                    for m, cols in enumerate((slice(0, P), slice(P, 3 * P))):
                        ins = v.tensor_reduce(out=att_st[:, x, m:m + 1], in_=att_s[:, x, cols], axis=AX.X, op=ALU.max)
                    then(dve, ins, s_max, 2 * i + x + 1)
                    v.tensor_scalar(att_st[:, x, 2:4], att_st[:, x, 0:2], -SCALE, None, ALU.mult).then_inc(s_nmax, 1)
                if qq in (5, 6):
                    x = qq - 5
                    dve.wait_ge(s_exp, 2 * i + x + 1)
                    then(dve, v.reciprocal(att_st[:, x, 6:8], att_st[:, x, 4:6]), s_rcp, 2 * i + x + 1)
                    for m, cols in enumerate((slice(0, P), slice(P, 3 * P))):
                        ins = v.tensor_scalar(att_s[:, x, cols], att_s[:, x, cols], att_st[:, x, 6 + m:7 + m], None,
                                              ALU.mult)
                    ins.then_inc(s_norm, 1)

            blocks(dve, ph_xbc, lo_of(ph_xbc), conv_evac, None, attn_dve)()

            dve.wait_ge(tail_cp, CT)
            dve.wait_ge(dt_act, 4)
            then(dve, v.tensor_scalar(dt_w[:, 3, :], dt_raw[:, :], heads_c[:, 0:1], 0.0, ALU.add, ALU.max), dt_dve, 1)
            then(dve, v.tensor_tensor(dt_w[:, 4, :], dt_w[:, 3, :], dt_w[:, 2, :], ALU.add), dt_dve, 2)
            then(dve, v.tensor_scalar(dt_w[:, 5, :], dt_w[:, 4, :], heads_c[:, 2:3], -1.0, ALU.mult, ALU.mult),
                 dt_dve, 3)
            dve.wait_ge(dt_tr, 1)
            then(dve, v.tensor_copy(dtok[:, :, :, :].rearrange("p k c h -> p (k c h)"), side[0][:, 0:P]), dt_tok, 1)
            dve.wait_ge(dt_sum, 1)
            then(dve, v.tensor_copy(acum[:, :, :].rearrange("p c h -> p (c h)"), side[1][:, 0:2 * SH]), dt_ac, 1)
            v.tensor_tensor(dend[:, :, :].rearrange("p c h -> p (c h)"), side[1][:, 2 * SH:4 * SH],
                            acum[:, :, :].rearrange("p c h -> p (c h)"), ALU.subtract).then_inc(dt_ac, 1)
            for n in range(12):
                c, m = n // 6, n % 6
                if m < 4:
                    dve.wait_ge(xb_tr, n + 1)
                    w = dtok[:, 0, c, 8 * m:8 * m + 8].unsqueeze(2).to_broadcast([P, 8, HD])
                    v.tensor_tensor(xdt[:, c, m * 512:(m + 1) * 512].rearrange("p (h d) -> p h d", d=HD),
                                    side[n % 4][:, :].rearrange("p (h d) -> p h d", d=HD), w, ALU.mult)\
                        .then_inc(xb_cp[0], 1)

            def ssd_seg(s):
                g, c = s // 2, s % 2
                dve.wait_ge(r_mm, s + 1)
                wait(dve, y_mm, s - 1)
                for h in range(4):
                    ins = v.tensor_scalar(seg[:, c, h * P:(h + 1) * P], side[c][:, h * P:(h + 1) * P],
                                          acum[:, c, 4 * g + h:4 * g + h + 1], 0.0, ALU.subtract, ALU.min)
                ins.then_inc(seg_done, 1)
                dve.wait_ge(cb_mm, s + 1)
                mul(cbm[:, c, :], side[2 + c][:, 0:P], upper[:, :]).then_inc(cbm_done, 1)

            def ssd_y(s):
                g, c = s // 2, s % 2
                dve.wait_ge(y_mm, s + 1)
                for t in range(2):
                    x = xbc[:, 2 * g + t, c * P:(c + 1) * P]
                    ins = stt(x, x, dskip[:, 2 * g + t:2 * g + t + 1], gemm_ps[c][:, t * P:(t + 1) * P],
                              ALU.mult, ALU.add)
                ins.then_inc(y_done, 1)

            ssd_seg(0)
            for s in range(2 * NG):
                g, c = s // 2, s % 2
                if s + 1 < 2 * NG:
                    ssd_seg(s + 1)
                dve.wait_ge(dec_done, s + 1)
                dve.wait_ge(cbm_done, s + 1)
                mul(seg[:, c, :].rearrange("p (h i) -> p h i", h=4), dec[:, c, :].rearrange("p (h i) -> p h i", h=4),
                    cbm[:, c, :].unsqueeze(1).to_broadcast([P, 4, P])).then_inc(m_done, 1)
                if c == 1:
                    dve.wait_ge(cx_exp, g + 1)
                    cx = cexp[:, :].rearrange("p (h i) -> p h i", h=4)
                    mul(cx, cx, xbc[:, XT + NG + g, P:2 * P].unsqueeze(1).to_broadcast([P, 4, P])).then_inc(cx_done, 1)
                if s:
                    ssd_y(s - 1)
            ssd_y(2 * NG - 1)
            dve.wait_ge(ex_cp, 1)
            mul(xdts[:, :, :], xbc[:, 0:XT, TP:T], scal[:, :, 0:NB]).then_inc(sx_mul, 1)

            dve.wait_ge(own_in, 48)
            qk = own_qk[:, 0, :]
            then(dve, mul(qk, qk, own_qk[:, 1, :]), own_mul, 1)
            then(dve, v.tensor_reduce(out=m_w[0:NB, 0, 0:HEADS], in_=qk.rearrange("p (h d) -> p h d", d=HD), axis=AX.X,
                                      op=ALU.add), own_sum, 1)
            then(dve, v.tensor_copy(sc[:, NPG], dmask[:, :].unsqueeze(2).to_broadcast([P, NB, HEADS])), own_sum, 2)
            v.tensor_tensor(sc[0:NB, NPG], sc[0:NB, NPG],
                            m_w[0:NB, 0, 0:HEADS].unsqueeze(1).to_broadcast([NB, NB, HEADS]), ALU.add)\
                .then_inc(own_put, 1)

            def k_sum(b, g):
                dve.wait_ge(k_mul, NPG * b + g + 1)
                v.tensor_reduce(out=sc[:, g, bass.ds(b, 1), :].rearrange("p o h -> p (o h)"),
                                in_=kv[:, g % 4].rearrange("p (h d) -> p h d", d=HD), axis=AX.X, op=ALU.add)\
                    .then_inc(k_red, 1)

            def k_sums(ph):
                def side_work(i, m):
                    at_ = earlier(i, m, 2, 8)
                    if at_:
                        k_sum(*kpage(ph, *at_))
                    elif ph is ph_ga:
                        k_sum(NB // 2 - 1, m + 6)
                return side_work

            blocks(dve, ph_gs, lo_of(ph_gs), None, None, k_sums(ph_gs))
            blocks(dve, ph_ga, lo_of(ph_ga), None, None, k_sums(ph_ga))
            for m in (6, 7):
                k_sum(NB - 1, m)
            dve.wait_ge(sel_mm, 1)
            step = [0]

            def sel(ins):
                step[0] += 1
                then(dve, ins, sel_dve, step[0])

            scp = sc[:, :, :, :].rearrange("p g b h -> p g (b h)")
            for n in range(2):
                sel(v.tensor_reduce(out=m_w[:, 2 * n:2 * n + 2, :],
                                    in_=side[n][:, :].rearrange("p (k u x) -> p k x u", u=2, x=P), axis=AX.X,
                                    op=ALU.add))
            low, eq, rest = m_w[:, 4, :], m_w[:, 5, :], m_w[:, 6, :]
            sel(v.tensor_tensor(low, m_w[:, 0, :], m_w[:, 1, :], ALU.min))
            sel(v.tensor_tensor(eq, m_w[:, 2, :], m_w[:, 3, :], ALU.min))
            sel(v.tensor_tensor(low, low, eq, ALU.min))
            sel(v.tensor_tensor(m_w[:, 3, :], m_w[:, 3, :], low, ALU.is_equal))
            sel(v.tensor_scalar(rest, m_w[:, 3, :], -1.0, 1.0, ALU.mult, ALU.add))
            for n in (2, 1):
                sel(v.tensor_tensor(eq, m_w[:, n, :], low, ALU.is_equal))
                sel(mul(m_w[:, n, :], eq, rest))
                sel(v.tensor_tensor(rest, rest, m_w[:, n, :], ALU.subtract))
            for n in range(NBLK):
                drop = (rest if n == 0 else m_w[:, n, :]).unsqueeze(1).to_broadcast([P, 2, P])
                sel(stt(scp[:, 2 * n:2 * n + 2], drop, NEG, scp[:, 2 * n:2 * n + 2], ALU.mult, ALU.add))
            v.tensor_reduce(out=m_w[:, 5, :], in_=scp.rearrange("p g x -> p x g"), axis=AX.X, op=ALU.max)\
                .then_inc(max_dve, 1)
            dve.wait_ge(max_tr, 1)
            then(dve, v.tensor_reduce(out=m_w[:, 6, 0:1], in_=side[2][:, 0:P], axis=AX.X, op=ALU.max), max_dve, 2)
            v.tensor_scalar(m_w[:, 7, :], ident[:, :], m_w[:, 6, 0:1], None, ALU.mult).then_inc(max_dve, 1)
            dve.wait_ge(max_mm, 1)
            every = [P, NPG + 1, P]
            v.tensor_tensor(scp, scp, side[3][:, 0:P].unsqueeze(1).to_broadcast(every), ALU.subtract).then_inc(p_sub, 1)
            dve.wait_ge(p_exp, 1)
            v.tensor_reduce(out=m_w[:, 8, :], in_=scp.rearrange("p g x -> p x g"), axis=AX.X, op=ALU.add)\
                .then_inc(p_sum, 1)
            dve.wait_ge(p_mm, 1)
            then(dve, v.reciprocal(m_w[:, 9, :], side[0][:, 0:P]), p_rcp, 1)
            mul(scp, scp, m_w[:, 9, :].unsqueeze(1).to_broadcast(every)).then_inc(p_done, 1)

            def z_evac(pr, par, gen):
                for n in range(2):
                    t = 2 * pr + n
                    dve.wait_ge(z_tanh, t + 1)
                    then(dve, stt(tmp[:, n, :], sq[:, n, :], 1.0, gemm_ps[2 * par + n][:, 0:T], ALU.add, ALU.mult),
                         free_out[par], 2 * gen + n + 1)
                    x = one(xbc, t)
                    v.tensor_copy(one(zs, t), tmp[:, n, TP:T])
                    stt(x[:, 0:TP], tmp[:, n, 0:TP], 0.5, x[:, 0:TP], ALU.mult, ALU.mult).then_inc(u_done, 1)

            def state_step(i, m):
                b, r, s, n = 2 * i + m // 4, m % 4, m % 2, 8 * i + m
                dve.wait_ge(stx_done, n + 1)
                for t in range(4):
                    ins = stt(st[:, s, t, :], st[:, s, t, :], scal[:, 4 * r + t, bass.ds(NB + b, 1)], stx[:, t, :],
                              ALU.mult, ALU.add)
                then(dve, ins, st_new, n + 1)
                cb = bc[:, s, 1, :].rearrange("p (g n) -> p g n", g=2).unsqueeze(2).to_broadcast([P, 2, 2, P])
                then(dve, mul(stx[:, :, :].rearrange("p (g t) n -> p g t n", g=2),
                              st[:, s].rearrange("p (g t) n -> p g t n", g=2), cb), st_prod, n + 1)
                v.tensor_reduce(out=ysam[:, 4 * r:4 * r + 4, bass.ds(b, 1)].rearrange("p t o -> p (t o)"),
                                in_=stx[:, :, :], axis=AX.X, op=ALU.add).then_inc(st_sum, 1)

            blocks(dve, ph_z, lo_of(ph_z), z_evac, None, state_step)()
            dve.wait_ge(v_mm, NB * NPG + 1)
            for n in range(2):
                own = hmask[:, 8 * n:8 * n + 8].unsqueeze(2).to_broadcast([P, 8, HD])
                v.tensor_tensor(vm[:, n * 512:(n + 1) * 512].rearrange("p (h d) -> p h d", d=HD),
                                side[n][:, :].rearrange("p (h d) -> p h d", d=HD), own, ALU.mult).then_inc(vm_done, 1)
            dve.wait_ge(u_done, KT)
            dve.wait_ge(st_sum, 4 * NB)
            xn = xbc[:, 0:XT, TP:T]
            then(dve, mul(xn, xn, dskip[:, :].unsqueeze(2).to_broadcast([P, XT, NB])), ysam_done, 1)
            then(dve, v.tensor_tensor(xn, xn, ysam[:, :, :], ALU.add), ysam_done, 2)
            then(dve, mul(xn, xn, zs[:, :, :]), ysam_done, 3)
            then(dve, v.tensor_scalar(xn, xn, 0.5, None, ALU.mult), ysam_done, 4)
            dve.wait_ge(v_mm, NB * NPG + 2)
            v.tensor_copy(attn[:, :, TP:T], side[2][:, 0:AT * NB].rearrange("p (k b) -> p k b", b=NB)).then_inc(v_cp, 1)
            x_lo_from(attn, a_hi, a_lo, (a_hi_done, a_lo_done), 0, AT)

            def u_lo_of(g):
                for n in range(2):
                    t = 2 * g + n
                    dve.wait_ge(u_hi, t + 1)
                    v.tensor_tensor(one(x_lo, t), one(xbc, t), one(x_hi, t).bitcast(fp32), ALU.subtract)\
                        .then_inc(u_lo, 1)

            def norm_dve(i, qq):
                g = 4 * i + qq // 2
                if qq % 2 == 0:
                    wait(dve, un_mm, 2 * g)
                    for n in range(2):
                        x = one(xbc, 2 * g + n)
                        mul(sq[:, n, :], x, x).then_inc(un_sq, 1)
                    if not (isinstance(i, int) and g < 2):
                        u_lo_of(g - 2)
                else:
                    dve.wait_ge(un_sd, g + 1)
                    then(dve, v.reciprocal(un[:, 1, :], un[:, 0, :]), un_rs, g + 1)
                    for n in range(2):
                        t = 2 * g + n
                        stt(one(xbc, t), one(xbc, t), gains[:, 4, bass.ds(t, 1)], un[:, 1, :], ALU.mult, ALU.mult)\
                            .then_inc(un_mul, 1)

            def ao_evac(pr, par, gen):
                for n in range(2):
                    t = one(gate_a, 2 * pr + n)
                    dve.wait_ge(mm_done, last_block(ph_ao, pr, n))
                    stt(t, t, 1.0, gemm_ps[2 * par + n][:, 0:T], ALU.add, ALU.mult).then_inc(free_out[par], 1)

            def so_evac(pr, par, gen):
                for n in range(2):
                    t = 2 * pr + n
                    ga, gs = one(gate_a, t), one(gate_s, t)
                    dve.wait_ge(mm_done, last_block(ph_so, pr, n))
                    then(dve, stt(gs, gs, 1.0, gemm_ps[2 * par + n][:, 0:T], ALU.add, ALU.mult),
                         free_out[par], 2 * gen + n + 1)
                    v.tensor_tensor(gs, gs, ga, ALU.add).then_inc(ao_sum, 1)
                for n in range(2):
                    t = 2 * pr + n
                    dve.wait_ge(ao_hi, t + 1)
                    stt(one(m_lo, t), one(gate_s, t), 0.5, one(m_hi, t).bitcast(fp32), ALU.mult, ALU.subtract)\
                        .then_inc(ao_lo, 1)

            last = blocks(dve, ph_ao, lo_of(ph_ao), ao_evac, None, norm_dve)
            for g in (NG - 2, NG - 1):
                u_lo_of(g)
            blocks(dve, ph_so, lo_of(ph_so), so_evac, last)()
            blocks(dve, ph_o, lo_of(ph_o))
            for par in range(2):
                dve.wait_ge(free_out[par], none_free(ph_o)[par])
            squares(mo, 1)
            scale_by_norm(mo, mo, 1, 1, (o_scaled, 1))
            for k in range(KT):
                dve.wait_ge(x_cp, KT + k + 1)
                dve.wait_ge(o_scaled, k + 1)
                v.tensor_tensor(x1[:, k, :], x1[:, k, :], mo[:, k, :], ALU.add).then_inc(x1_done, 1)
            squares(x1, 2, (x1_done, 0))
            scale_by_norm(mo, x1, 2, 2, (h_mul, 1))
            x_lo_from(mo, x_hi, x_lo, (h_hi, h_lo), KT, KT)

            def ff_evac(pr, par, gen):
                other = 1 - par
                if par == ph_ff.pair0 % 2:
                    for n in range(2):
                        dve.wait_ge(ff_tanh, pr + n + 1)
                        stt(glu[:, 1, n, :], glu[:, 0, n, :], 1.0, gemm_ps[2 * par + n][:, 0:T], ALU.add, ALU.mult)\
                            .then_inc(free_out[par], 1)
                else:
                    for n in range(2):
                        dve.wait_ge(mm_done, last_block(ph_ff, pr, n))
                        dve.wait_ge(free_out[other], 2 * (gen - ph_ff.pair0 % 2) + n + 1)
                        stt(glu[:, 2, n, :], glu[:, 1, n, :], 0.5, gemm_ps[2 * par + n][:, 0:T], ALU.mult, ALU.mult)\
                            .then_inc(free_out[par], 1)
                    for n in range(2):
                        t = pr - 1 + n
                        dve.wait_ge(ff_hi, t + 1)
                        v.tensor_tensor(one(g_lo, t), glu[:, 2, n, :], one(g_hi, t).bitcast(fp32), ALU.subtract)\
                            .then_inc(ff_lo, 1)

            dve.wait_ge(x1_out, 16)
            blocks(dve, ph_ff, lo_of(ph_ff), ff_evac)()
            blocks(dve, ph_dn, lo_of(ph_dn))
            for par in range(2):
                dve.wait_ge(free_out[par], none_free(ph_dn)[par])
            squares(fo, 3)
            scale_by_norm(fo, fo, 3, 3, (f_scaled, 1))
            dve.wait_ge(x1_in, 16)
            for k in range(KT):
                dve.wait_ge(f_scaled, k + 1)
                v.tensor_tensor(x2[:, k, :], x2[:, k, :], fo[:, k, :], ALU.add).then_inc(y2_done, 1)
            for n in range(1, 12, 2):
                dve.wait_ge(y_tr, n + 1)
                v.tensor_copy(*y_dst(n)).then_inc(y_cp2, 1)

        @block.tensor
        def _(pe):
            mm = nc.tensor.matmul

            def turn(out, in_):
                k = in_.shape[0]
                return mm(out, in_, ident[0:k, 0:k], start=True, stop=True)

            def mm_of(ph):
                def step(i, j, q, qq):
                    n, kg, kts = q % 2, q // 2, k_tiles(ph, q)
                    par = (ph.pair0 + j) % 2
                    if q == 0:
                        wait(pe, free_out[par], 2 * ((ph.pair0 + j) // 2 + ph.per // 2 * i))
                    pe.wait_ge(lo_done, block_no(ph, i, qq) + 1)
                    w = (2 * ph.load0 + qq) % RING
                    out = gemm_ps[2 * par + n][:, 0:T]
                    for k in range(kts):
                        x = kg * KG + k
                        mm(out, w_hi[:, w, k], ph.hi[:, x], start=(x == 0), stop=False)
                        mm(out, w_hi[:, w, k], ph.lo[:, x], start=False, stop=False)
                        ins = mm(out, w_lo[:, w, k], ph.hi[:, x], start=False, stop=(x == ph.kt - 1))
                    ins.then_inc(mm_done, 1)
                return step

            def x_turns(src, n0):
                for k in range(KT):
                    if n0:
                        wait(pe, x_cp, n0 + k - 3)
                    else:
                        wait(pe, x_cp, k - 3)
                    cols = slice(k * P, (k + 1) * P)
                    for c in range(2):
                        turn(side[k % 4][:, c * P:(c + 1) * P], src[:, c, cols])
                    turn(side[k % 4][:, TP:T], src[0:NB, 2, cols]).then_inc(x_tr, 1)

            def norm_sums(n, out):
                for k in range(KT):
                    pe.wait_ge(nrm_sq, KT * n + k + 1)
                    mm(out[:, 0:T], ones[:, :], sq[:, k % 2, :], start=(k == 0), stop=(k == KT - 1)).then_inc(nrm_mm, 1)

            pe.wait_ge(consts_made, 3)
            pe.wait_ge(x_in, 48)
            x_turns(xtok, 0)
            pe.wait_ge(x_cp, KT)
            norm_sums(0, side[3])
            pe.wait_ge(state_in, 16)
            pe.wait_ge(nrm_sd, 1)
            for n in range(8):
                wait(pe, cst_cp, n - 3)
                for u in range(4):
                    t = 4 * n + u
                    ins = turn(side[n % 4][:, u * 24:(u + 1) * 24], ctok[:, t * P:(t + 1) * P])
                ins.then_inc(cst_tr, 1)
            pe.wait_ge(h_lo, KT)
            blocks(pe, ph_qkv, mm_of(ph_qkv))
            blocks(pe, ph_dt, mm_of(ph_dt))
            pe.wait_ge(cst_cp, 8)
            for par in range(2):
                pe.wait_ge(free_out[par], none_free(ph_dt)[par])
            for n in range(14):
                wait(pe, tok_cp[n % 2], (n - 4) // 2 + 1)
                if n < 8:
                    for u in range(4):
                        src = qkv[:, AT * (1 + n // 4) + 4 * (n % 2) + u, (n // 2) % 2 * P:((n // 2) % 2 + 1) * P]
                        ins = turn(side[n % 4][:, u * P:(u + 1) * P], src)
                else:
                    for u in range(4):
                        ins = turn(side[n % 4][0:NB, u * P:(u + 1) * P], qkv[:, 4 * (n - 8) + u, TP:T])
                ins.then_inc(tok_tr, 1)
            for s in tok_cp:
                pe.wait_ge(s, 7)

            def attn_pe(i, qq):
                if qq in (0, 1):
                    x = qq
                    if x == 0:
                        pe.wait_ge(qk_staged, i + 1)
                    wait(pe, s_masked, 2 * i - 1 + x)
                    q, k = (qk_head[x * HD:(x + 1) * HD, w, :] for w in range(2))
                    mm(side[x][:, 0:P], q[:, 0:P], k[:, 0:P], start=True, stop=True)
                    mm(side[x][:, P:3 * P], q[:, P:TP], k[:, 0:TP], start=True, stop=True).then_inc(s_mm, 1)
                if qq in (4, 5):
                    x = qq - 4
                    pe.wait_ge(s_norm, 2 * i + x + 1)
                    wait(pe, pt_cp, 2 * i + x)
                    for m in range(3):
                        ins = turn(side[2][:, m * P:(m + 1) * P], att_s[:, x, m * P:(m + 1) * P])
                    ins.then_inc(pt_mm, 1)
                if qq == 7:
                    pe.wait_ge(v_staged, i + 1)
                    wait(pe, attn_cp, i)
                    for x in range(2):
                        pe.wait_ge(pt_cp, 2 * i + x + 1)
                        rows = slice(x * HD, (x + 1) * HD)
                        mm(side[3][rows, 0:TP], v_head[:, 0, rows], att_pt[:, x, 0:TP], start=True, stop=False)
                        mm(side[3][rows, P:TP], v_head[:, 1, rows], att_pt[:, x, TP:3 * P], start=False, stop=True)\
                            .then_inc(pv_mm, 1)

            def xbc_step(ph):
                step = mm_of(ph)

                def both(i, j, q, qq):
                    attn_pe(i, qq) if qq < 7 else None
                    step(i, j, q, qq)
                    attn_pe(i, qq) if qq == 7 else None
                return both

            blocks(pe, ph_xbc, xbc_step(ph_xbc))

            pe.wait_ge(dt_dve, 3)
            pe.wait_ge(attn_cp, AT)
            for par in range(2):
                pe.wait_ge(free_out[par], none_free(ph_xbc)[par])
            for w in range(2):
                for c in range(2):
                    ins = turn(side[0][:, (2 * w + c) * SH:(2 * w + c + 1) * SH], dt_w[:, 4 + w, c * P:(c + 1) * P])
            ins.then_inc(dt_tr, 1)
            pe.wait_ge(dt_tok, 1)
            for w, m in enumerate((upper, ones)):
                for c in range(2):
                    ins = mm(side[1][:, (2 * w + c) * SH:(2 * w + c + 1) * SH], m[:, :], dtok[:, 1, c, :],
                             start=True, stop=True)
            ins.then_inc(dt_sum, 1)
            pe.wait_ge(dt_de, 2)
            pe.wait_ge(xbc_done, CT)

            def copied(n):
                if n >= 0:
                    c, m = n // 6, n % 6
                    pe.wait_ge(xb_cp[m // 4], 4 * c + m + 1 if m < 4 else 2 * c + m - 3)

            for n in range(12):
                c, m = n // 6, n % 6
                copied(n - 4)
                for u in range(4):
                    ins = turn(side[n % 4][:, u * P:(u + 1) * P], xbc[:, 4 * m + u, c * P:(c + 1) * P])
                ins.then_inc(xb_tr, 1)
            for n in range(8, 12):
                copied(n)

            def ssd_rc(s):
                g, c = s // 2, s % 2
                wait(pe, seg_done, s - 1)
                if c:
                    wait(pe, cx_exp, g)
                for h in range(4):
                    ins = mm(side[c][:, h * P:(h + 1) * P], dtok[:, 1, c, 4 * g + h:4 * g + h + 1].to_broadcast([P, P]),
                             upper[:, :], start=True, stop=True)
                ins.then_inc(r_mm, 1)
                wait(pe, cbm_done, s - 1)
                mm(side[2 + c][:, 0:P], xbc[:, XT + g, c * P:(c + 1) * P], xbc[:, XT + NG + g, c * P:(c + 1) * P],
                   start=True, stop=True).then_inc(cb_mm, 1)

            ssd_rc(0)
            for s in range(2 * NG):
                g, c = s // 2, s % 2
                if s + 1 < 2 * NG:
                    ssd_rc(s + 1)
                if c == 0:
                    pe.wait_ge(xw_done, 2 * g + 1)
                    wait(pe, ht_cp, g)
                    mm(gemm_ps[2][:, 0:256], btok[:, 0, g * P:(g + 1) * P], xw1[:, 0, :], start=True, stop=True)\
                        .then_inc(ht_mm, 1)
                pe.wait_ge(m_done, s + 1)
                if c:
                    pe.wait_ge(cx_done, g + 1)
                    pe.wait_ge(ht_cp, g + 1)
                wait(pe, y_done, s - 1)
                for h in range(4):
                    out = gemm_ps[c][(h % 2) * HD:(h % 2 + 1) * HD, (h // 2) * P:(h // 2 + 1) * P]
                    ins = mm(out, xdt[:, c, (4 * g + h) * HD:(4 * g + h + 1) * HD], seg[:, c, h * P:(h + 1) * P],
                             start=True, stop=(c == 0))
                    if c:
                        ins = mm(out, hT0[:, h * HD:(h + 1) * HD], cexp[:, h * P:(h + 1) * P], start=False, stop=True)
                ins.then_inc(y_mm, 1)
                if c:
                    pe.wait_ge(xwf_done, g + 1)
                    pe.wait_ge(xw_done, 2 * g + 2)
                    wait(pe, fin_cp, g)
                    for t in range(2):
                        out, cols = gemm_ps[3][:, t * P:(t + 1) * P], slice(t * P, (t + 1) * P)
                        mm(out, xw[:, cols], btok[:, 0, g * P:(g + 1) * P], start=True, stop=False)
                        ins = mm(out, xw1[:, 1, cols], btok[:, 1, g * P:(g + 1) * P], start=False, stop=True)
                    ins.then_inc(fin_mm, 1)
            pe.wait_ge(seg_done, 2 * NG)
            pe.wait_ge(cx_exp, NG)
            pe.wait_ge(cbm_done, 2 * NG)
            for n in range(4):
                for u in range(4):
                    ins = turn(side[n][0:NB, u * P:(u + 1) * P], xbc[:, XT + 4 * n + u, TP:T])
                ins.then_inc(bc_tr, 1)
            pe.wait_ge(bc_cp, 4)
            pe.wait_ge(ex_made, 3)
            pe.wait_ge(dt_act, 6)
            for t in range(XT):
                ins = mm(side[0][:, t * 2 * NB:(t + 1) * 2 * NB], expand[:, t * P:(t + 1) * P], dt_w[:, 3, 0:2 * NB],
                         start=True, stop=True)
            ins.then_inc(ex_mm, 1)
            pe.wait_ge(ex_cp, 1)
            pe.wait_ge(tail_cp, CT)
            for n in range(8):
                wait(pe, ct_cp, n - 3)
                for u in range(4):
                    ins = turn(side[n % 4][0:3 + NB, u * P:(u + 1) * P], tails[:, 4 * n + u, :])
                ins.then_inc(ct_tr, 1)
            pe.wait_ge(y_done, 2 * NG)
            pe.wait_ge(fin_cp, NG)
            blocks(pe, ph_gs, mm_of(ph_gs))
            blocks(pe, ph_ga, mm_of(ph_ga))
            pe.wait_ge(ct_cp, 8)
            pe.wait_ge(k_red, NB * NPG)
            for n in range(2):
                ins = mm(side[n][:, :], ones[:, :], sc[:, 4 * n:4 * n + 4].rearrange("p g b h -> p (g b h)"),
                         start=True, stop=True)
            ins.then_inc(sel_mm, 1)
            pe.wait_ge(max_dve, 1)
            turn(side[2][:, 0:P], m_w[:, 5, :]).then_inc(max_tr, 1)
            pe.wait_ge(max_dve, 3)
            mm(side[3][:, 0:P], ones[:, :], m_w[:, 7, :], start=True, stop=True).then_inc(max_mm, 1)
            pe.wait_ge(p_sum, 1)
            mm(side[0][:, 0:P], ones[:, :], m_w[:, 8, :], start=True, stop=True).then_inc(p_mm, 1)
            pe.wait_ge(p_done, 1)
            def v_page(i, m):
                b, g = 2 * i + m // NPG, m % NPG
                if g == 0:
                    pe.wait_ge(pz_done, 2 * b + 2)
                pe.wait_ge(kv_in[g % 4], 16 * (NB * NPG // 4 + 2 * b + g // 4 + 1))
                for n in range(2):
                    ins = mm(side[n][:, :], pz[:, g, :], kv[:, g % 4, n * 512:(n + 1) * 512],
                             start=(isinstance(i, int) and i == 0 and m == 0), stop=False)
                ins.then_inc(v_mm, 1)

            def z_side(i, qq):
                for u in range(2):
                    v_page(i, 2 * qq + u)

            pe.wait_ge(p_sub, 1)
            pe.wait_ge(p_done, 1)
            blocks(pe, ph_z, mm_of(ph_z), None, None, z_side)
            for n in range(2):
                ins = mm(side[n][:, :], sc[0:NB, NPG].rearrange("p b h -> p (b h)"), own_v[:, n * 512:(n + 1) * 512],
                         start=False, stop=True)
            ins.then_inc(v_mm, 1)
            pe.wait_ge(vm_done, 2)
            for k in range(AT):
                ins = mm(side[2][:, k * NB:(k + 1) * NB], vm[:, k * P:(k + 1) * P], bsel[:, :], start=True, stop=True)
            ins.then_inc(v_mm, 1)
            pe.wait_ge(a_lo_done, AT)

            def norm_pe(i, qq):
                if qq % 2:
                    g = 4 * i + qq // 2
                    wait(pe, un_sd, g)
                    for n in range(2):
                        pe.wait_ge(un_sq, 2 * g + n + 1)
                        mm(side[3][:, 0:T], ones[:, :], sq[:, n, :], start=(n == 0), stop=(n == 1)).then_inc(un_mm, 1)

            blocks(pe, ph_ao, mm_of(ph_ao), None, None, norm_pe)
            pe.wait_ge(u_lo, KT)
            blocks(pe, ph_so, mm_of(ph_so))
            pe.wait_ge(ao_lo, KT)
            blocks(pe, ph_o, mm_of(ph_o))
            pe.wait_ge(x_in, 96)
            pe.wait_ge(v_cp, 1)
            x_turns(xtok2, KT)
            pe.wait_ge(x_cp, 2 * KT)
            norm_sums(1, side[3])
            pe.wait_ge(nrm_sd, 2)
            norm_sums(2, side[3])
            pe.wait_ge(h_lo, 2 * KT)
            blocks(pe, ph_ff, mm_of(ph_ff))
            pe.wait_ge(ff_lo, FT)
            blocks(pe, ph_dn, mm_of(ph_dn))
            pe.wait_ge(nrm_sd, 3)
            norm_sums(3, side[3])
            pe.wait_ge(y2_done, KT)
            pe.wait_ge(nrm_sd, 4)
            for n in range(12):
                m = n // 3
                wait(pe, (y_cp, y_cp2)[n % 2], (n - 4) // 2 + 1)
                c = n % 3
                for u in range(4):
                    out = side[n % 4][0:(P if c < 2 else NB), u * P:(u + 1) * P]
                    ins = turn(out, x2[:, 4 * m + u, c * P:(c + 1) * P if c < 2 else T])
                ins.then_inc(y_tr, 1)


_INS = ["x_prompt", "x_sample", "cache_k", "cache_v", "state_conv", "state_ssm", "page_table",
        "norm_mix_pre", "w_in", "conv_w", "conv_b", "dt_bias", "a_log", "d_skip", "ssm_norm",
        "w_attn_out", "w_ssm_out", "w_out", "norm_mix_post",
        "norm_ffn_pre", "w_gate", "w_up", "w_down", "norm_ffn_post"]
_OUTS = [("y_prompt", (1, TP, D)), ("y_sample", (NB, 1, D)),
         ("k_prompt", (1, 1, TP, HEADS, HD)), ("v_prompt", (1, 1, TP, HEADS, HD)),
         ("conv_prompt", (1, 1, 3, CONVC)), ("ssm_prompt", (1, 1, SH, HD, NST)),
         ("k_sample", (1, NB, 1, HEADS, HD)), ("v_sample", (1, NB, 1, HEADS, HD)),
         ("conv_sample", (1, NB, 3, CONVC)), ("ssm_sample", (1, NB, SH, HD, NST))]


def kernel(**inputs):
    import numpy as np
    import concourse.bacc as bacc
    from concourse.bass_utils import run_bass_kernel_spmd

    nc = bacc.Bacc("TRN2", target_bir_lowering=False, num_devices=1)
    arrays, a, o = {}, {}, {}
    for name in _INS:
        x = np.ascontiguousarray(inputs[name])
        arrays[f"in_{name}"] = x
        a[name] = nc.dram_tensor(f"in_{name}", x.shape, mybir.dt.from_np(x.dtype), kind="ExternalInput").ap()
    for name, shape in _OUTS:
        o[name] = nc.dram_tensor(f"out_{name}", shape, fp32, kind="ExternalOutput").ap()
    bass_hybrid_decoder_layer(nc, a, o)
    r = run_bass_kernel_spmd(nc, [arrays], core_ids=[0])
    return tuple(r.results[0][f"out_{name}"] for name, _ in _OUTS)
```

```python
import concourse.bass as bass
from concourse import mybir
from contextlib import ExitStack

fp32 = mybir.dt.float32
f32r = mybir.dt.float32r
i32 = mybir.dt.int32
ALU = mybir.AluOpType
ACT = mybir.ActivationFunctionType
AX = mybir.AxisListType

P = 128
D = 2048
KT = D // P
TP = 256
NB = 8
T = TP + NB
HEADS = 16
HD = 64
AW = HEADS * HD
AT = AW // P
SH = 32
NG = 8
NST = 128
XT = 16
CT = XT + 2 * NG
FF = 5632
FT = FF // P
PAST = 1024
PG = 128
NPG = PAST // PG
NBLK = 4
EPS = 1e-6
NEG = -1e30
SCALE = HD ** -0.5
CONVC = CT * P
COL_Q, COL_Z, COL_X, COL_DT, COL_GA, COL_GS = 0, 3072, 5120, 9216, 9248, 11296
KG = 8
RING = 4
LAG = 3


def bass_hybrid_decoder_layer(nc, a, o):
    ctx = ExitStack()
    with ctx:
        def sem(name):
            return ctx.enter_context(nc.semaphore(name))

        base = (nc.sbuf_base + 63) // 64 * 64
        room = [base]

        def keep(name, shape, dt=fp32):
            n = 4
            for s in shape[1:]:
                n *= s
            t = nc.alloc_sbuf_tensor_at(name, shape, dt, offset=room[0])
            room[0] += (n + 63) // 64 * 64
            return t

        raw = keep("raw", [P, RING, KG, 256])
        w_hi = keep("w_hi", [P, RING, KG, P], f32r)
        w_lo = keep("w_lo", [P, RING, KG, P], f32r)
        ident = keep("ident", [P, P])
        ones = keep("ones", [P, P])
        upper = keep("upper", [P, P])
        dmask = keep("dmask", [P, NB])
        hmask = keep("hmask", [P, HEADS])
        bsel = keep("bsel", [P, NB])
        eps = keep("eps", [P, 1])
        zero = keep("zero", [P, 1])
        gains = keep("gains", [P, 5, KT])
        conv_k = keep("conv_k", [P, 4, CT])
        conv_bias = keep("conv_bias", [P, CT])
        dskip = keep("dskip", [P, XT])
        heads_c = keep("heads_c", [SH, 4])
        pages = keep("pages", [1, NB * NPG], i32)
        stat = keep("stat", [P, T])
        stat_r = keep("stat_r", [P, T])
        sq = keep("sq", [P, 2, T])
        tmp = keep("tmp", [P, 2, T])
        arena = room[0]
        room_end = nc.sbuf_usable_end - 64

        def at(name, shape, dt, offset):
            n = 4
            for s in shape[1:]:
                n *= s
            assert arena + offset + n <= room_end, (name, arena + offset + n - room_end)
            return nc.alloc_sbuf_tensor_at(name, shape, dt, offset=arena + offset)

        K = 1024
        M0 = (room_end - arena - 16 * K) // 64 * 64
        attn = at("attn", [P, AT, T], fp32, M0)
        tails = at("tails", [P, CT, 3 + NB], fp32, M0 + AT * T * 4)
        state_t = at("state_t", [P, CT, NB, 3], fp32, M0 + 10 * K)
        cmask = at("cmask", [P, 3 * P], fp32, M0 + 13 * K)
        dt_raw = at("dt_raw", [SH, T], fp32, M0 + 14 * K + 512)
        TILE16 = KT * T * 4
        x_hi = at("x_hi", [P, KT, T], f32r, 0)
        x_lo = at("x_lo", [P, KT, T], f32r, TILE16)
        A0 = 2 * TILE16
        xtok = at("xtok", [P, 3, D], fp32, A0)
        xT = at("xT", [P, KT, T], fp32, A0 + 24 * K)
        xh = at("xh", [P, KT, T], fp32, A0 + 58 * K)
        ctok = at("ctok", [24, CONVC], fp32, A0 + 42 * K)
        xbc = at("xbc", [P, CT, T], fp32, A0)
        A1 = A0 + 2 * TILE16
        qkv = at("qkv", [P, 24, T], fp32, A1)
        A2 = A1 + 24 * T * 4
        vtok = at("vtok", [P, 2, AW], fp32, A2)
        att_s = at("att_s", [P, 2, 3 * P], fp32, A2 + 8 * K)
        att_pt = at("att_pt", [P, 2, 3 * P], fp32, A2 + 11 * K)
        att_st = at("att_st", [P, 2, 8], fp32, A2 + 14 * K)
        qk_head = at("qk_head", [P, 2, TP], fp32, A2 + 14 * K + 64)
        v_head = at("v_head", [P, 2, P], fp32, A2 + 16 * K + 64)
        conv_in = at("conv_in", [P, 2, 3 + TP + 4 * NB], fp32, A2 + 17 * K + 64)
        conv_out = at("conv_out", [P, 2, TP + 4 * NB], fp32, A2 + 19 * K + 512)
        conv_th = at("conv_th", [P, 2, TP + 4 * NB], fp32, A2 + 22 * K)
        ktok = at("ktok", [P, 2, AW], fp32, A0 + 12 * T * 4)
        stok = at("stok", [NB, 3 * AW], fp32, A0 + 12 * T * 4 + 8 * K)
        assert 12 * T * 4 + 20 * K <= 2 * TILE16
        dt_w = at("dt_w", [SH, 6, T], fp32, A1)
        S0 = A1 - K
        bcrow = at("bcrow", [NB, 2 * NG * P], fp32, S0 + 40 * K)
        xdt = at("xdt", [P, 2, D], fp32, S0 + 8 * K)
        btok = at("btok", [P, 2, NG * P], fp32, S0 + 24 * K)
        xw = at("xw", [P, 256], fp32, S0 + 32 * K)
        xw1 = at("xw1", [P, 2, 256], fp32, S0 + 33 * K)
        hT0 = at("hT0", [P, 256], fp32, S0 + 35 * K)
        seg = at("seg", [P, 2, 4 * P], fp32, S0 + 36 * K)
        dec = at("dec", [P, 2, 4 * P], fp32, S0 + 40 * K)
        cexp = at("cexp", [P, 4 * P], fp32, S0 + 44 * K)
        cbm = at("cbm", [P, 2, P], fp32, S0 + 46 * K)
        dtok = at("dtok", [P, 2, 2, SH], fp32, S0 + 47 * K)
        acum = at("acum", [P, 2, SH], fp32, S0 + 47 * K + 512)
        dend = at("dend", [P, 2, SH], fp32, S0 + 47 * K + 768)
        cdec = at("cdec", [P, SH], fp32, S0 + 48 * K)
        hfin = at("hfin", [P, 2, P], fp32, S0 + 48 * K + 128)
        crow = at("crow", [3 + NB, CONVC], fp32, A1)
        scal = at("scal", [P, XT, 2 * NB], fp32, M0 + 14 * K)
        xdts = at("xdts", [P, XT, NB], fp32, M0 + 15 * K)
        ysam = at("ysam", [P, XT, NB], fp32, M0 + 15 * K + 512)
        un = at("un", [P, 4, T], fp32, M0 + 10 * K)
        zs = at("zs", [P, XT, NB], fp32, M0 + AT * T * 4)
        gate_s = at("gate_s", [P, KT, T], fp32, A0 + TILE16)
        gate_a = at("gate_a", [P, KT, T], fp32, A1)
        F0 = A1 + TILE16
        kv = at("kv", [P, 4, AW], fp32, F0)
        vm = at("vm", [P, AW], fp32, F0)
        qb = at("qb", [P, 2, AW], fp32, F0 + 16 * K)
        pz = at("pz", [P, NPG, P], fp32, F0 + 16 * K)
        bc = at("bc", [P, 2, 2, 256], fp32, F0 + 20 * K)
        sc = at("sc", [P, NPG + 1, NB, HEADS], fp32, F0 + 24 * K)
        W0 = F0 + 24 * K + (NPG + 1) * P * 4
        m_w = at("m_w", [P, 10, P], fp32, W0)
        st = at("st", [P, 2, 4, P], fp32, W0)
        stx = at("stx", [P, 4, P], fp32, W0 + 4 * K)
        assert W0 + 6 * K <= M0
        own_v = at("own_v", [NB, AW], fp32, M0 + 10 * K)
        own_qk = at("own_qk", [NB, 2, AW], fp32, F0 + 8 * K)
        a_hi = at("a_hi", [P, AT, T], f32r, F0)
        a_lo = at("a_lo", [P, AT, T], f32r, F0 + AT * T * 4)
        u_sq = at("u_sq", [P, KT, T], fp32, F0 + TILE16)
        m_hi = at("m_hi", [P, KT, T], f32r, A0)
        m_lo = at("m_lo", [P, KT, T], f32r, F0)
        mo = at("mo", [P, KT, T], fp32, A1)
        x1 = at("x1", [P, KT, T], fp32, A0 + TILE16)
        g_hi = at("g_hi", [P, FT, T], f32r, A0)
        g_lo = at("g_lo", [P, FT, T], f32r, A0 + FT * T * 4)
        glu = at("glu", [P, 3, 2, T], fp32, A0 + 2 * FT * T * 4)
        fo = at("fo", [P, KT, T], fp32, 0)
        x2 = at("x2", [P, KT, T], fp32, TILE16)
        ytok = at("ytok", [P, 3, D], fp32, A0)

        gemm_ps = [ctx.enter_context(nc.psum_tensor(f"gemm{n}", [P, 512], fp32)) for n in range(4)]
        side = [ctx.enter_context(nc.psum_tensor(f"side{n}", [P, 512], fp32)) for n in range(4)]

        q_row = nc.dram_tensor("q_row", [NB, AW], fp32, kind="Internal").ap()
        bc_row = nc.dram_tensor("bc_row", [NB, 2, NG * P], fp32, kind="Internal").ap()
        x_kept = nc.dram_tensor("x_kept", [P, KT * T], fp32, kind="Internal").ap()
        x1_spill = nc.dram_tensor("x1_spill", [P, KT * T], fp32, kind="Internal").ap()

        w_in, w_ao, w_so, w_o = a["w_in"][0], a["w_attn_out"][0], a["w_ssm_out"][0], a["w_out"][0]
        w_g, w_u, w_d = a["w_gate"][0], a["w_up"][0], a["w_down"][0]

        class Phase:
            made = []

            def __init__(self, ws, col, kt, pairs, hi, lo, per=2):
                self.ws, self.col, self.kt, self.pairs, self.per = ws, col, kt, pairs, per
                self.hi, self.lo = hi, lo
                self.loads = -(-kt // KG)
                self.lag = min(LAG, 2 * self.loads - 1)
                before = Phase.made[-1] if Phase.made else None
                self.load0 = before.load0 + before.pairs * before.loads if before else 0
                self.pair0 = before.pair0 + before.pairs if before else 0
                self.iters = pairs // per
                assert pairs % per == 0 and (self.load0 % 2 == 0) and self.pair0 % 2 in (0, 1)
                assert self.iters == 1 or (per * self.loads % RING == 0 and per % 2 == 0)
                Phase.made.append(self)

        ph_qkv = Phase([w_in], COL_Q, KT, 12, x_hi, x_lo)
        ph_dt = Phase([w_in], COL_DT, KT, 1, x_hi, x_lo, per=1)
        ph_xbc = Phase([w_in], COL_X, KT, 16, x_hi, x_lo)
        ph_gs = Phase([w_in], COL_GS, KT, 8, x_hi, x_lo)
        ph_ga = Phase([w_in], COL_GA, KT, 8, x_hi, x_lo)
        ph_z = Phase([w_in], COL_Z, KT, 8, x_hi, x_lo)
        ph_ao = Phase([w_ao], 0, AT, 8, a_hi, a_lo, per=4)
        ph_so = Phase([w_so], 0, KT, 8, x_hi, x_lo)
        ph_o = Phase([w_o], 0, KT, 8, m_hi, m_lo)
        ph_ff = Phase([w_g, w_u], 0, KT, 44, x_hi, x_lo)
        ph_dn = Phase([w_d], 0, FT, 8, g_hi, g_lo)

        loaded = [sem(f"loaded{s}") for s in range(RING)]
        free_out = [sem("free_out0"), sem("free_out1")]
        (hi_done, lo_done, mm_done, consts_in, pages_in, state_in, consts_made, x_in, x_tr, x_cp, nrm_sq, nrm_mm,
         nrm_sd, nrm_rs, h_mul, h_hi, h_lo, tok_tr, tok_out, cst_tr, cst_cp, qk_staged, v_staged, s_mm, s_masked,
         s_max, s_nmax, s_exp, s_rcp, s_norm, pt_mm, pt_cp, pv_mm, attn_cp, conv_st, conv_step, conv_tanh,
         xbc_done, tail_cp, dt_act, dt_dve, dt_tr, dt_tok, dt_sum, dt_ac, dt_de, xb_tr, r_mm, cb_mm, seg_done,
         cbm_done, dec_done, m_done, cx_exp, cx_done, xw_done, xwf_done, ht_mm, ht_cp, y_mm, y_done, fin_mm,
         fin_cp, fin_out, ct_tr, ct_cp, ct_out, bc_tr, bc_cp, bc_out, ex_mm, ex_cp, sx_mul, stx_done, st_new,
         st_prod, st_sum, ysam_done, z_tanh, u_done, un_sq, un_mm, un_sd, un_rs, un_mul, own_in, own_mul, own_sum,
         own_put, k_mul, k_red, sel_mm, sel_dve, max_tr, max_dve, max_mm, p_sub, p_exp, p_sum, p_mm, p_rcp, p_done,
         v_mm, v_cp, u_hi, u_lo, a_hi_done, a_lo_done, ao_sum, ao_hi, ao_lo, x1_done, x1_out, x1_in, ff_tanh,
         ff_hi, ff_lo, y2_done, y_tr, y_cp, y_out, cs_out, y_cp2, o_scaled, f_scaled, qb_in, pz_done, vm_done,
         x_keep, x_back) = [sem(n) for n in (
            "hi_done lo_done mm_done consts_in pages_in state_in consts_made x_in x_tr x_cp nrm_sq nrm_mm nrm_sd "
            "nrm_rs h_mul h_hi h_lo tok_tr tok_out cst_tr cst_cp qk_staged v_staged s_mm s_masked s_max s_nmax s_exp "
            "s_rcp s_norm pt_mm pt_cp pv_mm attn_cp conv_st conv_step conv_tanh xbc_done tail_cp dt_act dt_dve dt_tr "
            "dt_tok dt_sum dt_ac dt_de xb_tr r_mm cb_mm seg_done cbm_done dec_done m_done cx_exp cx_done xw_done "
            "xwf_done ht_mm ht_cp y_mm y_done fin_mm fin_cp fin_out ct_tr ct_cp ct_out bc_tr bc_cp bc_out ex_mm ex_cp "
            "sx_mul stx_done st_new st_prod st_sum ysam_done z_tanh u_done un_sq un_mm un_sd un_rs un_mul own_in "
            "own_mul own_sum own_put k_mul k_red sel_mm sel_dve max_tr max_dve max_mm p_sub p_exp p_sum p_mm p_rcp "
            "p_done v_mm v_cp u_hi u_lo a_hi_done a_lo_done ao_sum ao_hi ao_lo x1_done x1_out x1_in ff_tanh ff_hi "
            "ff_lo y2_done y_tr y_cp y_out cs_out y_cp2 o_scaled f_scaled qb_in pz_done vm_done x_keep x_back ").split()]
        tok_cp = [sem("tok_cp0"), sem("tok_cp1")]
        xb_cp = [sem("xb_cp0"), sem("xb_cp1")]
        kv_in = [sem(f"kv_in{s}") for s in range(4)]
        st_in = [sem(f"st_in{s}") for s in range(2)]
        st_out = [sem(f"st_out{s}") for s in range(2)]
        CONSTS = 13 + 5 + NB

        def wait(eng, s, v):
            if not isinstance(v, int) or v > 0:
                eng.wait_ge(s, v)

        def then(eng, ins, s, v):
            ins.then_inc(s, 1)
            eng.wait_ge(s, v)

        def block_no(ph, i, qq):
            return 2 * (ph.load0 + ph.per * ph.loads * i) + qq

        def k_tiles(ph, q):
            return min(KG, ph.kt - KG * (q // 2))

        def last_block(ph, pr, n):
            return 2 * (ph.load0 + ph.loads * pr) + 2 * ph.loads - 1 + n

        def blocks(eng, ph, step, evac=None, before=None, side_work=None):
            n = 2 * ph.loads

            def previous(i, j):
                par = (ph.pair0 + j - 1) % 2
                evac(ph.per * i + j - 1, par, (ph.pair0 + j - 1 - par) // 2 + ph.per // 2 * i)

            def body(i, first):
                for j in range(ph.per):
                    for q in range(n):
                        step(i, j, q, j * n + q)
                        if q == ph.lag - 1 and j == 0:
                            first()
                        elif q == ph.lag - 1 and evac:
                            previous(i, j)
                        if side_work:
                            side_work(i, j * n + q)

            body(0, before or (lambda: None))
            if ph.iters > 1:
                with eng.Fori(1, ph.iters) as i:
                    body(i, (lambda: previous(i, 0)) if evac else (lambda: None))
            end = ph.pairs - 1
            par = (ph.pair0 + end) % 2
            return (lambda: evac(end, par, (ph.pair0 + end - par) // 2)) if evac else None

        def none_free(ph):
            total = ph.pair0 + ph.pairs
            return [2 * ((total + 1) // 2), 2 * (total // 2)]

        CW = TP + 4 * NB

        def news(t, n):
            return t[:, n, TP + 3:TP + 3 + 4 * NB].rearrange("p (b w) -> p b w", w=4)

        def one(t, k):
            return t[:, bass.ds(k, 1)].rearrange("p o t -> p (o t)")

        def tok_dst(n):
            if n < 8:
                dst = (ktok, vtok)[n // 4][:, (n // 2) % 2, (n % 2) * 512:(n % 2) * 512 + 512]
                return dst, side[n % 4][:, :]
            return stok[:, (n - 8) * 512:(n - 7) * 512], side[n % 4][0:NB, :]

        def earlier(i, m, lag, per):
            i, m = (i - 1, m - lag + per) if m < lag else (i, m - lag)
            return None if isinstance(i, int) and i < 0 else (i, m)

        def beside(work):
            def side_work(i, qq):
                work(i, qq)
                if not (isinstance(i, int) and i == 0):
                    work(i - 1, qq + 8)
            return side_work

        def finish(work, last=None):
            for pos in range(8, 16):
                if pos == 8 + LAG - 1 and last:
                    last()
                work(ph_xbc.iters - 1, pos)

        SP_LAG = 4

        def kpage(ph, i, m):
            return (0 if ph is ph_gs else NB // 2) + i, m

        def y_dst(n):
            m, c = n // 3, n % 3
            rows = P if c < 2 else NB
            return ytok[0:rows, c, m * 512:(m + 1) * 512], side[n % 4][0:rows, :]

        block = ctx.enter_context(nc.Block())

        @block.sync
        def _(sp):
            def vec(ap):
                return ap.rearrange("(k p) -> p k", p=P)

            for c in range(2):
                sp.dma_start(xtok[:, c, :], a["x_prompt"][0, c * P:(c + 1) * P, :]).then_inc(x_in, 16)
            sp.dma_start(xtok[0:NB, 2, :], a["x_sample"][:, 0, :]).then_inc(x_in, 16)

            def load(ph, i, l):
                j, kg = l // ph.loads, l % ph.loads
                kts = min(KG, ph.kt - KG * kg)
                s = (ph.load0 + l) % RING
                w = ph.ws[j % len(ph.ws)]
                pair = (ph.per * i + j) if len(ph.ws) == 1 else i
                src = w[kg * KG * P:(kg * KG + kts) * P, bass.ds(ph.col + 256 * pair, 256)]
                wait(sp, lo_done, 2 * (ph.load0 + ph.per * ph.loads * i + l - RING) + 2)
                sp.dma_start(raw[:, s, 0:kts, :], src.rearrange("(k p) n -> p k n", p=P)).then_inc(loaded[s], 16)

            def weights(ph, side_work=None):
                def body(i):
                    for l in range(ph.per * ph.loads):
                        load(ph, i, l)
                        if side_work:
                            side_work(i, l)

                body(0)
                if ph.iters > 1:
                    with sp.Fori(1, ph.iters) as i:
                        body(i)

            with nc.allow_non_contiguous_dma(reason="per-channel vectors"):
                for n, g in enumerate(("norm_mix_pre", "norm_mix_post", "norm_ffn_pre", "norm_ffn_post", "ssm_norm")):
                    sp.dma_start(gains[:, n, :], vec(a[g][0])).then_inc(consts_in, 16)
                for n in range(4):
                    sp.dma_start(conv_k[:, n, :], vec(a["conv_w"][0, n])).then_inc(consts_in, 16)
                sp.dma_start(conv_bias[:, :], vec(a["conv_b"][0])).then_inc(consts_in, 16)
                for n, g in enumerate(("dt_bias", "a_log")):
                    sp.dma_start(heads_c[:, n:n + 1], a[g][0].rearrange("(h o) -> h o", o=1)).then_inc(consts_in, 16)
                for h in range(2):
                    d = a["d_skip"][0].rearrange("(t h) -> h t", h=2)[h]
                    sp.dma_start(dskip[h * HD:(h + 1) * HD, :], d.partition_broadcast(HD)).then_inc(consts_in, 16)
            sp.dma_start(pages[0:1, :], a["page_table"].rearrange("b g -> (b g)").rearrange("(o n) -> o n", o=1))\
                .then_inc(pages_in, 16)
            sp.dma_start(ctok[:, :], a["state_conv"][0].rearrange("b w c -> (b w) c")).then_inc(state_in, 16)
            sp.dma_start(o["conv_sample"][0, :, 0:2, :], a["state_conv"][0, :, 1:3, :]).then_inc(cs_out, 16)
            weights(ph_qkv)
            weights(ph_dt)
            def token_rows(i, l):
                if not (isinstance(i, int) and i == 0 and l == 3):
                    return
                for s in tok_cp:
                    sp.wait_ge(s, 7)
                for c in range(2):
                    rows = slice(c * P, (c + 1) * P)
                    for name, t in (("k_prompt", ktok), ("v_prompt", vtok)):
                        sp.dma_start(o[name][0, 0, rows].rearrange("s h d -> s (h d)"), t[:, c, :]).then_inc(tok_out, 16)
                sp.dma_start(q_row, stok[:, 0:AW]).then_inc(tok_out, 16)
                for n, name in enumerate(("k_sample", "v_sample")):
                    sp.dma_start(o[name][0, :, 0].rearrange("b h d -> b (h d)"), stok[:, (n + 1) * AW:(n + 2) * AW])\
                        .then_inc(tok_out, 16)

            weights(ph_xbc, token_rows)
            def ssd_results():
                for g in range(NG):
                    sp.wait_ge(fin_cp, g + 1)
                    dst = o["ssm_prompt"][0, 0].rearrange("h p n -> (h p) n")[g * 256:(g + 1) * 256]
                    sp.dma_start(dst.rearrange("(t p) n -> p t n", p=P), hfin[:, :, :]).then_inc(fin_out, 16)
                sp.wait_ge(bc_cp, 4)
                sp.dma_start(bc_row.rearrange("b w n -> b (w n)"), bcrow[:, :]).then_inc(bc_out, 16)
                sp.wait_ge(bc_out, 16)
                sp.wait_ge(y_done, 2 * NG)
                sp.wait_ge(fin_out, 16 * NG)
                sp.wait_ge(ex_cp, 1)
                sp.wait_ge(tok_out, 16 * 7)
                sp.dma_start(own_qk[:, 0, :], q_row).then_inc(own_in, 16)
                sp.dma_start(own_qk[:, 1, :], o["k_sample"][0, :, 0].rearrange("b h d -> b (h d)")).then_inc(own_in, 16)
                sp.dma_start(own_v[:, :], o["v_sample"][0, :, 0].rearrange("b h d -> b (h d)")).then_inc(own_in, 16)

            kc = a["cache_k"][0].rearrange("g s h d -> g s (h d)")
            vc = a["cache_v"][0].rearrange("g s h d -> g s (h d)")

            def page_in(cache, b, g, freed, v):
                pg = sp.value_load(pages[0:1, bass.ds(NPG * b + g, 1)], min_val=0, max_val=a["cache_k"].shape[1] - 1)
                src = cache[bass.ds(pg, 1)].rearrange("g p n -> p g n")
                wait(sp, freed, v)
                sp.dma_start(kv[:, g % 4:g % 4 + 1, :], src).then_inc(kv_in[g % 4], 16)

            def k_in(b, g):
                if g == 0:
                    src = q_row[bass.ds(b, 1), :].rearrange("o n -> (o n)").partition_broadcast(P)
                    dst = qb[:, bass.ds(b % 2, 1), :].rearrange("p o n -> p (o n)")
                    if not (isinstance(b, int) and b == 0):
                        wait(sp, k_mul, NPG * b - NPG + 1)
                    sp.dma_start(dst, src).then_inc(qb_in, 16)
                page_in(kc, b, g, k_red, NPG * b + g - 3)

            def k_side(ph):
                def side_work(i, l):
                    if ph is ph_gs and isinstance(i, int) and i == 0 and l == 1:
                        ssd_results()
                        sp.wait_ge(pages_in, 16)
                        sp.wait_ge(own_put, 1)
                    for m in (2 * l, 2 * l + 1):
                        at_ = earlier(i, m, SP_LAG, 8)
                        if at_:
                            k_in(*kpage(ph, *at_))
                        elif ph is ph_ga:
                            k_in(NB // 2 - 1, m + 8 - SP_LAG)
                return side_work

            weights(ph_gs, k_side(ph_gs))
            sp.wait_ge(ct_cp, 8)
            sp.dma_start(o["conv_prompt"][0, 0], crow[0:3, :]).then_inc(ct_out, 16)
            sp.dma_start(o["conv_sample"][0, :, 2, :], crow[3:3 + NB, :]).then_inc(ct_out, 16)
            weights(ph_ga, k_side(ph_ga))
            for m in range(8 - SP_LAG, 8):
                k_in(NB - 1, m)

            hs = a["state_ssm"][0].rearrange("b h p n -> b (h p) n")
            ho = o["ssm_sample"][0].rearrange("b h p n -> b (h p) n")

            def state_rows(x, b, r):
                return x[bass.ds(b, 1), r * 512:(r + 1) * 512, :].rearrange("o (t p) n -> p (o t) n", p=P)

            def state_store(i, m):
                dst = state_rows(ho, 2 * i + m // 4, m % 4)
                sp.wait_ge(st_sum, 8 * i + m + 1)
                sp.dma_start(dst, st[:, m % 2]).then_inc(st_out[m % 2], 16)

            def state_load(i, m):
                b, r = 2 * i + m // 4, m % 4
                src = state_rows(hs, b, r)
                rows = bc_row[bass.ds(b, 1), :, r * 256:(r + 1) * 256].rearrange("o w n -> (o w) n")
                wait(sp, st_out[m % 2], 16 * (4 * i + m // 2))
                sp.dma_start(st[:, m % 2], src).then_inc(st_in[m % 2], 16)
                sp.dma_start(bc[:, m % 2], rows.partition_broadcast(P)).then_inc(st_in[m % 2], 16)

            def v_in(i, m):
                page_in(vc, 2 * i + m // NPG, m % NPG, v_mm, 16 * i + m - 3)

            def z_items(i, l, lag):
                if isinstance(i, int) and i == 0 and l == 2:
                    sp.wait_ge(k_red, NB * NPG)
                    sp.wait_ge(k_mul, NB * NPG)
                    sp.wait_ge(p_done, 1)
                for m in (2 * l, 2 * l + 1):
                    before = earlier(i, m, lag + 2, 8)
                    if before:
                        state_store(*before)
                    at_ = earlier(i, m, lag, 8)
                    if at_:
                        for u in range(2):
                            v_in(at_[0], 2 * at_[1] + u)
                        state_load(*at_)

            weights(ph_z, lambda i, l: z_items(i, l, SP_LAG))
            for l in range(2):
                z_items(ph_z.iters, l, SP_LAG)
            for m in (6, 7):
                state_store(ph_z.iters - 1, m)
            weights(ph_ao)
            weights(ph_so)
            weights(ph_o)
            for s in range(2):
                sp.wait_ge(st_out[s], 16 * 2 * NB)
            sp.wait_ge(ct_out, 32)
            sp.wait_ge(ao_lo, KT)
            sp.wait_ge(x_keep, 16)
            sp.dma_start(x1[:, :, :].rearrange("p k t -> p (k t)"), x_kept).then_inc(x_back, 16)

            def spill(i, l):
                if isinstance(i, int) and i == 0 and l == 3:
                    sp.wait_ge(x1_done, KT)
                    sp.dma_start(x1_spill, x1[:, :, :].rearrange("p k t -> p (k t)")).then_inc(x1_out, 16)

            weights(ph_ff, spill)
            weights(ph_dn)
            sp.wait_ge(x1_out, 16)
            sp.wait_ge(mm_done, block_no(ph_dn, 0, 0))
            sp.dma_start(x2[:, :, :].rearrange("p k t -> p (k t)"), x1_spill).then_inc(x1_in, 16)
            for n in range(12):
                m, c = n // 3, n % 3
                sp.wait_ge((y_cp, y_cp2)[n % 2], n // 2 + 1)
                cols = slice(m * 512, (m + 1) * 512)
                if c < 2:
                    sp.dma_start(o["y_prompt"][0, c * P:(c + 1) * P, cols], ytok[:, c, cols]).then_inc(y_out, 16)
                else:
                    sp.dma_start(o["y_sample"][:, 0, cols], ytok[0:NB, 2, cols]).then_inc(y_out, 16)
            sp.wait_ge(y_out, 16 * 12)
            sp.wait_ge(cs_out, 16)

        @block.gpsimd
        def _(gp):
            made = [0]

            def made_one(ins):
                made[0] += 1
                then(gp, ins, consts_made, made[0])

            made_one(gp.memset(ident[:, :], 0.0))
            made_one(gp.affine_select(out=ident[:, :], in_=ident[:, :], compare_op=ALU.not_equal, fill=1.0, base=0,
                                      pattern=[[-1, P]], channel_multiplier=1))
            made_one(gp.memset(ones[:, :], 1.0))
            made_one(gp.memset(eps[:, :], EPS))
            made_one(gp.affine_select(out=upper[:, :], in_=ones[:, :], compare_op=ALU.is_ge, fill=0.0, base=0,
                                      pattern=[[1, P]], channel_multiplier=-1))
            made_one(gp.memset(cmask[:, :], 0.0))
            for c in (0, 2):
                made_one(gp.affine_select(out=cmask[:, c * P:(c + 1) * P], in_=cmask[:, c * P:(c + 1) * P],
                                          compare_op=ALU.is_ge, fill=NEG, base=0, pattern=[[-1, P]],
                                          channel_multiplier=1))
            made_one(gp.memset(dmask[:, :], 0.0))
            made_one(gp.affine_select(out=dmask[:, :], in_=dmask[:, :], compare_op=ALU.is_equal, fill=NEG, base=0,
                                      pattern=[[-1, NB]], channel_multiplier=1))
            made_one(gp.memset(conv_in[:, :, 0:3], 0.0))
            gp.wait_ge(consts_in, 16 * 14)
            made_one(gp.tensor_scalar(out=conv_k[:, :, :], in0=conv_k[:, :, :], scalar1=0.5, scalar2=None,
                                      op0=ALU.mult))
            made_one(gp.tensor_scalar(out=conv_bias[:, :], in0=conv_bias[:, :], scalar1=0.5, scalar2=None,
                                      op0=ALU.mult))
            made_one(gp.memset(bsel[:, :], 1.0))
            for sign, off in ((1, 0), (-1, HEADS - 1)):
                made_one(gp.affine_select(out=bsel[:, :], in_=bsel[:, :], compare_op=ALU.is_ge, fill=0.0, base=off,
                                          pattern=[[-sign * HEADS, NB]], channel_multiplier=sign))
            made_one(gp.memset(hmask[:, :], 0.0))
            made_one(gp.memset(zero[:, :], 0.0))
            for b in range(NB):
                ins = gp.affine_select(out=hmask[:, :], in_=hmask[:, :], compare_op=ALU.not_equal, fill=1.0,
                                       base=-HEADS * b, pattern=[[-1, HEADS]], channel_multiplier=1)
                made_one(ins)
            assert made[0] == CONSTS

            for par in range(2):
                gp.wait_ge(free_out[par], none_free(ph_qkv)[par])
            gp.wait_ge(cst_cp, 8)

            def stage_qk(i):
                for w in range(2):
                    ins = gp.tensor_copy(qk_head[:, w:w + 1, :],
                                         qkv[:, bass.ds(i + AT * w, 1), 0:TP])
                ins.then_inc(qk_staged, 1)

            def stage_v(i):
                wait(gp, pv_mm, 2 * i)
                gp.tensor_copy(v_head[:, :, :], vtok[:, :, bass.ds(P * i, P)]).then_inc(v_staged, 1)

            def conv_pair(i, j):
                base = (ph_xbc.pair0 + j) // 2 * 2 + 2 * i
                for n in range(2):
                    t = 4 * i + 2 * j + n
                    wait(gp, conv_step, 8 * (2 * i + j) + n - 1)
                    gp.tensor_copy(news(conv_in, n)[:, :, 0:3],
                                   state_t[:, bass.ds(t, 1)].rearrange("p o b w -> p (o b) w")).then_inc(conv_st, 1)
                for n in range(2):
                    t = 4 * i + 2 * j + n
                    gp.wait_ge(free_out[(ph_xbc.pair0 + j) % 2], base + n + 1)
                    gp.tensor_copy(tails[:, bass.ds(t, 1), 0:3], conv_in[:, n:n + 1, TP:TP + 3])
                    gp.tensor_copy(tails[:, bass.ds(t, 1), 3:3 + NB],
                                   news(conv_in, n)[:, :, 3:4].rearrange("p b o -> p o b")).then_inc(tail_cp, 1)

            stage_qk(0)
            for s in tok_cp:
                gp.wait_ge(s, 7)

            def xbc_iter(i, more):
                conv_pair(i, 0)
                stage_v(i)
                if more:
                    gp.wait_ge(s_mm, 2 * i + 2)
                    stage_qk(i + 1)
                conv_pair(i, 1)

            xbc_iter(0, True)
            with gp.Fori(1, ph_xbc.iters - 1) as i:
                xbc_iter(i, True)
            xbc_iter(ph_xbc.iters - 1, False)
            gp.wait_ge(dt_de, 2)
            gp.wait_ge(xb_cp[0], 8)
            gp.wait_ge(xb_cp[1], 4)

            def by_head(x):
                return x.rearrange("p (h d) -> p h d", d=HD)

            for g in range(NG):
                for c in range(2):
                    wait(gp, fin_mm, g)
                    w = dend[:, c, 4 * g:4 * g + 4].unsqueeze(2).to_broadcast([P, 4, HD])
                    then(gp, gp.tensor_tensor(out=by_head(xw1[:, c]), in0=by_head(xdt[:, c, g * 256:(g + 1) * 256]),
                                              in1=w, op=ALU.mult), xw_done, 2 * g + c + 1)
                w = cdec[:, 4 * g:4 * g + 4].unsqueeze(2).to_broadcast([P, 4, HD])
                gp.tensor_tensor(out=by_head(xw[:, :]), in0=by_head(xw1[:, 0]), in1=w, op=ALU.mult).then_inc(xwf_done, 1)
            def k_times_q(i):
                for n in range(2):
                    b = 2 * i + n
                    gp.wait_ge(qb_in, 16 * b + 16)
                    for g in range(NPG):
                        s = g % 4
                        gp.wait_ge(kv_in[s], 16 * (2 * b + g // 4 + 1))
                        gp.tensor_tensor(out=kv[:, s], in0=kv[:, s], in1=qb[:, n], op=ALU.mult).then_inc(k_mul, 1)

            k_times_q(0)
            with gp.Fori(1, NB // 2) as i:
                k_times_q(i)
            gp.wait_ge(p_done, 1)

            def place_p(b):
                cols = sc[:, 0:NPG, bass.ds(b, 1), :].rearrange("p g b h -> p g (b h)")
                if not isinstance(b, int):
                    gp.wait_ge(v_mm, NPG * b)
                    then(gp, gp.tensor_copy(pz[:, :, bass.ds(HEADS * b - HEADS, HEADS)],
                                            zero[:, :].unsqueeze(2).to_broadcast([P, NPG, HEADS])), pz_done, 2 * b + 1)
                gp.tensor_copy(pz[:, :, bass.ds(HEADS * b, HEADS)], cols).then_inc(pz_done, 1)

            then(gp, gp.memset(pz[:, :, :], 0.0), pz_done, 1)
            place_p(0)
            with gp.Fori(1, NB) as b:
                place_p(b)

        @block.scalar
        def _(act):
            def func(out, in_, f=ACT.Copy, **kw):
                return nc.scalar.activation(out, in_, f, **kw)

            def hi_of(ph):
                def step(i, j, q, qq):
                    s, n, kts = (ph.load0 + qq // 2) % RING, qq % 2, k_tiles(ph, q)
                    if n == 0:
                        act.wait_ge(loaded[s], 16 * ((ph.load0 + qq // 2) // RING + 1 + ph.per * ph.loads // RING * i))
                    wait(act, mm_done, block_no(ph, i, qq) - RING + 1)
                    func(w_hi[:, (2 * ph.load0 + qq) % RING, 0:kts], raw[:, s, 0:kts, n * P:(n + 1) * P])\
                        .then_inc(hi_done, 1)
                return step

            def x_copies(dst, n0):
                for k in range(KT):
                    act.wait_ge(x_tr, n0 + k + 1)
                    func(dst[:, k, :], side[k % 3][:, 0:T]).then_inc(x_cp, 1)

            def root(n):
                act.wait_ge(nrm_mm, KT * (n + 1))
                wait(act, nrm_rs, n)
                func(stat[:, :], side[3][:, 0:T], ACT.Sqrt, bias=eps[:, 0:1], scale=1.0 / D).then_inc(nrm_sd, 1)

            def x_hi_from(src, n):
                for k in range(KT):
                    act.wait_ge(h_mul, KT * n + k + 1)
                    func(x_hi[:, k, :], src[:, k, :]).then_inc(h_hi, 1)

            act.wait_ge(consts_made, CONSTS)
            x_copies(xT, 0)
            act.wait_ge(x_cp, KT)
            act.dma_start(x_kept, xT[:, :, :].rearrange("p k t -> p (k t)")).then_inc(x_keep, 16)
            root(0)
            x_hi_from(xh, 0)
            for n in range(8):
                act.wait_ge(cst_tr, n + 1)
                src = side[n % 4][:, 0:4 * 3 * NB].rearrange("p (t b w) -> p t b w", t=4, w=3)
                func(state_t[:, 4 * n:4 * n + 4], src).then_inc(cst_cp, 1)

            def qkv_evac(pr, par, gen):
                for n in range(2):
                    act.wait_ge(mm_done, last_block(ph_qkv, pr, n))
                    func(one(qkv, 2 * pr + n), gemm_ps[2 * par + n][:, 0:T]).then_inc(free_out[par], 1)

            def dt_evac(pr, par, gen):
                act.wait_ge(mm_done, last_block(ph_dt, pr, 1))
                func(dt_raw[:, :], gemm_ps[2 * par][0:SH, 0:T]).then_inc(free_out[par], 2)

            act.wait_ge(x_keep, 16)
            last = blocks(act, ph_qkv, hi_of(ph_qkv), qkv_evac)
            last = blocks(act, ph_dt, hi_of(ph_dt), dt_evac, last)
            last()
            for n in range(0, 14, 2):
                act.wait_ge(tok_tr, n + 1)
                func(*tok_dst(n)).then_inc(tok_cp[0], 1)

            def conv_evac(pr, par, gen):
                for n in range(2):
                    t = 2 * pr + n
                    act.wait_ge(mm_done, last_block(ph_xbc, pr, n))
                    act.wait_ge(conv_st, t + 1)
                    wait(act, tail_cp, t - 1)
                    ps = gemm_ps[2 * par + n]
                    func(conv_in[:, n, 3:3 + TP], ps[:, 0:TP])
                    func(news(conv_in, n)[:, :, 3], ps[:, TP:T]).then_inc(free_out[par], 1)

            def conv_act(pr):
                for n in range(2):
                    act.wait_ge(conv_step, 8 * pr + 7 + n)
                    wait(act, xbc_done, 2 * pr + n - 1)
                    func(conv_th[:, n, :], conv_out[:, n, :], ACT.Tanh).then_inc(conv_tanh, 1)

            def attn_out(i):
                act.wait_ge(pv_mm, 2 * i + 2)
                func(attn[:, bass.ds(i, 1), 0:TP].rearrange("p o t -> p (o t)"), side[3][:, 0:TP]).then_inc(attn_cp, 1)

            def attn_act(i, pos):
                if pos in (5, 6):
                    x = pos - 5
                    act.wait_ge(s_nmax, 2 * i + x + 1)
                    wait(act, s_norm, 2 * i - 1 + x)
                    for m, cols in enumerate((slice(0, P), slice(P, 3 * P))):
                        ins = func(att_s[:, x, cols], att_s[:, x, cols], ACT.Exp, scale=SCALE,
                                   bias=att_st[:, x, 2 + m:3 + m], accum_out=att_st[:, x, 4 + m:5 + m])
                    ins.then_inc(s_exp, 1)
                if pos in (9, 11):
                    x = pos // 2 - 4
                    act.wait_ge(pt_mm, 2 * i + x + 1)
                    func(att_pt[:, x, :], side[2][:, 0:3 * P]).then_inc(pt_cp, 1)
                if pos == 13:
                    attn_out(i)
                if pos == 7:
                    conv_act(2 * i)
                if pos == 11:
                    conv_act(2 * i + 1)

            last = blocks(act, ph_xbc, hi_of(ph_xbc), conv_evac, None, beside(attn_act))
            finish(attn_act, last)

            act.wait_ge(free_out[ph_dt.pair0 % 2], none_free(ph_dt)[ph_dt.pair0 % 2])
            then(act, func(dt_w[:, 0, :], dt_raw[:, :], ACT.Abs, bias=heads_c[:, 0:1]), dt_act, 1)
            then(act, func(dt_w[:, 1, :], dt_w[:, 0, :], ACT.Exp, scale=-1.0), dt_act, 2)
            then(act, func(dt_w[:, 2, :], dt_w[:, 1, :], ACT.Ln, bias=1.0), dt_act, 3)
            then(act, func(heads_c[:, 2:3], heads_c[:, 1:2], ACT.Exp), dt_act, 4)
            act.wait_ge(dt_dve, 3)
            func(dt_w[:, 3, 0:NB], dt_w[:, 4, TP:T]).then_inc(dt_act, 1)
            func(dt_w[:, 3, NB:2 * NB], dt_w[:, 5, TP:T], ACT.Exp).then_inc(dt_act, 1)
            act.wait_ge(dt_ac, 2)
            func(dend[:, :, :], dend[:, :, :], ACT.Exp).then_inc(dt_de, 1)
            func(cdec[:, :], side[1][:, 3 * SH:4 * SH], ACT.Exp).then_inc(dt_de, 1)
            for n in range(12):
                c, m = n // 6, n % 6
                if m >= 4:
                    act.wait_ge(xb_tr, n + 1)
                    func(btok[:, c, (m - 4) * 512:(m - 3) * 512], side[n % 4][:, :]).then_inc(xb_cp[1], 1)

            def fin_copy(g):
                act.wait_ge(fin_mm, g + 1)
                wait(act, fin_out, 16 * g)
                func(hfin[:, :, :], gemm_ps[3][:, 0:256].rearrange("p (t n) -> p t n", t=2)).then_inc(fin_cp, 1)

            for s in range(2 * NG):
                g, c = s // 2, s % 2
                act.wait_ge(seg_done, s + 1)
                wait(act, m_done, s - 1)
                func(dec[:, c, :], seg[:, c, :], ACT.Exp).then_inc(dec_done, 1)
                if c == 1:
                    wait(act, y_mm, s - 1)
                    func(cexp[:, :], side[1][:, :], ACT.Exp).then_inc(cx_exp, 1)
                else:
                    if g:
                        fin_copy(g - 1)
                    act.wait_ge(ht_mm, g + 1)
                    wait(act, y_mm, 2 * g)
                    func(hT0[:, :], gemm_ps[2][:, 0:256]).then_inc(ht_cp, 1)
            fin_copy(NG - 1)
            act.wait_ge(y_mm, 2 * NG)
            act.wait_ge(m_done, 2 * NG)
            act.wait_ge(xw_done, 2 * NG)
            for n in range(4):
                act.wait_ge(bc_tr, n + 1)
                func(bcrow[:, n * 512:(n + 1) * 512], side[n % 4][0:NB, :]).then_inc(bc_cp, 1)
            act.wait_ge(ex_mm, 1)
            func(scal[:, :, :], side[0][:, 0:XT * 2 * NB].rearrange("p (t n) -> p t n", n=2 * NB)).then_inc(ex_cp, 1)

            def tail_copies(i, qq):
                if isinstance(i, int) and i == 0 and qq >= 4:
                    for n in (2 * qq - 8, 2 * qq - 7):
                        act.wait_ge(ct_tr, n + 1)
                        func(crow[:, n * 512:(n + 1) * 512], side[n % 4][0:3 + NB, :]).then_inc(ct_cp, 1)

            def gate_evac(ph, gate):
                def evac(pr, par, gen):
                    for n in range(2):
                        act.wait_ge(mm_done, last_block(ph, pr, n))
                        func(one(gate, 2 * pr + n), gemm_ps[2 * par + n][:, 0:T], ACT.Tanh, scale=0.5)\
                            .then_inc(free_out[par], 1)
                return evac

            last = blocks(act, ph_gs, hi_of(ph_gs), gate_evac(ph_gs, gate_s), None, tail_copies)
            act.wait_ge(ct_out, 32)
            last = blocks(act, ph_ga, hi_of(ph_ga), gate_evac(ph_ga, gate_a), last)
            last()
            act.wait_ge(p_sub, 1)
            func(sc[:, :, :, :], sc[:, :, :, :], ACT.Exp, scale=SCALE).then_inc(p_exp, 1)

            def z_evac(pr, par, gen):
                for n in range(2):
                    t = 2 * pr + n
                    act.wait_ge(mm_done, last_block(ph_z, pr, n))
                    wait(act, u_done, t - 1)
                    func(sq[:, n, :], gemm_ps[2 * par + n][:, 0:T], ACT.Tanh, scale=0.5).then_inc(z_tanh, 1)

            def state_act(i, m):
                b, r, s = 2 * i + m // 4, m % 4, m % 2
                act.wait_ge(st_in[s], 32 * (4 * i + m // 2 + 1))
                wait(act, st_sum, 8 * i + m)
                for t in range(4):
                    ins = func(stx[:, t, :], bc[:, s, 0, (t // 2) * P:(t // 2 + 1) * P],
                               scale=xdts[:, 4 * r + t, bass.ds(b, 1)])
                ins.then_inc(stx_done, 1)

            act.wait_ge(sx_mul, 1)
            blocks(act, ph_z, hi_of(ph_z), z_evac, None, state_act)()
            act.wait_ge(v_cp, 1)
            act.wait_ge(attn_cp, AT)
            for k in range(AT):
                func(a_hi[:, k, :], attn[:, k, :]).then_inc(a_hi_done, 1)

            act.wait_ge(mm_done, block_no(ph_ao, 0, 0))

            def u_hi_of(g):
                for n in range(2):
                    act.wait_ge(un_mul, 2 * g + n + 1)
                    func(x_hi[:, 2 * g + n, :], xbc[:, 2 * g + n, :]).then_inc(u_hi, 1)

            def norm_act(i, qq):
                B = 8 * i + qq
                if 0 <= B - 4 < NG:
                    g = B - 4
                    act.wait_ge(un_mm, g + 1)
                    wait(act, un_mul, 2 * g - 6)
                    func(un[:, g % 4, :], side[g % 4][:, 0:T], ACT.Sqrt, bias=eps[:, 0:1], scale=1.0 / 256)\
                        .then_inc(un_sd, 1)
                if 0 <= B - 7 < NG:
                    u_hi_of(B - 7)

            def so_evac(pr, par, gen):
                for n in range(2):
                    t = 2 * pr + n
                    act.wait_ge(ao_sum, t + 1)
                    func(one(m_hi, t), one(gate_s, t), scale=0.5).then_inc(ao_hi, 1)

            def copy_evac(ph, dst):
                def evac(pr, par, gen):
                    for n in range(2):
                        act.wait_ge(mm_done, last_block(ph, pr, n))
                        func(one(dst, 2 * pr + n), gemm_ps[2 * par + n][:, 0:T]).then_inc(free_out[par], 1)
                return evac

            blocks(act, ph_ao, hi_of(ph_ao), None, None, norm_act)
            blocks(act, ph_so, hi_of(ph_so), so_evac)()
            blocks(act, ph_o, hi_of(ph_o), copy_evac(ph_o, mo))()
            root(1)
            for k in range(KT):
                act.wait_ge(x1_done, k + 1)
                act.wait_ge(nrm_mm, KT * 2 + k - 1)
                func(sq[:, k % 2, :], x1[:, k, :], ACT.Square).then_inc(nrm_sq, 1)
            root(2)
            act.wait_ge(mm_done, block_no(ph_ff, 0, 0))
            x_hi_from(mo, 1)

            def ff_evac(pr, par, gen):
                if par == ph_ff.pair0 % 2:
                    for n in range(2):
                        act.wait_ge(mm_done, last_block(ph_ff, pr, n))
                        func(glu[:, 0, n, :], gemm_ps[2 * par + n][:, 0:T], ACT.Tanh, scale=0.5).then_inc(ff_tanh, 1)
                else:
                    for n in range(2):
                        act.wait_ge(free_out[par], 2 * gen + n + 1)
                        func(one(g_hi, pr - 1 + n), glu[:, 2, n, :]).then_inc(ff_hi, 1)

            blocks(act, ph_ff, hi_of(ph_ff), ff_evac)()
            blocks(act, ph_dn, hi_of(ph_dn), copy_evac(ph_dn, fo))()
            root(3)
            for n in range(0, 12, 2):
                act.wait_ge(y_tr, n + 1)
                func(*y_dst(n)).then_inc(y_cp, 1)

        @block.vector
        def _(dve):
            v = nc.vector

            def mul(out, x, y):
                return v.tensor_tensor(out, x, y, ALU.mult)

            def stt(out, x, scalar, y, op0, op1):
                return v.scalar_tensor_tensor(out=out, in0=x, scalar=scalar, in1=y, op0=op0, op1=op1)

            def lo_of(ph):
                def step(i, j, q, qq):
                    s, n, kts = (ph.load0 + qq // 2) % RING, qq % 2, k_tiles(ph, q)
                    w = (2 * ph.load0 + qq) % RING
                    dve.wait_ge(hi_done, block_no(ph, i, qq) + 1)
                    v.tensor_tensor(w_lo[:, w, 0:kts], raw[:, s, 0:kts, n * P:(n + 1) * P],
                                    w_hi[:, w, 0:kts].bitcast(fp32), ALU.subtract).then_inc(lo_done, 1)
                return step

            def squares(src, n, ready=None):
                for k in range(KT):
                    if ready:
                        dve.wait_ge(ready[0], ready[1] + k + 1)
                    wait(dve, nrm_mm, KT * n + k - 1)
                    mul(sq[:, k % 2, :], src[:, k, :], src[:, k, :]).then_inc(nrm_sq, 1)

            def square_evac(ph, src, n):
                def evac(pr, par, gen):
                    for m in range(2):
                        t = 2 * pr + m
                        dve.wait_ge(free_out[par], 2 * gen + m + 1)
                        wait(dve, nrm_mm, t + (KT * n - 1))
                        mul(sq[:, m, :], one(src, t), one(src, t)).then_inc(nrm_sq, 1)
                return evac

            def scale_and_add(src, n, gain, scaled, total, done):
                dve.wait_ge(nrm_sd, n + 1)
                then(dve, v.reciprocal(stat_r[:, :], stat[:, :]), nrm_rs, n + 1)
                for k in range(KT + 1):
                    if k < KT:
                        stt(src[:, k, :], src[:, k, :], gains[:, gain, k:k + 1], stat_r[:, :], ALU.mult, ALU.mult)\
                            .then_inc(scaled, 1)
                    if k:
                        dve.wait_ge(scaled, k)
                        v.tensor_tensor(total[:, k - 1, :], total[:, k - 1, :], src[:, k - 1, :], ALU.add)\
                            .then_inc(done, 1)

            def norm_and_lo(dst, src, n, gain, h0):
                dve.wait_ge(nrm_sd, n + 1)
                then(dve, v.reciprocal(stat_r[:, :], stat[:, :]), nrm_rs, n + 1)
                for k in range(KT + 2):
                    if k < KT:
                        stt(dst[:, k, :], src[:, k, :], gains[:, gain, k:k + 1], stat_r[:, :], ALU.mult, ALU.mult)\
                            .then_inc(h_mul, 1)
                    if k >= 2:
                        dve.wait_ge(h_hi, h0 + k - 1)
                        v.tensor_tensor(x_lo[:, k - 2, :], dst[:, k - 2, :], x_hi[:, k - 2, :].bitcast(fp32),
                                        ALU.subtract).then_inc(h_lo, 1)

            def x_lo_from(src, hi, lo, done, n, count):
                for k in range(count):
                    dve.wait_ge(done[0], n + k + 1)
                    v.tensor_tensor(lo[:, k, :], src[:, k, :], hi[:, k, :].bitcast(fp32), ALU.subtract)\
                        .then_inc(done[1], 1)

            dve.wait_ge(consts_made, CONSTS)
            squares(xT, 0, (x_cp, 0))
            norm_and_lo(xh, xT, 0, 0, 0)
            blocks(dve, ph_qkv, lo_of(ph_qkv))
            blocks(dve, ph_dt, lo_of(ph_dt))
            for n in range(1, 14, 2):
                dve.wait_ge(tok_tr, n + 1)
                v.tensor_copy(*tok_dst(n)).then_inc(tok_cp[1], 1)

            def conv_evac(pr, par, gen):
                for w in range(4):
                    for n in range(2):
                        t = 2 * pr + n
                        k = conv_k[:, w, bass.ds(t, 1)]
                        if w == 0:
                            wait(dve, xbc_done, t - 1)
                            dve.wait_ge(free_out[par], 2 * gen + n + 1)
                            ins = v.tensor_scalar(conv_out[:, n, :], conv_in[:, n, 0:CW], k, conv_bias[:, bass.ds(t, 1)],
                                                  ALU.mult, ALU.add)
                        else:
                            dve.wait_ge(conv_step, 8 * pr + 2 * w + n - 1)
                            ins = stt(conv_out[:, n, 0:CW], conv_in[:, n, w:w + CW], k, conv_out[:, n, 0:CW],
                                      ALU.mult, ALU.add)
                        ins.then_inc(conv_step, 1)

            def conv_dve(pr):
                for n in range(2):
                    t = 2 * pr + n
                    dve.wait_ge(conv_tanh, t + 1)
                    x = one(xbc, t)
                    stt(x[:, 0:TP], conv_th[:, n, 0:TP], 1.0, conv_out[:, n, 0:TP], ALU.add, ALU.mult)
                    new = [z[:, n, TP + 3:TP + 3 + 4 * NB - 3:4] for z in (conv_th, conv_out)]
                    stt(x[:, TP:T], new[0], 1.0, new[1], ALU.add, ALU.mult).then_inc(xbc_done, 1)

            def attn_dve(i, pos):
                if pos in (4, 5):
                    x = pos - 4
                    dve.wait_ge(s_mm, 2 * i + x + 1)
                    wait(dve, pt_mm, 2 * i - 1 + x)
                    then(dve, v.tensor_tensor(att_s[:, x, :], side[x][:, 0:3 * P], cmask[:, :], ALU.add),
                         s_masked, 2 * i + x + 1)
                    for m, cols in enumerate((slice(0, P), slice(P, 3 * P))):
                        ins = v.tensor_reduce(out=att_st[:, x, m:m + 1], in_=att_s[:, x, cols], axis=AX.X, op=ALU.max)
                    then(dve, ins, s_max, 2 * i + x + 1)
                    v.tensor_scalar(att_st[:, x, 2:4], att_st[:, x, 0:2], -SCALE, None, ALU.mult).then_inc(s_nmax, 1)
                if pos in (6, 7):
                    x = pos - 6
                    dve.wait_ge(s_exp, 2 * i + x + 1)
                    then(dve, v.reciprocal(att_st[:, x, 6:8], att_st[:, x, 4:6]), s_rcp, 2 * i + x + 1)
                    for m, cols in enumerate((slice(0, P), slice(P, 3 * P))):
                        ins = v.tensor_scalar(att_s[:, x, cols], att_s[:, x, cols], att_st[:, x, 6 + m:7 + m], None,
                                              ALU.mult)
                    ins.then_inc(s_norm, 1)
                if pos == 8:
                    conv_dve(2 * i)
                if pos == 12:
                    conv_dve(2 * i + 1)

            last = blocks(dve, ph_xbc, lo_of(ph_xbc), conv_evac, None, beside(attn_dve))
            finish(attn_dve, last)

            dve.wait_ge(tail_cp, CT)
            dve.wait_ge(dt_act, 4)
            then(dve, v.tensor_scalar(dt_w[:, 3, :], dt_raw[:, :], heads_c[:, 0:1], 0.0, ALU.add, ALU.max), dt_dve, 1)
            then(dve, v.tensor_tensor(dt_w[:, 4, :], dt_w[:, 3, :], dt_w[:, 2, :], ALU.add), dt_dve, 2)
            then(dve, v.tensor_scalar(dt_w[:, 5, :], dt_w[:, 4, :], heads_c[:, 2:3], -1.0, ALU.mult, ALU.mult),
                 dt_dve, 3)
            dve.wait_ge(dt_tr, 1)
            then(dve, v.tensor_copy(dtok[:, :, :, :].rearrange("p k c h -> p (k c h)"), side[0][:, 0:P]), dt_tok, 1)
            dve.wait_ge(dt_sum, 1)
            then(dve, v.tensor_copy(acum[:, :, :].rearrange("p c h -> p (c h)"), side[1][:, 0:2 * SH]), dt_ac, 1)
            v.tensor_tensor(dend[:, :, :].rearrange("p c h -> p (c h)"), side[1][:, 2 * SH:4 * SH],
                            acum[:, :, :].rearrange("p c h -> p (c h)"), ALU.subtract).then_inc(dt_ac, 1)
            for n in range(12):
                c, m = n // 6, n % 6
                if m < 4:
                    dve.wait_ge(xb_tr, n + 1)
                    w = dtok[:, 0, c, 8 * m:8 * m + 8].unsqueeze(2).to_broadcast([P, 8, HD])
                    v.tensor_tensor(xdt[:, c, m * 512:(m + 1) * 512].rearrange("p (h d) -> p h d", d=HD),
                                    side[n % 4][:, :].rearrange("p (h d) -> p h d", d=HD), w, ALU.mult)\
                        .then_inc(xb_cp[0], 1)

            def ssd_seg(s):
                g, c = s // 2, s % 2
                dve.wait_ge(r_mm, s + 1)
                wait(dve, y_mm, s - 1)
                for h in range(4):
                    ins = v.tensor_scalar(seg[:, c, h * P:(h + 1) * P], side[c][:, h * P:(h + 1) * P],
                                          acum[:, c, 4 * g + h:4 * g + h + 1], 0.0, ALU.subtract, ALU.min)
                ins.then_inc(seg_done, 1)
                dve.wait_ge(cb_mm, s + 1)
                mul(cbm[:, c, :], side[2 + c][:, 0:P], upper[:, :]).then_inc(cbm_done, 1)

            def ssd_y(s):
                g, c = s // 2, s % 2
                dve.wait_ge(y_mm, s + 1)
                for t in range(2):
                    x = xbc[:, 2 * g + t, c * P:(c + 1) * P]
                    ins = stt(x, x, dskip[:, 2 * g + t:2 * g + t + 1], gemm_ps[c][:, t * P:(t + 1) * P],
                              ALU.mult, ALU.add)
                ins.then_inc(y_done, 1)

            ssd_seg(0)
            for s in range(2 * NG):
                g, c = s // 2, s % 2
                if s + 1 < 2 * NG:
                    ssd_seg(s + 1)
                dve.wait_ge(dec_done, s + 1)
                dve.wait_ge(cbm_done, s + 1)
                mul(seg[:, c, :].rearrange("p (h i) -> p h i", h=4), dec[:, c, :].rearrange("p (h i) -> p h i", h=4),
                    cbm[:, c, :].unsqueeze(1).to_broadcast([P, 4, P])).then_inc(m_done, 1)
                if c == 1:
                    dve.wait_ge(cx_exp, g + 1)
                    cx = cexp[:, :].rearrange("p (h i) -> p h i", h=4)
                    mul(cx, cx, xbc[:, XT + NG + g, P:2 * P].unsqueeze(1).to_broadcast([P, 4, P])).then_inc(cx_done, 1)
                if s:
                    ssd_y(s - 1)
            ssd_y(2 * NG - 1)
            dve.wait_ge(ex_cp, 1)
            mul(xdts[:, :, :], xbc[:, 0:XT, TP:T], scal[:, :, 0:NB]).then_inc(sx_mul, 1)

            dve.wait_ge(own_in, 48)
            qk = own_qk[:, 0, :]
            then(dve, mul(qk, qk, own_qk[:, 1, :]), own_mul, 1)
            then(dve, v.tensor_reduce(out=m_w[0:NB, 0, 0:HEADS], in_=qk.rearrange("p (h d) -> p h d", d=HD), axis=AX.X,
                                      op=ALU.add), own_sum, 1)
            then(dve, v.tensor_copy(sc[:, NPG], dmask[:, :].unsqueeze(2).to_broadcast([P, NB, HEADS])), own_sum, 2)
            v.tensor_tensor(sc[0:NB, NPG], sc[0:NB, NPG],
                            m_w[0:NB, 0, 0:HEADS].unsqueeze(1).to_broadcast([NB, NB, HEADS]), ALU.add)\
                .then_inc(own_put, 1)

            def k_sum(b, g):
                dve.wait_ge(k_mul, NPG * b + g + 1)
                v.tensor_reduce(out=sc[:, g, bass.ds(b, 1), :].rearrange("p o h -> p (o h)"),
                                in_=kv[:, g % 4].rearrange("p (h d) -> p h d", d=HD), axis=AX.X, op=ALU.add)\
                    .then_inc(k_red, 1)

            def k_sums(ph):
                def side_work(i, m):
                    at_ = earlier(i, m, 2, 8)
                    if at_:
                        k_sum(*kpage(ph, *at_))
                    elif ph is ph_ga:
                        k_sum(NB // 2 - 1, m + 6)
                return side_work

            blocks(dve, ph_gs, lo_of(ph_gs), None, None, k_sums(ph_gs))
            blocks(dve, ph_ga, lo_of(ph_ga), None, None, k_sums(ph_ga))
            for m in (6, 7):
                k_sum(NB - 1, m)
            dve.wait_ge(sel_mm, 1)
            step = [0]

            def sel(ins):
                step[0] += 1
                then(dve, ins, sel_dve, step[0])

            scp = sc[:, :, :, :].rearrange("p g b h -> p g (b h)")
            for n in range(2):
                sel(v.tensor_reduce(out=m_w[:, 2 * n:2 * n + 2, :],
                                    in_=side[n][:, :].rearrange("p (k u x) -> p k x u", u=2, x=P), axis=AX.X,
                                    op=ALU.add))
            low, eq, rest = m_w[:, 4, :], m_w[:, 5, :], m_w[:, 6, :]
            sel(v.tensor_tensor(low, m_w[:, 0, :], m_w[:, 1, :], ALU.min))
            sel(v.tensor_tensor(eq, m_w[:, 2, :], m_w[:, 3, :], ALU.min))
            sel(v.tensor_tensor(low, low, eq, ALU.min))
            sel(v.tensor_tensor(m_w[:, 3, :], m_w[:, 3, :], low, ALU.is_equal))
            sel(v.tensor_scalar(rest, m_w[:, 3, :], -1.0, 1.0, ALU.mult, ALU.add))
            for n in (2, 1):
                sel(v.tensor_tensor(eq, m_w[:, n, :], low, ALU.is_equal))
                sel(mul(m_w[:, n, :], eq, rest))
                sel(v.tensor_tensor(rest, rest, m_w[:, n, :], ALU.subtract))
            for n in range(NBLK):
                drop = (rest if n == 0 else m_w[:, n, :]).unsqueeze(1).to_broadcast([P, 2, P])
                sel(stt(scp[:, 2 * n:2 * n + 2], drop, NEG, scp[:, 2 * n:2 * n + 2], ALU.mult, ALU.add))
            v.tensor_reduce(out=m_w[:, 5, :], in_=scp.rearrange("p g x -> p x g"), axis=AX.X, op=ALU.max)\
                .then_inc(max_dve, 1)
            dve.wait_ge(max_tr, 1)
            then(dve, v.tensor_reduce(out=m_w[:, 6, 0:1], in_=side[2][:, 0:P], axis=AX.X, op=ALU.max), max_dve, 2)
            v.tensor_scalar(m_w[:, 7, :], ident[:, :], m_w[:, 6, 0:1], None, ALU.mult).then_inc(max_dve, 1)
            dve.wait_ge(max_mm, 1)
            every = [P, NPG + 1, P]
            v.tensor_tensor(scp, scp, side[3][:, 0:P].unsqueeze(1).to_broadcast(every), ALU.subtract).then_inc(p_sub, 1)
            dve.wait_ge(p_exp, 1)
            v.tensor_reduce(out=m_w[:, 8, :], in_=scp.rearrange("p g x -> p x g"), axis=AX.X, op=ALU.add)\
                .then_inc(p_sum, 1)
            dve.wait_ge(p_mm, 1)
            then(dve, v.reciprocal(m_w[:, 9, :], side[0][:, 0:P]), p_rcp, 1)
            mul(scp, scp, m_w[:, 9, :].unsqueeze(1).to_broadcast(every)).then_inc(p_done, 1)

            def z_evac(pr, par, gen):
                for n in range(2):
                    t = 2 * pr + n
                    dve.wait_ge(z_tanh, t + 1)
                    then(dve, stt(tmp[:, n, :], sq[:, n, :], 1.0, gemm_ps[2 * par + n][:, 0:T], ALU.add, ALU.mult),
                         free_out[par], 2 * gen + n + 1)
                    x = one(xbc, t)
                    v.tensor_copy(one(zs, t), tmp[:, n, TP:T])
                    stt(x[:, 0:TP], tmp[:, n, 0:TP], 0.5, x[:, 0:TP], ALU.mult, ALU.mult).then_inc(u_done, 1)

            def state_step(i, m):
                b, r, s, n = 2 * i + m // 4, m % 4, m % 2, 8 * i + m
                dve.wait_ge(stx_done, n + 1)
                for t in range(4):
                    ins = stt(st[:, s, t, :], st[:, s, t, :], scal[:, 4 * r + t, bass.ds(NB + b, 1)], stx[:, t, :],
                              ALU.mult, ALU.add)
                then(dve, ins, st_new, n + 1)
                cb = bc[:, s, 1, :].rearrange("p (g n) -> p g n", g=2).unsqueeze(2).to_broadcast([P, 2, 2, P])
                then(dve, mul(stx[:, :, :].rearrange("p (g t) n -> p g t n", g=2),
                              st[:, s].rearrange("p (g t) n -> p g t n", g=2), cb), st_prod, n + 1)
                v.tensor_reduce(out=ysam[:, 4 * r:4 * r + 4, bass.ds(b, 1)].rearrange("p t o -> p (t o)"),
                                in_=stx[:, :, :], axis=AX.X, op=ALU.add).then_inc(st_sum, 1)

            blocks(dve, ph_z, lo_of(ph_z), z_evac, None, state_step)()
            dve.wait_ge(v_mm, NB * NPG + 1)
            for n in range(2):
                own = hmask[:, 8 * n:8 * n + 8].unsqueeze(2).to_broadcast([P, 8, HD])
                v.tensor_tensor(vm[:, n * 512:(n + 1) * 512].rearrange("p (h d) -> p h d", d=HD),
                                side[n][:, :].rearrange("p (h d) -> p h d", d=HD), own, ALU.mult).then_inc(vm_done, 1)
            dve.wait_ge(u_done, KT)
            dve.wait_ge(st_sum, 4 * NB)
            xn = xbc[:, 0:XT, TP:T]
            then(dve, mul(xn, xn, dskip[:, :].unsqueeze(2).to_broadcast([P, XT, NB])), ysam_done, 1)
            then(dve, v.tensor_tensor(xn, xn, ysam[:, :, :], ALU.add), ysam_done, 2)
            then(dve, mul(xn, xn, zs[:, :, :]), ysam_done, 3)
            then(dve, v.tensor_scalar(xn, xn, 0.5, None, ALU.mult), ysam_done, 4)
            dve.wait_ge(v_mm, NB * NPG + 2)
            v.tensor_copy(attn[:, :, TP:T], side[2][:, 0:AT * NB].rearrange("p (k b) -> p k b", b=NB)).then_inc(v_cp, 1)
            x_lo_from(attn, a_hi, a_lo, (a_hi_done, a_lo_done), 0, AT)
            for s in range(2):
                dve.wait_ge(st_out[s], 16 * 2 * NB)
            dve.wait_ge(ysam_done, 4)

            def u_lo_of(g):
                for n in range(2):
                    t = 2 * g + n
                    dve.wait_ge(u_hi, t + 1)
                    v.tensor_tensor(x_lo[:, t, :], xbc[:, t, :], x_hi[:, t, :].bitcast(fp32), ALU.subtract)\
                        .then_inc(u_lo, 1)

            def norm_dve(i, qq):
                B = 8 * i + qq
                if B < NG:
                    for t in (2 * B, 2 * B + 1):
                        mul(u_sq[:, t, :], xbc[:, t, :], xbc[:, t, :]).then_inc(un_sq, 1)
                if 0 <= B - 5 < NG:
                    g = B - 5
                    dve.wait_ge(un_sd, g + 1)
                    then(dve, v.reciprocal(un[:, g % 4, :], un[:, g % 4, :]), un_rs, g + 1)
                    for t in (2 * g, 2 * g + 1):
                        stt(xbc[:, t, :], xbc[:, t, :], gains[:, 4, t:t + 1], un[:, g % 4, :], ALU.mult, ALU.mult)\
                            .then_inc(un_mul, 1)
                if 0 <= B - 8 < NG:
                    u_lo_of(B - 8)

            def ao_evac(pr, par, gen):
                for n in range(2):
                    t = one(gate_a, 2 * pr + n)
                    dve.wait_ge(mm_done, last_block(ph_ao, pr, n))
                    stt(t, t, 1.0, gemm_ps[2 * par + n][:, 0:T], ALU.add, ALU.mult).then_inc(free_out[par], 1)

            def so_evac(pr, par, gen):
                for n in range(2):
                    t = 2 * pr + n
                    ga, gs = one(gate_a, t), one(gate_s, t)
                    dve.wait_ge(mm_done, last_block(ph_so, pr, n))
                    then(dve, stt(gs, gs, 1.0, gemm_ps[2 * par + n][:, 0:T], ALU.add, ALU.mult),
                         free_out[par], 2 * gen + n + 1)
                    v.tensor_tensor(gs, gs, ga, ALU.add).then_inc(ao_sum, 1)
                for n in range(2):
                    t = 2 * pr + n
                    dve.wait_ge(ao_hi, t + 1)
                    stt(one(m_lo, t), one(gate_s, t), 0.5, one(m_hi, t).bitcast(fp32), ALU.mult, ALU.subtract)\
                        .then_inc(ao_lo, 1)

            last = blocks(dve, ph_ao, lo_of(ph_ao), ao_evac, None, norm_dve)
            blocks(dve, ph_so, lo_of(ph_so), so_evac, last)()
            blocks(dve, ph_o, lo_of(ph_o), square_evac(ph_o, mo, 1))()
            dve.wait_ge(x_back, 16)
            scale_and_add(mo, 1, 1, o_scaled, x1, x1_done)
            norm_and_lo(mo, x1, 2, 2, KT)

            def ff_evac(pr, par, gen):
                other = 1 - par
                if isinstance(pr, int) and pr == 0:
                    dve.wait_ge(x1_out, 16)
                if par == ph_ff.pair0 % 2:
                    for n in range(2):
                        dve.wait_ge(ff_tanh, pr + n + 1)
                        stt(glu[:, 1, n, :], glu[:, 0, n, :], 1.0, gemm_ps[2 * par + n][:, 0:T], ALU.add, ALU.mult)\
                            .then_inc(free_out[par], 1)
                else:
                    for n in range(2):
                        dve.wait_ge(mm_done, last_block(ph_ff, pr, n))
                        dve.wait_ge(free_out[other], 2 * (gen - ph_ff.pair0 % 2) + n + 1)
                        stt(glu[:, 2, n, :], glu[:, 1, n, :], 0.5, gemm_ps[2 * par + n][:, 0:T], ALU.mult, ALU.mult)\
                            .then_inc(free_out[par], 1)
                    for n in range(2):
                        t = pr - 1 + n
                        dve.wait_ge(ff_hi, t + 1)
                        v.tensor_tensor(one(g_lo, t), glu[:, 2, n, :], one(g_hi, t).bitcast(fp32), ALU.subtract)\
                            .then_inc(ff_lo, 1)

            blocks(dve, ph_ff, lo_of(ph_ff), ff_evac)()
            blocks(dve, ph_dn, lo_of(ph_dn), square_evac(ph_dn, fo, 3))()
            dve.wait_ge(x1_in, 16)
            scale_and_add(fo, 3, 3, f_scaled, x2, y2_done)
            for n in range(1, 12, 2):
                dve.wait_ge(y_tr, n + 1)
                v.tensor_copy(*y_dst(n)).then_inc(y_cp2, 1)

        @block.tensor
        def _(pe):
            mm = nc.tensor.matmul

            def turn(out, in_):
                k = in_.shape[0]
                return mm(out, in_, ident[0:k, 0:k], start=True, stop=True)

            def mm_of(ph, ready=None, base=0):
                def step(i, j, q, qq):
                    n, kg, kts = q % 2, q // 2, k_tiles(ph, q)
                    par = (ph.pair0 + j) % 2
                    if q == 0:
                        wait(pe, free_out[par], 2 * ((ph.pair0 + j) // 2 + ph.per // 2 * i))
                    pe.wait_ge(lo_done, block_no(ph, i, qq) + 1)
                    w = (2 * ph.load0 + qq) % RING
                    out = gemm_ps[2 * par + n][:, 0:T]
                    for k in range(kts):
                        x = kg * KG + k
                        if ready and n == 0 and j == 0 and isinstance(i, int) and i == 0:
                            pe.wait_ge(ready, base + x + 1)
                        mm(out, w_hi[:, w, k], ph.hi[:, x], start=(x == 0), stop=False)
                        mm(out, w_hi[:, w, k], ph.lo[:, x], start=False, stop=False)
                        ins = mm(out, w_lo[:, w, k], ph.hi[:, x], start=False, stop=(x == ph.kt - 1))
                    ins.then_inc(mm_done, 1)
                return step

            def x_turns(src, then_sum):
                for k in range(KT):
                    wait(pe, x_cp, k - 2)
                    cols = slice(k * P, (k + 1) * P)
                    for c in range(2):
                        turn(side[k % 3][:, c * P:(c + 1) * P], src[:, c, cols])
                    turn(side[k % 3][:, TP:T], src[0:NB, 2, cols]).then_inc(x_tr, 1)
                    if k >= 3:
                        then_sum(k - 3)

            def norm_sum(n, k):
                pe.wait_ge(nrm_sq, KT * n + k + 1)
                mm(side[3][:, 0:T], ones[:, :], sq[:, k % 2, :], start=(k == 0), stop=(k == KT - 1)).then_inc(nrm_mm, 1)

            def sum_evac(ph, n):
                def evac(pr, par, gen):
                    for m in range(2):
                        t = 2 * pr + m
                        static = isinstance(t, int)
                        pe.wait_ge(nrm_sq, t + (KT * n + 1))
                        mm(side[3][:, 0:T], ones[:, :], sq[:, m, :], start=(static and t == 0),
                           stop=(static and t == KT - 1)).then_inc(nrm_mm, 1)
                return evac

            def norm_sums(n):
                for k in range(KT):
                    norm_sum(n, k)

            pe.wait_ge(consts_made, 3)
            pe.wait_ge(x_in, 48)
            x_turns(xtok, lambda k: norm_sum(0, k))
            for k in range(KT - 3, KT):
                norm_sum(0, k)
            pe.wait_ge(state_in, 16)
            pe.wait_ge(nrm_sd, 1)
            for n in range(8):
                wait(pe, cst_cp, n - 3)
                for u in range(4):
                    t = 4 * n + u
                    ins = turn(side[n % 4][:, u * 24:(u + 1) * 24], ctok[:, t * P:(t + 1) * P])
                ins.then_inc(cst_tr, 1)
            blocks(pe, ph_qkv, mm_of(ph_qkv, h_lo))
            blocks(pe, ph_dt, mm_of(ph_dt))
            pe.wait_ge(cst_cp, 8)
            for par in range(2):
                pe.wait_ge(free_out[par], none_free(ph_dt)[par])
            for n in range(14):
                wait(pe, tok_cp[n % 2], (n - 4) // 2 + 1)
                if n < 8:
                    for u in range(4):
                        src = qkv[:, AT * (1 + n // 4) + 4 * (n % 2) + u, (n // 2) % 2 * P:((n // 2) % 2 + 1) * P]
                        ins = turn(side[n % 4][:, u * P:(u + 1) * P], src)
                else:
                    for u in range(4):
                        ins = turn(side[n % 4][0:NB, u * P:(u + 1) * P], qkv[:, 4 * (n - 8) + u, TP:T])
                ins.then_inc(tok_tr, 1)
            for s in tok_cp:
                pe.wait_ge(s, 7)

            def attn_pe(i, pos):
                if pos in (0, 1):
                    x = pos
                    if x == 0:
                        pe.wait_ge(qk_staged, i + 1)
                    wait(pe, s_masked, 2 * i - 1 + x)
                    q, k = (qk_head[x * HD:(x + 1) * HD, w, :] for w in range(2))
                    mm(side[x][:, 0:P], q[:, 0:P], k[:, 0:P], start=True, stop=True)
                    mm(side[x][:, P:3 * P], q[:, P:TP], k[:, 0:TP], start=True, stop=True).then_inc(s_mm, 1)
                if pos in (5, 7):
                    x = pos // 2 - 2
                    pe.wait_ge(s_norm, 2 * i + x + 1)
                    wait(pe, pt_cp, 2 * i + x)
                    for m in range(3):
                        ins = turn(side[2][:, m * P:(m + 1) * P], att_s[:, x, m * P:(m + 1) * P])
                    ins.then_inc(pt_mm, 1)
                if pos == 9:
                    pe.wait_ge(v_staged, i + 1)
                    for x in range(2):
                        pe.wait_ge(pt_cp, 2 * i + x + 1)
                        rows = slice(x * HD, (x + 1) * HD)
                        mm(side[3][rows, 0:TP], v_head[:, 0, rows], att_pt[:, x, 0:TP], start=True, stop=False)
                        mm(side[3][rows, P:TP], v_head[:, 1, rows], att_pt[:, x, TP:3 * P], start=False, stop=True)\
                            .then_inc(pv_mm, 1)

            blocks(pe, ph_xbc, mm_of(ph_xbc), None, None, beside(attn_pe))
            finish(attn_pe)

            pe.wait_ge(dt_dve, 3)
            pe.wait_ge(attn_cp, AT)
            for par in range(2):
                pe.wait_ge(free_out[par], none_free(ph_xbc)[par])
            for w in range(2):
                for c in range(2):
                    ins = turn(side[0][:, (2 * w + c) * SH:(2 * w + c + 1) * SH], dt_w[:, 4 + w, c * P:(c + 1) * P])
            ins.then_inc(dt_tr, 1)
            pe.wait_ge(dt_tok, 1)
            for w, m in enumerate((upper, ones)):
                for c in range(2):
                    ins = mm(side[1][:, (2 * w + c) * SH:(2 * w + c + 1) * SH], m[:, :], dtok[:, 1, c, :],
                             start=True, stop=True)
            ins.then_inc(dt_sum, 1)
            pe.wait_ge(dt_de, 2)
            pe.wait_ge(xbc_done, CT)

            def copied(n):
                if n >= 0:
                    c, m = n // 6, n % 6
                    pe.wait_ge(xb_cp[m // 4], 4 * c + m + 1 if m < 4 else 2 * c + m - 3)

            for n in range(12):
                c, m = n // 6, n % 6
                copied(n - 4)
                for u in range(4):
                    ins = turn(side[n % 4][:, u * P:(u + 1) * P], xbc[:, 4 * m + u, c * P:(c + 1) * P])
                ins.then_inc(xb_tr, 1)
            for n in range(8, 12):
                copied(n)

            def ssd_rc(s):
                g, c = s // 2, s % 2
                wait(pe, seg_done, s - 1)
                if c:
                    wait(pe, cx_exp, g)
                for h in range(4):
                    ins = mm(side[c][:, h * P:(h + 1) * P], dtok[:, 1, c, 4 * g + h:4 * g + h + 1].to_broadcast([P, P]),
                             upper[:, :], start=True, stop=True)
                ins.then_inc(r_mm, 1)
                wait(pe, cbm_done, s - 1)
                mm(side[2 + c][:, 0:P], xbc[:, XT + g, c * P:(c + 1) * P], xbc[:, XT + NG + g, c * P:(c + 1) * P],
                   start=True, stop=True).then_inc(cb_mm, 1)

            ssd_rc(0)
            for s in range(2 * NG):
                g, c = s // 2, s % 2
                if s + 1 < 2 * NG:
                    ssd_rc(s + 1)
                if c == 0:
                    pe.wait_ge(xw_done, 2 * g + 1)
                    wait(pe, ht_cp, g)
                    mm(gemm_ps[2][:, 0:256], btok[:, 0, g * P:(g + 1) * P], xw1[:, 0, :], start=True, stop=True)\
                        .then_inc(ht_mm, 1)
                pe.wait_ge(m_done, s + 1)
                if c:
                    pe.wait_ge(cx_done, g + 1)
                    pe.wait_ge(ht_cp, g + 1)
                wait(pe, y_done, s - 1)
                for h in range(4):
                    out = gemm_ps[c][(h % 2) * HD:(h % 2 + 1) * HD, (h // 2) * P:(h // 2 + 1) * P]
                    ins = mm(out, xdt[:, c, (4 * g + h) * HD:(4 * g + h + 1) * HD], seg[:, c, h * P:(h + 1) * P],
                             start=True, stop=(c == 0))
                    if c:
                        ins = mm(out, hT0[:, h * HD:(h + 1) * HD], cexp[:, h * P:(h + 1) * P], start=False, stop=True)
                ins.then_inc(y_mm, 1)
                if c:
                    pe.wait_ge(xwf_done, g + 1)
                    pe.wait_ge(xw_done, 2 * g + 2)
                    wait(pe, fin_cp, g)
                    for t in range(2):
                        out, cols = gemm_ps[3][:, t * P:(t + 1) * P], slice(t * P, (t + 1) * P)
                        mm(out, xw[:, cols], btok[:, 0, g * P:(g + 1) * P], start=True, stop=False)
                        ins = mm(out, xw1[:, 1, cols], btok[:, 1, g * P:(g + 1) * P], start=False, stop=True)
                    ins.then_inc(fin_mm, 1)
            pe.wait_ge(seg_done, 2 * NG)
            pe.wait_ge(cx_exp, NG)
            pe.wait_ge(cbm_done, 2 * NG)
            for n in range(4):
                for u in range(4):
                    ins = turn(side[n][0:NB, u * P:(u + 1) * P], xbc[:, XT + 4 * n + u, TP:T])
                ins.then_inc(bc_tr, 1)
            pe.wait_ge(bc_cp, 4)
            pe.wait_ge(dt_act, 6)
            for t in range(XT):
                for e in range(2):
                    head = ident[0:SH, 2 * t + e:2 * t + e + 1].to_broadcast([SH, HD])
                    ins = mm(side[0][e * HD:(e + 1) * HD, t * 2 * NB:(t + 1) * 2 * NB], head, dt_w[:, 3, 0:2 * NB],
                             start=True, stop=True)
            ins.then_inc(ex_mm, 1)
            pe.wait_ge(ex_cp, 1)
            pe.wait_ge(tail_cp, CT)
            pe.wait_ge(y_done, 2 * NG)
            pe.wait_ge(fin_cp, NG)

            def tail_turns(i, qq):
                if isinstance(i, int) and i == 0 and qq < 4:
                    for n in (2 * qq, 2 * qq + 1):
                        wait(pe, ct_cp, n - 3)
                        for u in range(4):
                            ins = turn(side[n % 4][0:3 + NB, u * P:(u + 1) * P], tails[:, 4 * n + u, :])
                        ins.then_inc(ct_tr, 1)

            blocks(pe, ph_gs, mm_of(ph_gs), None, None, tail_turns)
            blocks(pe, ph_ga, mm_of(ph_ga))
            pe.wait_ge(ct_cp, 8)
            pe.wait_ge(k_red, NB * NPG)
            for n in range(2):
                ins = mm(side[n][:, :], ones[:, :], sc[:, 4 * n:4 * n + 4].rearrange("p g b h -> p (g b h)"),
                         start=True, stop=True)
            ins.then_inc(sel_mm, 1)
            pe.wait_ge(max_dve, 1)
            turn(side[2][:, 0:P], m_w[:, 5, :]).then_inc(max_tr, 1)
            pe.wait_ge(max_dve, 3)
            mm(side[3][:, 0:P], ones[:, :], m_w[:, 7, :], start=True, stop=True).then_inc(max_mm, 1)
            pe.wait_ge(p_sum, 1)
            mm(side[0][:, 0:P], ones[:, :], m_w[:, 8, :], start=True, stop=True).then_inc(p_mm, 1)
            pe.wait_ge(p_done, 1)
            def v_page(i, m):
                b, g = 2 * i + m // NPG, m % NPG
                if g == 0:
                    pe.wait_ge(pz_done, 2 * b + 2)
                pe.wait_ge(kv_in[g % 4], 16 * (NB * NPG // 4 + 2 * b + g // 4 + 1))
                for n in range(2):
                    ins = mm(side[n][:, :], pz[:, g, :], kv[:, g % 4, n * 512:(n + 1) * 512],
                             start=(isinstance(i, int) and i == 0 and m == 0), stop=False)
                ins.then_inc(v_mm, 1)

            def z_side(i, qq):
                for u in range(2):
                    v_page(i, 2 * qq + u)

            pe.wait_ge(p_sub, 1)
            pe.wait_ge(p_done, 1)
            blocks(pe, ph_z, mm_of(ph_z), None, None, z_side)
            for n in range(2):
                ins = mm(side[n][:, :], sc[0:NB, NPG].rearrange("p b h -> p (b h)"), own_v[:, n * 512:(n + 1) * 512],
                         start=False, stop=True)
            ins.then_inc(v_mm, 1)
            pe.wait_ge(vm_done, 2)
            for k in range(AT):
                ins = mm(side[2][:, k * NB:(k + 1) * NB], vm[:, k * P:(k + 1) * P], bsel[:, :], start=True, stop=True)
            ins.then_inc(v_mm, 1)

            def norm_pe(i, qq):
                if isinstance(i, int) and i == 0:
                    g = qq
                    wait(pe, un_sd, g - 3)
                    for n in range(2):
                        pe.wait_ge(un_sq, 2 * g + n + 1)
                        ins = mm(side[g % 4][:, 0:T], ones[:, :], u_sq[:, 2 * g + n, :], start=(n == 0), stop=(n == 1))
                    ins.then_inc(un_mm, 1)

            blocks(pe, ph_ao, mm_of(ph_ao, a_lo_done), None, None, norm_pe)
            blocks(pe, ph_so, mm_of(ph_so, u_lo))
            pe.wait_ge(un_sd, NG)
            blocks(pe, ph_o, mm_of(ph_o, ao_lo), sum_evac(ph_o, 1))()
            pe.wait_ge(nrm_sd, 2)
            norm_sums(2)
            blocks(pe, ph_ff, mm_of(ph_ff, h_lo, KT))
            pe.wait_ge(nrm_sd, 3)
            blocks(pe, ph_dn, mm_of(ph_dn, ff_lo), sum_evac(ph_dn, 3))()
            pe.wait_ge(nrm_sd, 4)
            for n in range(12):
                m = n // 3
                wait(pe, (y_cp, y_cp2)[n % 2], (n - 4) // 2 + 1)
                pe.wait_ge(y2_done, 4 * m + 4)
                c = n % 3
                for u in range(4):
                    out = side[n % 4][0:(P if c < 2 else NB), u * P:(u + 1) * P]
                    ins = turn(out, x2[:, 4 * m + u, c * P:(c + 1) * P if c < 2 else T])
                ins.then_inc(y_tr, 1)


_INS = ["x_prompt", "x_sample", "cache_k", "cache_v", "state_conv", "state_ssm", "page_table",
        "norm_mix_pre", "w_in", "conv_w", "conv_b", "dt_bias", "a_log", "d_skip", "ssm_norm",
        "w_attn_out", "w_ssm_out", "w_out", "norm_mix_post",
        "norm_ffn_pre", "w_gate", "w_up", "w_down", "norm_ffn_post"]
_OUTS = [("y_prompt", (1, TP, D)), ("y_sample", (NB, 1, D)),
         ("k_prompt", (1, 1, TP, HEADS, HD)), ("v_prompt", (1, 1, TP, HEADS, HD)),
         ("conv_prompt", (1, 1, 3, CONVC)), ("ssm_prompt", (1, 1, SH, HD, NST)),
         ("k_sample", (1, NB, 1, HEADS, HD)), ("v_sample", (1, NB, 1, HEADS, HD)),
         ("conv_sample", (1, NB, 3, CONVC)), ("ssm_sample", (1, NB, SH, HD, NST))]


def kernel(**inputs):
    import numpy as np
    import concourse.bacc as bacc
    from concourse.bass_utils import run_bass_kernel_spmd

    nc = bacc.Bacc("TRN2", target_bir_lowering=False, num_devices=1)
    arrays, a, o = {}, {}, {}
    for name in _INS:
        x = np.ascontiguousarray(inputs[name])
        arrays[f"in_{name}"] = x
        a[name] = nc.dram_tensor(f"in_{name}", x.shape, mybir.dt.from_np(x.dtype), kind="ExternalInput").ap()
    for name, shape in _OUTS:
        o[name] = nc.dram_tensor(f"out_{name}", shape, fp32, kind="ExternalOutput").ap()
    bass_hybrid_decoder_layer(nc, a, o)
    r = run_bass_kernel_spmd(nc, [arrays], core_ids=[0])
    return tuple(r.results[0][f"out_{name}"] for name, _ in _OUTS)
```
